# Optimizing a Trainium2 kernel written in Bass

```python
import math
import jax, jax.numpy as jnp
from jax import lax
import numpy as np

D_MODEL = 1024
BATCH = 1
SEQ = 128
DEPTH = 2
DEC_BATCH = 1
DEC_SEQ = 512
PAST_LEN = 128

GRID_W = 64
HEAD_DIM = 64
N_Q_HEADS = 8
N_KV_HEADS = 2
Q_PER_KV = N_Q_HEADS // N_KV_HEADS
ATTN_W = N_Q_HEADS * HEAD_DIM
KV_W = N_KV_HEADS * HEAD_DIM
WINDOW = 128
BLOCK = 128
ATTN_SCALE = 0.125
ROPE_THETA = 10000.0
NEG = -1e30
RWKV_HEADS = 4
RWKV_W = RWKV_HEADS * HEAD_DIM
DECAY_RANK = 64
ICLR_RANK = 64
GATE_RANK = 128
SHIFT_WIDTH = 3
DECAY_SCALE = 0.6065306597126334
GN_EPS = 64e-5
RWKV_IN_W = 3 * RWKV_W + GATE_RANK + 2 * DECAY_RANK + 2 * ICLR_RANK
RWKV_SPLITS = (RWKV_W, 2 * RWKV_W, 3 * RWKV_W, 3 * RWKV_W + GATE_RANK,
               3 * RWKV_W + GATE_RANK + 2 * DECAY_RANK)
FNET_GROUPS = 4
FNET_W = FNET_GROUPS * HEAD_DIM
MIX_W = ATTN_W + RWKV_W + FNET_W
IN_W = ATTN_W + 2 * KV_W + RWKV_IN_W + FNET_W
IN_SPLITS = (ATTN_W, ATTN_W + KV_W, ATTN_W + 2 * KV_W, ATTN_W + 2 * KV_W + RWKV_IN_W)
D_FF = -(-8 * D_MODEL // (3 * 256)) * 256
RMS_EPS = 1e-6

kernel_name = "hybrid_dit_gqa_rwkv7_fnet_step"

def rmsnorm(x, g):
    xf = x.astype(jnp.float32)
    y = xf * lax.rsqrt(jnp.mean(xf * xf, axis=-1, keepdims=True) + RMS_EPS)
    return (y * g.astype(jnp.float32)).astype(x.dtype)

def modulate(h, shift, scale):
    return h * (1.0 + scale) + shift

def axial_rope(x):
    T = x.shape[1]
    n_rows = T // GRID_W
    row = jnp.repeat(jnp.arange(n_rows), GRID_W)
    col = jnp.tile(jnp.arange(GRID_W), n_rows)
    half = HEAD_DIM // 2
    quarter = half // 2
    inv = ROPE_THETA ** (-jnp.arange(quarter, dtype=jnp.float32) / quarter)

    def rot(xh, pos):
        ang = pos.astype(jnp.float32)[:, None] * inv[None, :]
        cos = jnp.cos(ang)[None, :, None, :]
        sin = jnp.sin(ang)[None, :, None, :]
        x1, x2 = xh[..., :quarter], xh[..., quarter:]
        return jnp.concatenate([x1 * cos - x2 * sin, x2 * cos + x1 * sin], axis=-1)

    xf = x.astype(jnp.float32)
    out = jnp.concatenate([rot(xf[..., :half], row), rot(xf[..., half:], col)], axis=-1)
    return out.astype(x.dtype)

def softmax_with_sink(s, sink):
    sk = sink.astype(jnp.float32).reshape(N_KV_HEADS, Q_PER_KV, 1, 1)
    m = jnp.maximum(jnp.max(s, axis=-1, keepdims=True), sk)
    e = jnp.exp(s - m)
    return e / (jnp.sum(e, axis=-1, keepdims=True) + jnp.exp(sk - m))

def context_attention(q, k, v, sink):
    B, C = q.shape[:2]
    nqb = C // BLOCK
    qb = jnp.moveaxis(q.reshape(B, nqb, BLOCK, N_KV_HEADS, Q_PER_KV, HEAD_DIM), 1, 0)
    kf = k.astype(jnp.float32)
    vf = v.astype(jnp.float32)

    def one_block(qblk):
        s = jnp.einsum('bqkgd,bckd->bkgqc', qblk.astype(jnp.float32), kf) * ATTN_SCALE
        p = softmax_with_sink(s, sink)
        return jnp.einsum('bkgqc,bckd->bqkgd', p, vf)

    o = lax.map(one_block, qb)
    return jnp.moveaxis(o, 0, 1).reshape(B, C, ATTN_W).astype(q.dtype)

def latent_attention(q, k, v, k_ctx, v_ctx, sink):
    B, T = q.shape[:2]
    nb = T // BLOCK
    qb = q.reshape(B, nb, BLOCK, N_KV_HEADS, Q_PER_KV, HEAD_DIM).astype(jnp.float32)
    pad = ((0, 0), (BLOCK, BLOCK), (0, 0), (0, 0))
    kp = jnp.pad(k, pad).reshape(B, nb + 2, BLOCK, N_KV_HEADS, HEAD_DIM)
    vp = jnp.pad(v, pad).reshape(B, nb + 2, BLOCK, N_KV_HEADS, HEAD_DIM)
    kband = jnp.concatenate([kp[:, :-2], kp[:, 1:-1], kp[:, 2:]], axis=2).astype(jnp.float32)
    vband = jnp.concatenate([vp[:, :-2], vp[:, 1:-1], vp[:, 2:]], axis=2).astype(jnp.float32)
    s_lat = jnp.einsum('bnqkgd,bnskd->bnkgqs', qb, kband) * ATTN_SCALE
    s_ctx = jnp.einsum('bnqkgd,bckd->bnkgqc', qb, k_ctx.astype(jnp.float32)) * ATTN_SCALE
    qi = jnp.arange(BLOCK)[:, None]
    kj = jnp.arange(3 * BLOCK)[None, :]
    in_window = jnp.abs(kj - BLOCK - qi) <= WINDOW
    kpos = jnp.arange(nb)[:, None, None] * BLOCK - BLOCK + kj[None]
    mask = in_window[None] & (kpos >= 0) & (kpos < T)
    s_lat = jnp.where(mask[None, :, None, None], s_lat, NEG)
    p = softmax_with_sink(jnp.concatenate([s_lat, s_ctx], axis=-1), sink)
    o = (jnp.einsum('bnkgqs,bnskd->bnqkgd', p[..., :3 * BLOCK], vband)
         + jnp.einsum('bnkgqc,bckd->bnqkgd', p[..., 3 * BLOCK:], v_ctx.astype(jnp.float32)))
    return o.reshape(B, T, ATTN_W).astype(q.dtype)

def centred_shift(u, w):
    T = u.shape[1]
    half = SHIFT_WIDTH // 2
    up = jnp.pad(u, ((0, 0), (half, half), (0, 0)))
    return sum(up[:, j:j + T] * w[j] for j in range(SHIFT_WIDTH))

def rwkv_heads(t):
    return t.reshape(t.shape[:-1] + (RWKV_HEADS, HEAD_DIM))

def rwkv_scan(s0, r, w, k, v, kk, a, reverse):
    def step(S, inp):
        r_t, w_t, k_t, v_t, kk_t, a_t = inp
        S = (S * w_t[:, :, None, :]
             - jnp.einsum('bhvk,bhk->bhv', S, kk_t)[..., None] * (kk_t * a_t)[:, :, None, :]
             + v_t[..., None] * k_t[:, :, None, :])
        return S, jnp.einsum('bhvk,bhk->bhv', S, r_t)

    xs = tuple(jnp.moveaxis(t, 1, 0) for t in (r, w, k, v, kk, a))
    s_fin, ys = lax.scan(step, s0, xs, reverse=reverse)
    return s_fin, jnp.moveaxis(ys, 0, 1)

def rwkv_mix(u, s_fwd, s_bwd, p):
    B, T = u.shape[:2]
    u = centred_shift(u, p['rwkv_shift_w']).astype(jnp.float32)
    r, k, v, gd, wd, ad = jnp.split(u, RWKV_SPLITS, axis=-1)
    wd = wd.reshape(B, T, 2, DECAY_RANK)
    ad = ad.reshape(B, T, 2, ICLR_RANK)
    log_w = -DECAY_SCALE * jax.nn.sigmoid(
        p['rwkv_w0'] + jnp.einsum('btdr,drc->btdc', jnp.tanh(wd), p['rwkv_w_up']))
    a = jax.nn.sigmoid(p['rwkv_a0'] + jnp.einsum('btdr,drc->btdc', ad, p['rwkv_a_up']))
    g = jax.nn.sigmoid(gd) @ p['rwkv_g_up']
    r, k, v = rwkv_heads(r), rwkv_heads(k), rwkv_heads(v)
    kk = k * rwkv_heads(p['rwkv_k_k'])
    kk = kk * lax.rsqrt(jnp.sum(kk * kk, axis=-1, keepdims=True) + 1e-12)
    k_a = rwkv_heads(p['rwkv_k_a'])
    ys = []
    finals = []
    for d, (s0, rev) in enumerate(((s_fwd, False), (s_bwd, True))):
        a_d = rwkv_heads(a[:, :, d])
        k_d = k * (1.0 + (a_d - 1.0) * k_a)
        s_fin, y_d = rwkv_scan(s0.astype(jnp.float32), r, jnp.exp(rwkv_heads(log_w[:, :, d])),
                               k_d, v, kk, a_d, rev)
        ys.append(y_d)
        finals.append(s_fin)
    y = ys[0] + ys[1]
    mean = jnp.mean(y, axis=-1, keepdims=True)
    var = jnp.mean(jnp.square(y - mean), axis=-1, keepdims=True)
    y = ((y - mean) * lax.rsqrt(var + GN_EPS)).reshape(B, T, RWKV_W) * p['rwkv_ln_g'] + p['rwkv_ln_b']
    bonus = (jnp.sum(r * k * p['rwkv_r_k'], axis=-1, keepdims=True) * v).reshape(B, T, RWKV_W)
    return (y + bonus) * g, finals[0], finals[1]

def fourier_mix(u):
    B, T = u.shape[:2]
    z = u.astype(jnp.float32).reshape(B, T, FNET_GROUPS, HEAD_DIM)
    y = jnp.fft.fftn(z, axes=(1, 3), norm='ortho').real
    return y.reshape(B, T, FNET_W).astype(u.dtype)

def split_projection(h, w_in):
    B, T = h.shape[:2]
    q, k, v, u_rwkv, u_fnet = jnp.split(h @ w_in, IN_SPLITS, axis=-1)
    q = q.reshape(B, T, N_Q_HEADS, HEAD_DIM)
    k = k.reshape(B, T, N_KV_HEADS, HEAD_DIM)
    v = v.reshape(B, T, N_KV_HEADS, HEAD_DIM)
    return q, k, v, u_rwkv, u_fnet

def merge_and_ffn(x, o_attn, o_rwkv, o_fnet, mod, p):
    _, _, g1, sh2, sc2, g2 = mod
    o = jnp.concatenate([o_attn.astype(x.dtype), o_rwkv.astype(x.dtype), o_fnet.astype(x.dtype)],
                        axis=-1) @ p['w_out']
    x = x + g1 * o
    h = modulate(rmsnorm(x, p['norm_ffn_g']), sh2, sc2)
    gt, up = jnp.split(h @ p['ffn_w_in'], 2, axis=-1)
    return x + g2 * ((jax.nn.silu(gt) * up) @ p['ffn_w_out'])

def context_layer(x, mod_vec, p):
    mod = jnp.split(mod_vec, 6, axis=-1)
    h = modulate(rmsnorm(x, p['norm_mix_g']), mod[0], mod[1])
    q, k, v, u_r, u_f = split_projection(h, p['w_in'])
    o_attn = context_attention(q, k, v, p['attn_sink'])
    s0 = jnp.zeros((x.shape[0], RWKV_HEADS, HEAD_DIM, HEAD_DIM), jnp.float32)
    o_rwkv, s_f, s_b = rwkv_mix(u_r, s0, s0, p)
    o_fnet = fourier_mix(u_f)
    x = merge_and_ffn(x, o_attn, o_rwkv, o_fnet, mod, p)
    return x, k, v, jnp.stack([s_f, s_b], axis=1)

def latent_layer(x, mod_vec, k_ctx, v_ctx, s_ctx, p):
    mod = jnp.split(mod_vec[:, None, :], 6, axis=-1)
    h = modulate(rmsnorm(x, p['norm_mix_g']), mod[0], mod[1])
    q, k, v, u_r, u_f = split_projection(h, p['w_in'])
    o_attn = latent_attention(axial_rope(q), axial_rope(k), v, k_ctx, v_ctx, p['attn_sink'])
    o_rwkv, _, _ = rwkv_mix(u_r, s_ctx[:, 0], s_ctx[:, 1], p)
    o_fnet = fourier_mix(u_f)
    return merge_and_ffn(x, o_attn, o_rwkv, o_fnet, mod, p)

def setup_inputs(seed: int = 0) -> dict:
    key = jax.random.key(seed)
    ks = jax.random.split(key, 28)

    def n(k, shape, s):
        return s * jax.random.normal(k, shape, jnp.float32)

    L = DEPTH
    return {
        'x_prompt': n(ks[0], (BATCH, SEQ, D_MODEL), 1.0),
        'x_sample': n(ks[1], (DEC_BATCH, DEC_SEQ, D_MODEL), 1.0),
        'cache_k': n(ks[2], (DEC_BATCH, L, PAST_LEN, N_KV_HEADS, HEAD_DIM), 1.0),
        'cache_v': n(ks[3], (DEC_BATCH, L, PAST_LEN, N_KV_HEADS, HEAD_DIM), 1.0),
        'state_rwkv': n(ks[4], (DEC_BATCH, L, 2, RWKV_HEADS, HEAD_DIM, HEAD_DIM), 0.5),
        'c': n(ks[5], (DEC_BATCH, D_MODEL), 1.0),
        'c_ctx': n(ks[6], (D_MODEL,), 1.0),
        'w_ada': n(ks[7], (L, D_MODEL, 6 * D_MODEL), 0.3 * D_MODEL ** -0.5),
        'b_ada': n(ks[8], (L, 6 * D_MODEL), 0.02),
        'norm_mix_g': 1.0 + n(ks[9], (L, D_MODEL), 0.05),
        'norm_ffn_g': 1.0 + n(ks[10], (L, D_MODEL), 0.05),
        'w_in': n(ks[11], (L, D_MODEL, IN_W), D_MODEL ** -0.5),
        'w_out': n(ks[12], (L, MIX_W, D_MODEL), MIX_W ** -0.5),
        'attn_sink': n(ks[13], (L, N_Q_HEADS), 0.5),
        'rwkv_shift_w': jnp.array([0.25, 0.5, 0.25], jnp.float32)[None, :, None]
                        + n(ks[14], (L, SHIFT_WIDTH, RWKV_IN_W), 0.05),
        'rwkv_w0': jax.random.uniform(ks[15], (L, 2, RWKV_W), jnp.float32, -5.0, 1.0),
        'rwkv_w_up': n(ks[16], (L, 2, DECAY_RANK, RWKV_W), 0.1 * DECAY_RANK ** -0.5),
        'rwkv_a0': n(ks[17], (L, 2, RWKV_W), 0.5),
        'rwkv_a_up': n(ks[18], (L, 2, ICLR_RANK, RWKV_W), 0.1 * ICLR_RANK ** -0.5),
        'rwkv_g_up': n(ks[19], (L, GATE_RANK, RWKV_W), GATE_RANK ** -0.5),
        'rwkv_k_k': 0.85 + n(ks[20], (L, RWKV_W), 0.05),
        'rwkv_k_a': 1.0 + n(ks[21], (L, RWKV_W), 0.05),
        'rwkv_r_k': n(ks[22], (L, RWKV_HEADS, HEAD_DIM), 0.1),
        'rwkv_ln_g': 1.0 + n(ks[23], (L, RWKV_W), 0.05),
        'rwkv_ln_b': n(ks[24], (L, RWKV_W), 0.02),
        'ffn_w_in': n(ks[25], (L, D_MODEL, 2 * D_FF), D_MODEL ** -0.5),
        'ffn_w_out': n(ks[26], (L, D_FF, D_MODEL), D_FF ** -0.5),
        'norm_final_g': 1.0 + n(ks[27], (D_MODEL,), 0.05),
    }

def reference(x_prompt, x_sample, cache_k, cache_v, state_rwkv, c, c_ctx,
              w_ada, b_ada, norm_mix_g, norm_ffn_g, w_in, w_out, attn_sink,
              rwkv_shift_w, rwkv_w0, rwkv_w_up, rwkv_a0, rwkv_a_up, rwkv_g_up,
              rwkv_k_k, rwkv_k_a, rwkv_r_k, rwkv_ln_g, rwkv_ln_b,
              ffn_w_in, ffn_w_out, norm_final_g):
    y_p = x_prompt
    y_s = x_sample
    new_k, new_v, new_s = [], [], []
    for l in range(DEPTH):
        p = {
            'norm_mix_g': norm_mix_g[l], 'norm_ffn_g': norm_ffn_g[l],
            'w_in': w_in[l], 'w_out': w_out[l], 'attn_sink': attn_sink[l],
            'rwkv_shift_w': rwkv_shift_w[l], 'rwkv_w0': rwkv_w0[l], 'rwkv_w_up': rwkv_w_up[l],
            'rwkv_a0': rwkv_a0[l], 'rwkv_a_up': rwkv_a_up[l], 'rwkv_g_up': rwkv_g_up[l],
            'rwkv_k_k': rwkv_k_k[l], 'rwkv_k_a': rwkv_k_a[l], 'rwkv_r_k': rwkv_r_k[l],
            'rwkv_ln_g': rwkv_ln_g[l], 'rwkv_ln_b': rwkv_ln_b[l],
            'ffn_w_in': ffn_w_in[l], 'ffn_w_out': ffn_w_out[l],
        }
        mod_ctx = jax.nn.silu(c_ctx) @ w_ada[l] + b_ada[l]
        mod_lat = jax.nn.silu(c) @ w_ada[l] + b_ada[l]
        y_p, k_l, v_l, s_l = context_layer(y_p, mod_ctx, p)
        y_s = latent_layer(y_s, mod_lat, cache_k[:, l], cache_v[:, l], state_rwkv[:, l], p)
        new_k.append(k_l)
        new_v.append(v_l)
        new_s.append(s_l)
    y_prompt = rmsnorm(y_p, norm_final_g)
    y_sample = rmsnorm(y_s, norm_final_g)
    new_cache_k = jnp.stack(new_k, axis=1)
    new_cache_v = jnp.stack(new_v, axis=1)
    new_state_rwkv = jnp.stack(new_s, axis=1)
    return (y_prompt, y_sample, new_cache_k, new_cache_v, new_state_rwkv)


_drawn_inputs = setup_inputs


def setup_inputs(seed=0):
    import zlib

    import numpy as np

    out = dict(_drawn_inputs(seed))
    spreads = {}
    factors = {'cache_k': 6.656,
     'cache_v': 5.477,
     'state_rwkv': 7.99,
     'norm_ffn_g': 4.668,
     'attn_sink': 39.049,
     'rwkv_w_up': 6.491,
     'rwkv_r_k': 3.675,
     'rwkv_ln_g': 8.0,
     'rwkv_ln_b': 35.07}
    for name, (base, spread) in spreads.items():
        noise = np.random.default_rng([zlib.crc32(name.encode()), seed]).standard_normal(out[name].shape)
        drawn = base * np.exp(spread * noise) if base else spread * noise
        out[name] = __import__('jax').numpy.asarray(drawn.astype(out[name].dtype))
    for name, factor in factors.items():
        out[name] = (out[name] * factor).astype(out[name].dtype)
    return out
```

```python
import math
import numpy as np
import concourse.bass as bass
from concourse import mybir
from contextlib import ExitStack

D = 1024
NC_ = 128
NL = 512
T = NL + NC_
DEPTH = 2
KT = D // 128
DFF = 2816
FT = DFF // 128
HD = 64
IN_W = 2176
CH = 64
NCH = T // CH
LCH = NL // CH
DECAY = 0.6065306597126334
GN_EPS = 64e-5
RMS_EPS = 1e-6
STREAMS = ((0, NL), (NL, T))
LEVELS = (1, 2, 4, 8, 16, 32)
SLOTS = 3
SLOT_W = FT * 128

PR_ADA, PR_NMIX, PR_NFFN, PR_SHIFT, PR_W0, PR_A0, PR_KK, PR_KA, PR_RK, PR_LNG, PR_LNB = (
    0, 48, 56, 64, 91, 95, 99, 101, 103, 105, 107)
NPR = 109

def chunk_order():
    order = [("ada", i) for i in range(8)]
    proj = [("rw", i) for i in range(5)] + [("q", 0), ("q", 1), ("kv", 0), ("fn", 0)]
    ada = 8
    for n, p in enumerate(proj):
        order.append(p)
        if n < 8:
            order += [("ada", ada), ("ada", ada + 1)]
            ada += 2
    order += [("dftc", 0), ("dfts", 0)]
    order += [("wo", i) for i in range(4)] + [("f1", i) for i in range(FT)] + [("f2", i) for i in range(KT)]
    return order


CHUNKS = chunk_order()
CHUNK_AT = {c: i for i, c in enumerate(CHUNKS)}
NCHUNK = len(CHUNKS)
assert NCHUNK % SLOTS == 0
DMAS = {"ada": 1, "rw": 1, "q": 4, "kv": 1, "fn": 1, "dftc": 3, "dfts": 2, "wo": 3, "f1": 2, "f2": 1}


def ready_counts():
    tot, out = [0] * SLOTS, []
    for i, (kind, _) in enumerate(CHUNKS):
        tot[i % SLOTS] += 16 * DMAS[kind]
        out.append(tot[i % SLOTS])
    return out, tot


READY, READY_TOT = ready_counts()


LAST_ITEM = {("q", i): ("q", 2 * i + 1) for i in range(2)}
LAST_ITEM.update({("rw", i): ("rw", min(2 * i + 1, 8)) for i in range(5)})
LAST_ITEM.update({("kv", 0): ("v", 0), ("fn", 0): ("fn", 1), ("dftc", 0): ("ft2", 1), ("dfts", 0): ("ft2", 1)})
LAST_ITEM.update({("wo", i): ("out", 2 * i + 1) for i in range(4)})
LAST_ITEM.update({("f1", i): ("up", i) for i in range(FT)})
LAST_ITEM.update({("f2", i): ("f2", i) for i in range(KT)})


def item_order():
    o = [("norm", 0), ("small", 0)]
    o += [("rw", m) for m in range(9)]
    o += [("q", 0), ("q", 1), ("swap", 0), ("q", 2), ("swap", 1), ("q", 3), ("swap", 2),
          ("k", 0), ("swap", 3), ("v", 0), ("swap", 4), ("fn", 0), ("kvT", 0), ("fn", 1)]

    def prep(t):
        return [("w", t, 0), ("w", t, 1), ("a", t, 0), ("a", t, 1), ("kk", t), ("bonus", t)]

    def attn(blocks):
        r = []
        for b in blocks:
            r += [("s", b, i) for i in range(8)] + [("oT", b)]
        return r

    o += prep(0) + [("ft1", i) for i in range(5)] + [("ft2", 0), ("ft2", 1)] + attn(ATT_A)
    o += prep(1) + attn(ATT_B)
    o += [("mean", 0), ("mean", 1), ("var", 0), ("var", 1), ("g", 0), ("g", 1)]
    o += [("out", m) for m in range(KT)] + [("norm", 1)]
    for i in range(FT):
        o += [("gate", i), ("up", i)]
    o += [("f2", m) for m in range(KT)]
    return o


ATT_A = (0, 1)
ATT_B = (2, 3, 4)
ITEMS = item_order()
ITEM_AT = {x: i for i, x in enumerate(ITEMS)}
NITEM = len(ITEMS)
assert NITEM % 2 == 0 and len(ITEM_AT) == NITEM

def key_tiles(b):
    if b == 4:
        return [("cur", 4)]
    r = []
    if b > 0:
        r.append(("lat", b - 1))
    r += [("lat", b), ("cache", 0)]
    if b < 3:
        r.append(("lat", b + 1))
    return r


def mask_cols(b):
    if b == 4:
        return 128, 256
    return (0 if b > 0 else 128), (512 if b < 3 else 384)


GROUPS = [[(0, 0, 0), (1, 0, 1), (2, 1, 3), (3, 1, 2)],
          [(0, 0, 2), (1, 0, 3), (2, 1, 1), (3, 1, 0)],
          [(0, 0, 4), (2, 1, 4)]]
NPAIR = sum(len(g) for g in GROUPS)


def chain_steps(group):
    out = []
    per_dir = {0: [], 1: []}
    for p, d, t in group:
        for hf in ((0, 1) if d == 0 else (1, 0)):
            per_dir[d].append((p, d, t, hf, 2 * t + hf))
    for a, b in zip(per_dir[0], per_dir[1]):
        out += [a, b]
    return out


def first_touch(g, d, t):
    return (g == 0) or (g == 2 and d == 0)


def needs_state(chunk, d):
    return chunk != (LCH - 1 if d == 0 else 0)


def y_order(group):
    seen, out = {}, []
    for s in chain_steps(group):
        seen[s[0]] = seen.get(s[0], 0) + 1
        if seen[s[0]] == 2:
            out.append(s[:3])
    return out


def state_plan():
    plan, n = {}, 0
    for ht in range(2):
        for g, group in enumerate(GROUPS):
            if g != 1:
                cur = {0: (0, None), 1: (0, None)}
            for (p, d, t, hf, ck) in chain_steps(group):
                plan[(ht, g, d, ck)] = cur[d]
                if needs_state(ck, d):
                    n += 1
                    cur[d] = (1 - cur[d][0], n)
    return plan


class Signal:

    def __init__(self, sem, per_layer, primed=0):
        self.sem, self.per, self.made, self.primed = sem, per_layer, 0, primed

    def __call__(self, n=1):
        self.made += n
        return self.sem

    def upto(self, l, n):
        assert n + self.primed > 0
        return l * self.per + n + self.primed

    def check(self, name, extra=0):
        if self.made - extra != self.per:
            print("SIGNAL", name, "makes", self.made - extra, "per layer, declared", self.per)
        return self.made - extra == self.per


class Own:

    def __init__(self, eng, sem, per_layer):
        self.eng, self.sem, self.per, self.n, self.l, self.most = eng, sem, per_layer, 0, 0, 0

    def after(self, ins):
        self.n += 1
        ins.then_inc(self.sem, 1)
        self.most = max(self.most, self.n)
        self.eng.wait_ge(self.sem, self.l * self.per + self.n)


DVE_CHAIN, POOL_CHAIN = 117, 2


def build(nc, I, O):
    f32 = mybir.dt.float32
    ALU = mybir.AluOpType
    ACT = mybir.ActivationFunctionType
    AX = mybir.AxisListType
    MUL, ADD, SUB, MAX = ALU.mult, ALU.add, ALU.subtract, ALU.max
    ctx = ExitStack()
    with ctx:
        def sb(name, shape):
            return ctx.enter_context(nc.sbuf_tensor(name, shape, f32))

        signals = {}

        def sig(name, per, primed=0):
            s = Signal(ctx.enter_context(nc.semaphore(name)), per, primed)
            signals[name] = s
            return s

        def sem(name):
            return ctx.enter_context(nc.semaphore(name))

        x = sb("x", [128, KT, T])
        h = sb("h", [128, KT, T])
        ring = sb("ring", [128, SLOTS, SLOT_W])
        mix = sb("mix", [128, 25736])
        MN = sb("MN", [128, 4, 2, 2, 128])
        St = sb("St", [128, 2, 2, 128])
        masks = sb("masks", [128, 2, 256])
        lvl = sb("lvl", [128, 2, 6, 128])
        attmask = sb("attmask", [128, 512])
        mats = sb("mats", [128, 5, 128])
        reset = sb("reset", [128, T])
        lora = sb("lora", [128, 3, 256])
        prow = sb("prow", [NPR, 128])
        par = sb("par", [128, NPR])
        cvec = sb("cvec", [128, 24])
        csil = sb("csil", [128, KT, 2])
        csil_s = sb("csil_s", [128, 16])
        mod = sb("mod", [128, 48, 2])
        gain = sb("gain", [128, 3, KT, 2])
        sink = sb("sink", [128, 8])
        omka = sb("omka", [128, 2])
        eps = sb("eps", [128, 3])
        mid = sb("mid", [128, 2, NCH])
        end = sb("end", [128, 2, NCH])
        emid = sb("emid", [128, 2, NCH])
        eend = sb("eend", [128, 2, NCH])
        dec = sb("dec", [128, 2, NCH])
        negm = sb("negm", [128, 2, 8])
        den = sb("den", [128, 2, 8])
        esk = sb("esk", [128, 2, 8])
        kcT = sb("kcT", [128, 128])
        ckv = sb("ckv", [128, 2, 128])
        kvout = sb("kvout", [128, 128])

        ident, swapm, onesD, ones64, mean64 = (mats[:, i, :] for i in range(5))

        def mixv(at, n):
            return mix[:, at:at + n]

        def rows(at, n):
            return mix[:, at:at + n * T].rearrange("p (a t) -> p a t", t=T)

        ush = rows(0, 9)
        qt = rows(5760, 4)
        kt = mixv(8320, T)
        vtok = mixv(8960, T)
        uf = rows(9600, 2)
        S2 = rows(10880, 2)
        CC = rows(12160, 2)
        E0 = 13440
        raw = mix[:, E0:E0 + 1286].rearrange("p (a t) -> p a t", t=643)
        e01 = rows(E0, 2)
        KK = mixv(14726, T)
        rot = mixv(15366, T)
        hid = rows(0, FT)
        PB = 16006
        PW = 2432
        pb = [PB + PW * p for p in range(4)]
        assert pb[3] + PW <= 25736
        LP = [mix[:, b:b + 1024].rearrange("p (a t) -> p a t", a=2) for b in pb]
        Yi = [mix[:, b + 1024:b + 1280].rearrange("p (a t) -> p a t", a=2) for b in pb]
        Xi = [mix[:, b + 1280:b + 1536].rearrange("p (a t) -> p a t", a=2) for b in pb]
        P1 = [mix[:, b + 1536:b + 1792].rearrange("p (a t) -> p a t", a=2) for b in pb]
        TOK = [mix[:, b + 1792:b + 2176].rearrange("p (a t) -> p a t", a=3) for b in pb]
        W1A = [mix[:, b + 2176:b + 2432].rearrange("p (a t) -> p a t", a=2) for b in pb]
        UG = P1
        Qt = [mix[:, b + 1280:b + 1408] for b in pb]
        rope = mix[:, PB:PB + 1024].rearrange("p (a t) -> p a t", a=2)
        Z = mix[:, PB:PB + 2560].rearrange("p (a t) -> p a t", a=5)
        Pm = mix[:, PB:PB + 1536].rearrange("p (a t) -> p a t", a=3)
        PT = mix[:, PB + 1536:PB + 2560].rearrange("p (a t) -> p a t", a=2)
        otok = mix[:, PB + 2560:PB + 3584].rearrange("p (a t) -> p a t", a=2)
        stout = rot[:, 0:256].rearrange("p (a t) -> p a t", a=2)
        s0in = sb("s0in", [128, 2, 128])
        xin = mix[:, 0:5 * D].rearrange("p (a t) -> p a t", a=5)
        crow = mix[0:24, 5 * D:5 * D + 128]
        yout = mix[:, 0:2 * D].rearrange("p (a t) -> p a t", a=2)

        PS = ctx.enter_context(nc.psum_tensor("PS", [128, 8, 512], f32))
        ps = [PS[:, i, :] for i in range(8)]

        ld_const = sem("ld_const")
        ld_par = sig("ld_par", 16 * 21)
        ld_rope = sig("ld_rope", 16)
        ld_state = [sig(f"ld_state{t}", 64) for t in range(2)]
        w_ready = [sig(f"w_ready{s}", READY_TOT[s]) for s in range(SLOTS)]
        acc_ready = sig("acc_ready", NITEM)
        acc_free = [sig(f"acc_free{i}", NITEM // 2, primed=1) for i in range(2)]
        sq_ready = sig("sq_ready", 2 * KT)
        sq_used = sig("sq_used", 2 * (KT - 1))
        h_scaled = sig("h_scaled", 2 * KT)
        h_ready = sig("h_ready", 2 * KT)
        gain_ready = sig("gain_ready", 2)
        ada_done = sig("ada_done", 24)
        par_ready = sig("par_ready", 1, primed=1)
        conv_out = sig("conv_out", 9)
        pads_zero = sig("pads_zero", 1)
        rot_raw = sig("rot_raw", 5)
        rot_cos = sig("rot_cos", 5)
        rot_done = sig("rot_done", 5, primed=1)
        kv_stored = sig("kv_stored", 32)
        lora_in = sig("lora_in", 1)
        kk_raw = sig("kk_raw", 2)
        kk_sq = sig("kk_sq", 2)
        rk_prod = sig("rk_prod", 2)
        cum_ready = sig("cum_ready", 2)
        exps_ready = sig("exps_ready", 2)
        kk_ready = sig("kk_ready", 2)
        ar_done = sig("ar_done", 2)
        scaled_ready = sig("scaled_ready", 2)
        p_ready = sig("p_ready", 40)
        p_exp = sig("p_exp", 40)
        pt_ps = sig("pt_ps", 40, primed=1)
        pt_sb = sig("pt_sb", 40, primed=1)
        pv_done = sig("pv_done", 40, primed=1)
        esk_in = sig("esk_in", 5)
        esk_ready = sig("esk_ready", 5)
        o_ready = sig("o_ready", 5, primed=1)
        mn_zero = sem("mn_zero")
        ctx_zero = sig("ctx_zero", 2)
        n2 = 2 * NPAIR
        s0_ps = sig("s0_ps", 4, primed=1)
        s0_sb = sig("s0_sb", 4)
        tok_ps, tok_sb = sig("tok_ps", n2), sig("tok_sb", n2)
        prod_ps, prod_sb = sig("prod_ps", 2 * n2), sig("prod_sb", 2 * n2)
        inv0_sb = sig("inv0_sb", n2)
        xt_ps, xt_sb = sig("xt_ps", 5 * n2), sig("xt_sb", 5 * n2)
        p1_ps, p1_sb = sig("p1_ps", 5 * n2), sig("p1_sb", 5 * n2)
        yu_ps, yu_sb = sig("yu_ps", 5 * n2), sig("yu_sb", 5 * n2)
        w1_ps, w1_sb = sig("w1_ps", n2), sig("w1_sb", n2)
        ug_ps, ug_sb = sig("ug_ps", n2), sig("ug_sb", n2)
        qmn_ps, qmn_sb = sig("qmn_ps", n2), sig("qmn_sb", n2)
        nstep = 2 * sum(1 for g in GROUPS for s in chain_steps(g) if needs_state(s[4], s[1]))
        st_ps, st_sb = sig("st_ps", nstep), sig("st_sb", nstep)
        y_ps, y_sb = sig("y_ps", n2), sig("y_sb", n2)
        fin_ps, fin_sb, fin_st = sig("fin_ps", 2), sig("fin_sb", 2), sig("fin_st", 128)
        ysq_ready = sig("ysq_ready", 2)
        hid_sig = sig("hid_sig", FT)
        xT_ps, xT_sb, c_ready = sem("xT_ps"), sem("xT_sb"), sem("c_ready")
        yT_ps, yT_sb, y_stored = sem("yT_ps"), sem("yT_sb"), [sem("y_stored0"), sem("y_stored1")]
        dve_own, pool_own = sem("dve_own"), sem("pool_own")
        sp_passed, pool_passed = sem("sp_passed"), sem("pool_passed")

        def acc_item(name):
            i = ITEM_AT[name]
            return i, ps[i % 2], ps[2 + i % 2]

        def pair_index(ht, g, n):
            return ht * NPAIR + sum(len(q) for q in GROUPS[:g]) + n

        def taken(e, l, name, settled=None):
            i = ITEM_AT[name]
            e.wait_ge(acc_free[i % 2].sem, acc_free[i % 2].upto(l, i // 2 + 1))
            if settled:
                settled()

        def layer_before(e, l, settled=None):
            for f in acc_free:
                e.wait_ge(f.sem, f.upto(l, 0))
            if settled:
                settled()

        PLAN = state_plan()

        block = ctx.enter_context(nc.Block())

        @block.sync
        def _(e):
            def settled():
                e.sem_inc(sp_passed)

            e.dma_start(xin[:, 0:4, :], I["x_sample"][0].rearrange("(a p) d -> p a d", p=128)).then_inc(ld_const, 16)
            e.dma_start(xin[:, 4, :], I["x_prompt"][0]).then_inc(ld_const, 16)
            e.dma_start(crow[0:8, :], I["c"][0].rearrange("(a p) -> a p", p=128)).then_inc(ld_const, 16)
            e.dma_start(crow[8:16, :], I["c_ctx"].rearrange("(a p) -> a p", p=128)).then_inc(ld_const, 16)
            e.dma_start(crow[16:24, :], I["norm_final_g"].rearrange("(a p) -> a p", p=128)).then_inc(ld_const, 16)
            e.dma_start(mats[:, :, :], I["t_mats"]).then_inc(ld_const, 16)
            e.dma_start(masks[:, :, :], I["t_masks"]).then_inc(ld_const, 16)
            e.dma_start(lvl[:, :, :, :], I["t_lvl"]).then_inc(ld_const, 16)
            e.dma_start(attmask[:, :], I["t_attmask"]).then_inc(ld_const, 16)
            e.dma_start(reset[:, :], I["t_reset"]).then_inc(ld_const, 16)
            with e.Fori(0, DEPTH) as l:
                e.wait_ge(par_ready.sem, par_ready.upto(l, 0))
                settled()

                def prm(at, n, src):
                    e.dma_start(prow[at:at + n, :], src.rearrange("(a p) -> a p", p=128)).then_inc(ld_par(16), 16)

                prm(PR_ADA, 48, I["b_ada"][l])
                prm(PR_NMIX, 8, I["norm_mix_g"][l])
                prm(PR_NFFN, 8, I["norm_ffn_g"][l])
                for j in range(3):
                    prm(PR_SHIFT + 9 * j, 9, I["rwkv_shift_w"][l, j])
                for d in range(2):
                    prm(PR_W0 + 2 * d, 2, I["rwkv_w0"][l, d])
                    prm(PR_A0 + 2 * d, 2, I["rwkv_a0"][l, d])
                prm(PR_KK, 2, I["rwkv_k_k"][l])
                prm(PR_KA, 2, I["rwkv_k_a"][l])
                prm(PR_RK, 2, I["rwkv_r_k"][l].rearrange("h d -> (h d)"))
                prm(PR_LNG, 2, I["rwkv_ln_g"][l])
                prm(PR_LNB, 2, I["rwkv_ln_b"][l])
                layer_before(e, l, settled)
                e.dma_start(lora[:, 0, :], I["rwkv_w_up"][l].rearrange("d r c -> (d r) c")).then_inc(ld_par(16), 16)
                e.dma_start(lora[:, 1, :], I["rwkv_a_up"][l].rearrange("d r c -> (d r) c")).then_inc(ld_par(16), 16)
                e.dma_start(lora[:, 2, :], I["rwkv_g_up"][l]).then_inc(ld_par(16), 16)
                e.dma_start(ckv[:, 0, :], I["cache_k"][0, l].rearrange("s h d -> s (h d)")).then_inc(ld_par(16), 16)
                e.dma_start(ckv[:, 1, :], I["cache_v"][0, l].rearrange("s h d -> s (h d)")).then_inc(ld_par(16), 16)
                e.dma_start(sink[:, :], I["attn_sink"][l].partition_broadcast(128)).then_inc(ld_par(16), 16)
                e.dma_start(rope, I["t_rope"]).then_inc(ld_rope(16), 16)
                for n, (kind, i) in enumerate(CHUNKS):
                    if n >= SLOTS:
                        old = CHUNKS[n - SLOTS]
                        if old[0] == "ada":
                            e.wait_ge(ada_done.sem, ada_done.upto(l, old[1] + 1))
                            settled()
                        else:
                            e.wait_ge(acc_ready.sem, acc_ready.upto(l, ITEM_AT[LAST_ITEM[old]] + 1))
                            settled()
                    sl = n % SLOTS
                    dst = ring[:, sl, 0:2048].rearrange("p (k c) -> p k c", k=KT)
                    done = w_ready[sl]

                    def src(w, c0, n_):
                        return w[l, :, c0:c0 + n_].rearrange("(k p) c -> p k c", p=128)

                    if kind == "ada":
                        e.dma_start(dst, src(I["w_ada"], 256 * i, 256)).then_inc(done(16), 16)
                    elif kind == "rw":
                        w_ = 256 if i < 4 else 128
                        e.dma_start(dst[:, :, 0:w_], src(I["w_in"], 768 + 256 * i, w_)).then_inc(done(16), 16)
                    elif kind == "q":
                        for j in range(2):
                            for g in range(2):
                                e.dma_start(dst[:, :, 128 * j + 64 * g:128 * j + 64 * g + 64],
                                            src(I["w_in"], 128 * i + 64 * j + 256 * g, 64)).then_inc(done(16), 16)
                    elif kind == "kv":
                        e.dma_start(dst, src(I["w_in"], 512, 256)).then_inc(done(16), 16)
                    elif kind == "fn":
                        e.dma_start(dst, src(I["w_in"], 1920, 256)).then_inc(done(16), 16)
                    elif kind in ("dftc", "dfts"):
                        e.dma_start(ring[:, sl, 0:2048].rearrange("p (k c) -> p k c", k=4),
                                    I["t_" + kind]).then_inc(done(16), 16)
                        e.dma_start(ring[:, sl, 2048:2176], I["t_" + kind + "x"]).then_inc(done(16), 16)
                        if kind == "dftc":
                            e.dma_start(ring[:, sl, 2176:2432], I["t_chan"]).then_inc(done(16), 16)
                    elif kind == "wo":
                        wo = I["w_out"]
                        c0 = 256 * i
                        for g in range(2):
                            e.dma_start(dst[64 * g:64 * g + 64, 0:4, :],
                                        wo[l, 256 * g:256 * g + 256, c0:c0 + 256].rearrange(
                                            "(k p) c -> p k c", p=64)).then_inc(done(16), 16)
                        e.dma_start(dst[:, 4:8, :], wo[l, 512:1024, c0:c0 + 256].rearrange(
                            "(k p) c -> p k c", p=128)).then_inc(done(16), 16)
                    elif kind == "f1":
                        for g in range(2):
                            e.dma_start(dst[:, :, 128 * g:128 * g + 128],
                                        src(I["ffn_w_in"], DFF * g + 128 * i, 128)).then_inc(done(16), 16)
                    else:
                        e.dma_start(ring[:, sl, :].rearrange("p (k c) -> p k c", k=FT),
                                    I["ffn_w_out"][l, :, 128 * i:128 * i + 128].rearrange(
                                        "(k p) c -> p k c", p=128)).then_inc(done(16), 16)
            for t in range(5):
                e.wait_ge(yT_sb, t + 1)
                dst = O["y_s"][0, 128 * t:128 * t + 128, :] if t < 4 else O["y_p"][0]
                e.dma_start(dst, yout[:, t % 2, :]).then_inc(y_stored[t % 2], 16)
            e.wait_ge(y_stored[0], 48)
            e.wait_ge(y_stored[1], 32)

        @block.gpsimd
        def _(e):
            own = Own(e, pool_own, POOL_CHAIN)

            def settled():
                e.sem_inc(pool_passed)

            nc.gpsimd.memset(MN[:, :, :, :, :], 0.0).then_inc(mn_zero, 1)
            nc.gpsimd.memset(s0in[:, :, :], 0.0).then_inc(mn_zero, 1)
            nc.gpsimd.memset(eps[:, 0:1], RMS_EPS).then_inc(mn_zero, 1)
            nc.gpsimd.memset(eps[:, 1:2], 1e-12).then_inc(mn_zero, 1)
            nc.gpsimd.memset(eps[:, 2:3], GN_EPS).then_inc(mn_zero, 1)
            e.wait_ge(mn_zero, 5)
            e.wait_ge(xT_ps, 11)
            with e.Fori(0, DEPTH) as l:
                own.l, own.n = l, 0
                layer_before(e, l, settled)
                nc.gpsimd.memset(raw[:, :, 0:1], 0.0)
                nc.gpsimd.memset(raw[:, :, 513:514], 0.0)
                nc.gpsimd.memset(raw[:, :, 642:643], 0.0).then_inc(pads_zero(), 1)
                e.wait_ge(ld_rope.sem, ld_rope.upto(l, 16))
                settled()
                for r in range(5):
                    dst = qt[:, r, 0:NL] if r < 4 else kt[:, 0:NL]
                    e.wait_ge(rot_raw.sem, rot_raw.upto(l, r + 1))
                    settled()
                    nc.gpsimd.tensor_tensor(dst, raw[:, r % 2, 0:NL], rope[:, 0, :], MUL).then_inc(rot_cos(), 1)
                taken(e, l, ("kvT", 0), settled)
                e.dma_start(O["new_k"][0, l].rearrange("s h d -> s (h d)"), kvout[:, :]).then_inc(kv_stored(16), 16)
                e.dma_start(O["new_v"][0, l].rearrange("s h d -> s (h d)"), vtok[:, 512:640]).then_inc(kv_stored(16), 16)

                def prep(t):
                    e.wait_ge(conv_out.sem, conv_out.upto(l, 9))
                    settled()
                    e.wait_ge(acc_ready.sem, acc_ready.upto(l, ITEM_AT[("w", t, 0)] + 1))
                    settled()
                    nc.gpsimd.tensor_scalar(KK, ush[:, 2 + t, :], par[:, PR_KK + t:PR_KK + t + 1], None,
                                            MUL).then_inc(kk_raw(), 1)
                    own.after(nc.gpsimd.tensor_tensor(e01[:, 1, :], ush[:, t, :], ush[:, 2 + t, :], MUL))
                    settled()
                    nc.gpsimd.tensor_scalar(e01[:, 1, :], e01[:, 1, :], par[:, PR_RK + t:PR_RK + t + 1], None,
                                            MUL).then_inc(rk_prod(), 1)
                    e.wait_ge(s0_ps.sem, s0_ps.upto(l, 2 * t))
                    settled()
                    for d in range(2):
                        for g in range(2):
                            e.dma_start(s0in[64 * g:64 * g + 64, d, 64 * g:64 * g + 64],
                                        I["state_rwkv"][0, l, d, 2 * t + g]).then_inc(ld_state[t](16), 16)
                    e.wait_ge(exps_ready.sem, exps_ready.upto(l, t + 1))
                    settled()
                    e.wait_ge(kk_ready.sem, kk_ready.upto(l, t + 1))
                    settled()
                    rb = ush[:, t:t + 1, :].to_broadcast([128, 2, T])
                    kb = KK.unsqueeze(1).to_broadcast([128, 2, T])
                    nc.gpsimd.tensor_tensor(h[:, 2:4, :], h[:, 2:4, :], rb, MUL)
                    nc.gpsimd.tensor_tensor(h[:, 0:2, :], h[:, 0:2, :], kb, MUL).then_inc(ar_done(), 1)

                prep(0)
                prep(1)
                for t in range(2):
                    e.wait_ge(fin_sb.sem, fin_sb.upto(l, t + 1))
                    settled()
                    for d in range(2):
                        for g in range(2):
                            e.dma_start(O["new_s"][0, l, d, 2 * t + g],
                                        stout[64 * g:64 * g + 64, d, 64 * g:64 * g + 64]).then_inc(fin_st(16), 16)
                    e.wait_ge(fin_st.sem, fin_st.upto(l, 64 * (t + 1)))
                    settled()
                e.wait_ge(kv_stored.sem, kv_stored.upto(l, 32))
                settled()
            assert own.most == POOL_CHAIN, own.most

        @block.tensor
        def _(e):
            mm = nc.tensor.matmul
            tr = nc.tensor.transpose

            e.wait_ge(ld_const, 16 * 10)
            for t in range(5):
                for g in range(2):
                    n = 2 * t + g
                    if n >= 2:
                        e.wait_ge(xT_sb, n - 1)
                    for k in range(4):
                        last = tr(ps[4 + n % 2][:, 128 * k:128 * k + 128],
                                  xin[:, t, 512 * g + 128 * k:512 * g + 128 * k + 128], ident)
                    last.then_inc(xT_ps, 1)
            tr(ps[6][:, 0:24], crow, ident[0:24, 0:24]).then_inc(xT_ps, 1)
            e.wait_ge(c_ready, 3)
            e.wait_ge(xT_sb, 10)

            with e.Fori(0, DEPTH) as l:
                def begin(name):
                    i, lat, cx = acc_item(name)
                    e.wait_ge(acc_free[i % 2].sem, acc_free[i % 2].upto(l, i // 2))
                    return lat, cx

                def chunk(name):
                    n = CHUNK_AT[name]
                    e.wait_ge(w_ready[n % SLOTS].sem, w_ready[n % SLOTS].upto(l, READY[n]))
                    return ring[:, n % SLOTS, :]

                def both(lat, cx, w, k, n, v):
                    mm(lat[:, :], w, v[:, 0:NL], start=(k == 0), stop=(k == n - 1))
                    return mm(cx[:, 0:NC_], w, v[:, NL:T], start=(k == 0), stop=(k == n - 1))

                def norm(which):
                    lat, cx = begin(("norm", which))
                    for k in range(KT):
                        e.wait_ge(sq_ready.sem, sq_ready.upto(l, which * KT + k + 1))
                        last = both(lat, cx, onesD, k, KT, S2[:, k % 2, :])
                        last.then_inc(sq_used() if k < KT - 1 else acc_ready(), 1)

                def ada(i):
                    w = chunk(("ada", i))[:, 0:2048].rearrange("p (k c) -> p k c", k=KT)
                    bank = ps[4] if i < 8 else ps[5]
                    for g in range(2):
                        mt = 2 * i + g
                        for k in range(KT):
                            last = mm(bank[:, 2 * mt:2 * mt + 2], w[:, k, 128 * g:128 * g + 128], csil[:, k, :],
                                      start=(k == 0), stop=(k == KT - 1))
                    last.then_inc(ada_done(), 1)

                def gemm(name, w):
                    lat, cx = begin(name)
                    which = 1 if name[0] in ("gate", "up") else 0
                    for k in range(KT):
                        if name in (("rw", 0), ("gate", 0)):
                            e.wait_ge(h_ready.sem, h_ready.upto(l, which * KT + k + 1))
                        last = both(lat, cx, w[k], k, KT, h[:, k, :])
                    last.then_inc(acc_ready(), 1)

                norm(0)
                e.wait_ge(ld_par.sem, ld_par.upto(l, ld_par.per))
                lat, cx = begin(("small", 0))
                tr(lat[:, 0:NPR], prow[:, :], ident[0:NPR, 0:NPR])
                tr(lat[:, 128:256], ckv[:, 0, :], ident).then_inc(acc_ready(), 1)

                for i in range(8):
                    ada(i)

                def cols(name, g):
                    w = chunk(name)[:, 0:2048].rearrange("p (k c) -> p k c", k=KT)
                    return [w[:, k, 128 * g:128 * g + 128] for k in range(KT)]

                def swap(r):
                    lat, cx = begin(("swap", r))
                    e.wait_ge(rot_raw.sem, rot_raw.upto(l, r + 1))
                    mm(lat[:, :], swapm, raw[:, r % 2, 0:NL], start=True, stop=True).then_inc(acc_ready(), 1)

                nada = [8]

                def two_ada():
                    ada(nada[0])
                    ada(nada[0] + 1)
                    nada[0] += 2

                for m in range(9):
                    gemm(("rw", m), cols(("rw", m // 2), m % 2))
                    if m % 2 == 1 or m == 8:
                        two_ada()
                for j in range(4):
                    gemm(("q", j), cols(("q", j // 2), j % 2))
                    if j >= 1:
                        swap(j - 1)
                    if j % 2 == 1:
                        two_ada()
                gemm(("k", 0), cols(("kv", 0), 0))
                swap(3)
                gemm(("v", 0), cols(("kv", 0), 1))
                swap(4)
                two_ada()
                gemm(("fn", 0), cols(("fn", 0), 0))
                lat, cx = begin(("kvT", 0))
                taken(e, l, ("v", 0))
                for t in range(4):
                    tr(lat[:, 128 * t:128 * t + 128], KK[:, 128 * t:128 * t + 128], ident)
                tr(cx[:, 0:128], KK[:, NL:T], ident)
                tr(cx[:, 128:256], kt[:, NL:T], ident).then_inc(acc_ready(), 1)
                gemm(("fn", 1), cols(("fn", 0), 1))

                def prep(t):
                    if t == 0:
                        e.wait_ge(lora_in.sem, lora_in.upto(l, 1))
                    for kind, which, src in (("w", 0, 7), ("a", 1, 8)):
                        for d in range(2):
                            lat, cx = begin((kind, t, d))
                            both(lat, cx, lora[64 * d:64 * d + 64, which, 128 * t:128 * t + 128], 0, 1,
                                 ush[64 * d:64 * d + 64, src, :]).then_inc(acc_ready(), 1)
                    lat, cx = begin(("kk", t))
                    e.wait_ge(kk_sq.sem, kk_sq.upto(l, t + 1))
                    both(lat, cx, ones64, 0, 1, e01[:, 0, :]).then_inc(acc_ready(), 1)
                    lat, cx = begin(("bonus", t))
                    e.wait_ge(rk_prod.sem, rk_prod.upto(l, t + 1))
                    both(lat, cx, ones64, 0, 1, e01[:, 1, :]).then_inc(acc_ready(), 1)

                prep(0)

                taken(e, l, ("fn", 0))
                taken(e, l, ("fn", 1))
                tc_, ts_ = chunk(("dftc", 0)), chunk(("dfts", 0))
                for t in range(5):
                    lat, cx = begin(("ft1", t))
                    for f in range(2):
                        last = mm(lat[:, 256 * f:256 * f + 256], uf[:, f, 128 * t:128 * t + 128], tc_[:, 2176:2432],
                                  start=True, stop=True)
                    last.then_inc(acc_ready(), 1)
                for f in range(2):
                    lat, cx = begin(("ft2", f))
                    if f == 0:
                        taken(e, l, ("ft1", 3))
                        taken(e, l, ("ft1", 4))
                    for t in range(4):
                        mm(lat[:, :], Z[:, t, 256 * f:256 * f + 128], tc_[:, 512 * t:512 * t + 512],
                           start=(t == 0), stop=False)
                        mm(lat[:, :], Z[:, t, 256 * f + 128:256 * f + 256], ts_[:, 512 * t:512 * t + 512],
                           start=False, stop=(t == 3))
                    mm(cx[:, 0:128], Z[:, 4, 256 * f:256 * f + 128], tc_[:, 2048:2176], start=True, stop=False)
                    mm(cx[:, 0:128], Z[:, 4, 256 * f + 128:256 * f + 256], ts_[:, 2048:2176],
                       start=False, stop=True).then_inc(acc_ready(), 1)

                def attention(blocks, done):
                    seq = [(b, i) for b in blocks for i in range(8)]

                    def scores(n):
                        b, i = seq[n]
                        j, g = i % 4, i // 4
                        rowsl = slice(64 * g, 64 * g + 64)
                        q = qt[rowsl, j, 128 * b:128 * b + 128]
                        lat, cx = begin(("s", b, i))
                        at = 0
                        for kind, t in key_tiles(b):
                            src = kcT[rowsl, :] if kind == "cache" else kt[rowsl, 128 * t:128 * t + 128]
                            last = mm(lat[:, at:at + 128], q, src, start=True, stop=True)
                            at += 128
                        last.then_inc(acc_ready(), 1)

                    def transposes(n):
                        b, i = seq[n]
                        m = done + n
                        e.wait_ge(p_exp.sem, p_exp.upto(l, m + 1))
                        e.wait_ge(pt_sb.sem, pt_sb.upto(l, max(m - 1, 0)))
                        for c in range(len(key_tiles(b))):
                            last = tr(ps[4 + m % 2][:, 128 * c:128 * c + 128], Pm[:, m % 3, 128 * c:128 * c + 128],
                                      ident)
                        last.then_inc(pt_ps(), 1)

                    def values(n):
                        b, i = seq[n]
                        m = done + n
                        j, g = i % 4, i // 4
                        nb = m // 8
                        if i == 0:
                            e.wait_ge(o_ready.sem, o_ready.upto(l, max(nb - 1, 0)))
                        e.wait_ge(pt_sb.sem, pt_sb.upto(l, m + 1))
                        tiles = key_tiles(b)
                        for c, (kind, t) in enumerate(tiles):
                            v = (ckv[:, 1, 64 * g:64 * g + 64] if kind == "cache"
                                 else vtok[:, 128 * t + 64 * g:128 * t + 64 * g + 64])
                            last = mm(ps[6 + nb % 2][:, 128 * j + 64 * g:128 * j + 64 * g + 64],
                                      PT[:, m % 2, 128 * c:128 * c + 128], v,
                                      start=(c == 0), stop=(c == len(tiles) - 1))
                        last.then_inc(pv_done(), 1)
                        if i == 7:
                            pending.append(b)

                    def out_transposes():
                        b = pending.pop(0)
                        nb = b
                        lat, cx = begin(("oT", b))
                        e.wait_ge(o_ready.sem, o_ready.upto(l, nb + 1))
                        for j in range(4):
                            last = tr(lat[:, 128 * j:128 * j + 128], otok[:, nb % 2, 128 * j:128 * j + 128], ident)
                        last.then_inc(acc_ready(), 1)

                    pending = []
                    for bi, b in enumerate(blocks):
                        lo = 8 * bi
                        for n in range(lo, lo + 8 + 3):
                            if n < lo + 8:
                                scores(n)
                            if lo <= n - 2 < lo + 8:
                                transposes(n - 2)
                            if lo <= n - 3 < lo + 8:
                                values(n - 3)
                        out_transposes()

                e.wait_ge(rot_done.sem, rot_done.upto(l, 5))
                taken(e, l, ("kvT", 0))
                e.wait_ge(par_ready.sem, par_ready.upto(l, 1))
                attention(ATT_A, 0)

                nchain = [0]

                def recurrence(ht, items_before, heads_before):
                    for q_ in range(2):
                        e.wait_ge(acc_free[q_].sem, acc_free[q_].upto(l, (items_before + 1 - q_) // 2))
                    e.wait_ge(scaled_ready.sem, scaled_ready.upto(l, ht + 1))
                    e.wait_ge(ar_done.sem, ar_done.upto(l, ht + 1))
                    e.wait_ge(ld_state[ht].sem, ld_state[ht].upto(l, 64))
                    for d in range(2):
                        tr(ps[7][:, 128 * d:128 * d + 128], s0in[:, d, :], ident).then_inc(s0_ps(), 1)
                    for g, group in enumerate(GROUPS):
                        base = pair_index(ht, g, 0)
                        A_, R_, K_, B_ = 0, 2, 4, 6
                        for n, (p, d, t) in enumerate(group):
                            if g > 0:
                                e.wait_ge(st_sb.sem, st_sb.upto(l, nchain[0]))
                                e.wait_ge(y_sb.sem, y_sb.upto(l, base))
                            c = slice(128 * t, 128 * t + 128)
                            b0 = ps[2 * p]
                            tr(b0[:, 0:128], h[:, A_ + d, c], ident)
                            tr(b0[:, 128:256], h[:, K_ + d, c], ident)
                            tr(b0[:, 256:384], h[:, B_ + d, c], ident)
                            tr(b0[:, 384:512], ush[:, 4 + ht, c], ident).then_inc(tok_ps(), 1)
                        for hd in range(2):
                            hs = slice(64 * hd, 64 * hd + 64)
                            for n, (p, d, t) in enumerate(group):
                                c = slice(128 * t, 128 * t + 128)
                                bank = ps[2 * p + 1] if hd == 0 else ps[2 * p]
                                if hd == 0 and g == 0 and p == 3:
                                    e.wait_ge(s0_sb.sem, s0_sb.upto(l, 2 * ht + 2))
                                if hd == 1:
                                    e.wait_ge(tok_sb.sem, tok_sb.upto(l, base + n + 1))
                                ar = h[hs, d:d + 3:2, c]
                                mm(bank[:, 0:256], h[hs, K_ + d, c], ar, start=True, stop=True)
                                mm(bank[:, 256:512], h[hs, B_ + d, c], ar, start=True, stop=True).then_inc(
                                    prod_ps(), 1)

                        def flip(level, n, p):
                            b = ps[2 * p + 1]
                            for hd in range(2):
                                last = tr(b[:, 256 + 128 * hd:384 + 128 * hd], Yi[p][:, hd, :], ident)
                            last.then_inc(xt_ps(), 1)

                        gb = 5 * base
                        ng = len(group)
                        for n, (p, d, t) in enumerate(group):
                            e.wait_ge(inv0_sb.sem, inv0_sb.upto(l, base + n + 1))
                            flip(0, n, p)
                        for lv in range(1, 6):
                            at = gb + (lv - 1) * ng
                            for n, (p, d, t) in enumerate(group):
                                e.wait_ge(xt_sb.sem, xt_sb.upto(l, at + n + 1))
                                for hd in range(2):
                                    last = mm(ps[2 * p][:, 128 * hd:128 * hd + 128], LP[p][:, hd, 256:384],
                                              Xi[p][:, hd, :], start=True, stop=True)
                                last.then_inc(p1_ps(), 1)
                            for n, (p, d, t) in enumerate(group):
                                e.wait_ge(p1_sb.sem, p1_sb.upto(l, at + n + 1))
                                for hd in range(2):
                                    last = mm(ps[2 * p + 1][:, 128 * hd:128 * hd + 128], P1[p][:, hd, :],
                                              Yi[p][:, hd, :], start=True, stop=True)
                                last.then_inc(yu_ps(), 1)
                            if lv < 5:
                                for n, (p, d, t) in enumerate(group):
                                    e.wait_ge(yu_sb.sem, yu_sb.upto(l, at + n + 1))
                                    flip(lv, n, p)
                        for n, (p, d, t) in enumerate(group):
                            for hd in range(2):
                                last = mm(ps[2 * p][:, 64 * hd:64 * hd + 64], LP[p][:, hd, 0:128],
                                          TOK[p][:, 2, 64 * hd:64 * hd + 64], start=True, stop=True)
                            last.then_inc(w1_ps(), 1)
                        for n, (p, d, t) in enumerate(group):
                            e.wait_ge(yu_sb.sem, yu_sb.upto(l, gb + 4 * ng + n + 1))
                            e.wait_ge(w1_sb.sem, w1_sb.upto(l, base + n + 1))
                            for hd in range(2):
                                last = mm(ps[2 * p + 1][:, 256 + 128 * hd:384 + 128 * hd], Yi[p][:, hd, :],
                                          W1A[p][:, hd, :], start=True, stop=True)
                            last.then_inc(ug_ps(), 1)
                        for n, (p, d, t) in enumerate(group):
                            e.wait_ge(ug_sb.sem, ug_sb.upto(l, base + n + 1))
                            b0 = ps[2 * p]
                            for hd in range(2):
                                o = slice(64 * hd, 64 * hd + 64)
                                mm(b0[o, 0:128], UG[p][:, hd, 64:128], LP[p][:, hd, 384:512], start=True, stop=True)
                                for hf in range(2):
                                    r = slice(64 * hf, 64 * hf + 64)
                                    bh = ps[2 * p + hf]
                                    mm(bh[o, 128:192], UG[p][r, hd, 64:128], TOK[p][r, 1, o], start=True, stop=True)
                                    mm(bh[o, 256:320], TOK[p][r, 0, o], TOK[p][r, 2, o], start=True, stop=False)
                                    last = mm(bh[o, 256:320], TOK[p][r, 1, o], UG[p][r, hd, 0:64],
                                              start=False, stop=True)
                            last.then_inc(qmn_ps(), 1)
                        for n, (p, d, t) in enumerate(group):
                            b1 = ps[2 * p + 1]
                            e.wait_ge(qmn_sb.sem, qmn_sb.upto(l, base + n + 1))
                            for hd in range(2):
                                o = slice(64 * hd, 64 * hd + 64)
                                mm(b1[o, 0:128], TOK[p][:, 2, o], LP[p][:, hd, 128:256], start=True, stop=False,
                                   skip_group_check=True)
                                mm(b1[o, 0:128], UG[p][:, hd, 0:64], LP[p][:, hd, 384:512], start=False, stop=False,
                                   skip_group_check=True)
                        seen = {}
                        for (p, d, t, hf, ck) in chain_steps(group):
                            n = [q[0] for q in group].index(p)
                            e.wait_ge(qmn_sb.sem, qmn_sb.upto(l, base + n + 1))
                            slot, need = PLAN[(ht, g, d, ck)]
                            if need is None and g == 2:
                                e.wait_ge(ctx_zero.sem, ctx_zero.upto(l, ht + 1))
                            elif need is None:
                                e.wait_ge(s0_sb.sem, s0_sb.upto(l, 2 * ht + d + 1))
                            else:
                                e.wait_ge(st_sb.sem, st_sb.upto(l, need))
                            S = St[:, d, slot, :]
                            last = mm(ps[2 * p + 1][:, 64 * hf:64 * hf + 64], S, Qt[p][:, 64 * hf:64 * hf + 64],
                                      start=False, stop=True, skip_group_check=True)
                            seen[p] = seen.get(p, 0) + 1
                            if seen[p] == 2:
                                last.then_inc(y_ps(), 1)
                            if needs_state(ck, d):
                                mm(ps[2 * p][:, 384:512], MN[:, p, 0, hf, :], S, start=True, stop=True).then_inc(
                                    st_ps(), 1)
                                nchain[0] += 1
                    e.wait_ge(st_sb.sem, st_sb.upto(l, nchain[0]))
                    e.wait_ge(y_sb.sem, y_sb.upto(l, pair_index(ht, 2, 2)))
                    for d in range(2):
                        last = tr(ps[6][:, 128 * d:128 * d + 128], St[:, d, 0, :], ident)
                    last.then_inc(fin_ps(), 1)
                    e.wait_ge(fin_sb.sem, fin_sb.upto(l, ht + 1))

                recurrence(0, ITEM_AT[("w", 1, 0)], 16)
                prep(1)
                attention(ATT_B, 16)
                recurrence(1, ITEM_AT[("mean", 0)], 40)

                for t in range(2):
                    lat, cx = begin(("mean", t))
                    both(lat, cx, mean64, 0, 1, ush[:, 2 + t, :]).then_inc(acc_ready(), 1)
                for t in range(2):
                    lat, cx = begin(("var", t))
                    e.wait_ge(ysq_ready.sem, ysq_ready.upto(l, t + 1))
                    both(lat, cx, mean64, 0, 1, e01[:, t, :]).then_inc(acc_ready(), 1)
                for t in range(2):
                    lat, cx = begin(("g", t))
                    both(lat, cx, lora[:, 2, 128 * t:128 * t + 128], 0, 1, ush[:, 6, :]).then_inc(acc_ready(), 1)

                taken(e, l, ("ft2", 0))
                taken(e, l, ("ft2", 1))
                for b in (3, 4):
                    taken(e, l, ("oT", b))
                src_of = {0: qt[:, 0, :], 1: qt[:, 1, :], 2: qt[:, 2, :], 3: qt[:, 3, :],
                          4: ush[:, 2, :], 5: ush[:, 3, :], 6: uf[:, 0, :], 7: uf[:, 1, :]}
                for m in range(KT):
                    w = cols(("wo", m // 2), m % 2)
                    lat, cx = begin(("out", m))
                    for n, k in enumerate((0, 1, 2, 3, 6, 7, 4, 5)):
                        if m == 0 and k in (4, 5):
                            taken(e, l, ("g", k - 4))
                        last = both(lat, cx, w[k], n, KT, src_of[k])
                    last.then_inc(acc_ready(), 1)
                norm(1)
                for i in range(FT):
                    w = cols(("f1", i), 0)
                    gemm(("gate", i), w)
                    gemm(("up", i), cols(("f1", i), 1))
                for m in range(KT):
                    w = chunk(("f2", m)).rearrange("p (k c) -> p k c", k=FT)
                    lat, cx = begin(("f2", m))
                    for k in range(FT):
                        if m == 0:
                            taken(e, l, ("up", k))
                        last = both(lat, cx, w[:, k, :], k, FT, hid[:, k, :])
                    last.then_inc(acc_ready(), 1)

            lat, cx = ps[0], ps[2]
            layer_before(e, DEPTH)
            for k in range(KT):
                e.wait_ge(sq_ready.sem, sq_ready.upto(DEPTH, k + 1))
                mm(lat[:, :], onesD, S2[:, k % 2, 0:NL], start=(k == 0), stop=(k == KT - 1))
                mm(cx[:, 0:NC_], onesD, S2[:, k % 2, NL:T], start=(k == 0), stop=(k == KT - 1)).then_inc(
                    sq_used.sem if k < KT - 1 else acc_ready.sem, 1)
            e.wait_ge(h_scaled.sem, h_scaled.upto(DEPTH, KT))
            for t in range(5):
                for g in range(2):
                    n = 2 * t + g
                    if n >= 4:
                        e.wait_ge(yT_sb, n // 2 - 1)
                    for k in range(4):
                        last = tr(ps[4 + n % 4][:, 128 * k:128 * k + 128],
                                  h[:, 4 * g + k, 128 * t:128 * t + 128], ident)
                last.then_inc(yT_ps, 1)

        @block.scalar
        def _(e):
            
            act = nc.scalar.activation
            e.wait_ge(mn_zero, 5)
            for n in range(10):
                t, g = n // 2, n % 2
                e.wait_ge(xT_ps, n + 1)
                c = slice(128 * t, 128 * t + 128)
                act(x[:, 4 * g:4 * g + 4, c], ps[4 + n % 2][:, :].rearrange("p (k t) -> p k t", k=4),
                    ACT.Copy).then_inc(xT_sb, 1)
            e.wait_ge(xT_ps, 11)
            act(cvec[:, :], ps[6][:, 0:24], ACT.Copy).then_inc(c_ready, 1)
            e.wait_ge(c_ready, 1)
            act(csil_s[:, :], cvec[:, 0:16], ACT.Sigmoid).then_inc(c_ready, 1)

            def norm_square(l, which):
                for k in range(KT):
                    if which == 1:
                        taken(e, l, ("out", k))
                    if k >= 2:
                        e.wait_ge(sq_used.sem, sq_used.upto(l, which * (KT - 1) + k - 1))
                    act(S2[:, k % 2, :], x[:, k, :], ACT.Square).then_inc(sq_ready(), 1)

            def norm_root(l, which):
                i, lat, cx = acc_item(("norm", which))
                e.wait_ge(acc_ready.sem, acc_ready.upto(l, i + 1))
                act(rot[:, 0:NL], lat[:, :], ACT.Sqrt, bias=eps[:, 0:1])
                act(rot[:, NL:T], cx[:, 0:NC_], ACT.Sqrt, bias=eps[:, 0:1]).then_inc(acc_free[i % 2](), 1)

            def norm_shift(l, which):
                for k in range(KT):
                    e.wait_ge(h_scaled.sem, h_scaled.upto(l, which * KT + k + 1))
                    for s, (a, b) in enumerate(STREAMS):
                        last = act(h[:, k, a:b], h[:, k, a:b], ACT.Identity,
                                   bias=mod[:, 24 * which + k, s:s + 1])
                    last.then_inc(h_ready(), 1)

            e.wait_ge(xT_sb, 10)
            with e.Fori(0, DEPTH) as l:

                def ready(name):
                    i, lat, cx = acc_item(name)
                    e.wait_ge(acc_ready.sem, acc_ready.upto(l, i + 1))
                    return acc_free[i % 2], lat, cx

                layer_before(e, l)
                norm_square(l, 0)
                norm_root(l, 0)
                free, lat, cx = ready(("small", 0))
                act(par[:, :], lat[:, 0:NPR], ACT.Copy)
                act(kcT[:, :], lat[:, 128:256], ACT.Copy).then_inc(free(), 1)
                taken(e, l, ("small", 0))
                act(omka[:, :], par[:, PR_KA:PR_KA + 2], ACT.Copy, scale=-1.0, bias=1.0).then_inc(par_ready(), 1)
                norm_shift(l, 0)
                e.wait_ge(pads_zero.sem, pads_zero.upto(l, 1))
                for m in range(9):
                    free, lat, cx = ready(("rw", m))
                    if m >= 2:
                        e.wait_ge(conv_out.sem, conv_out.upto(l, m - 1))
                    act(raw[:, m % 2, 1:513], lat[:, :], ACT.Copy)
                    act(raw[:, m % 2, 514:642], cx[:, 0:NC_], ACT.Copy)
                    w1 = par[:, PR_SHIFT + 9 + m:PR_SHIFT + 10 + m]
                    act(ush[:, m, 0:NL], lat[:, :], ACT.Copy, scale=w1)
                    act(ush[:, m, NL:T], cx[:, 0:NC_], ACT.Copy, scale=w1).then_inc(free(), 1)
                for r, name in enumerate((("q", 0), ("q", 1), ("q", 2), ("q", 3), ("k", 0))):
                    free, lat, cx = ready(name)
                    sc = 0.125 if r < 4 else 1.0
                    dst = qt[:, r, NL:T] if r < 4 else kt[:, NL:T]
                    if r < 2:
                        e.wait_ge(conv_out.sem, conv_out.upto(l, 9))
                    else:
                        e.wait_ge(rot_cos.sem, rot_cos.upto(l, r - 1))
                        e.wait_ge(acc_ready.sem, acc_ready.upto(l, ITEM_AT[("swap", r - 2)] + 1))
                    act(raw[:, r % 2, 0:NL], lat[:, :], ACT.Copy, scale=sc).then_inc(rot_raw(), 1)
                    act(dst, cx[:, 0:NC_], ACT.Copy, scale=sc).then_inc(free(), 1)
                free, lat, cx = ready(("v", 0))
                act(KK[:, 0:NL], lat[:, :], ACT.Copy)
                act(KK[:, NL:T], cx[:, 0:NC_], ACT.Copy).then_inc(free(), 1)

                def fcopy(f):
                    free, lat, cx = ready(("fn", f))
                    act(uf[:, f, 0:NL], lat[:, :], ACT.Copy)
                    act(uf[:, f, NL:T], cx[:, 0:NC_], ACT.Copy).then_inc(free(), 1)

                fcopy(0)
                free, lat, cx = ready(("kvT", 0))
                act(vtok[:, 0:NL], lat[:, :], ACT.Copy)
                act(vtok[:, NL:T], cx[:, 0:128], ACT.Copy)
                act(kvout[:, :], cx[:, 128:256], ACT.Copy).then_inc(free(), 1)
                e.wait_ge(conv_out.sem, conv_out.upto(l, 9))
                act(ush[:, 6, :], ush[:, 6, :], ACT.Sigmoid)
                act(ush[:, 7, :], ush[:, 7, :], ACT.Tanh).then_inc(lora_in(), 1)
                fcopy(1)

                def prep(t):
                    for kind, slot0 in (("w", None), ("a", 6)):
                        for d in range(2):
                            free, lat, cx = ready((kind, t, d))
                            bias = par[:, (PR_W0 if kind == "w" else PR_A0) + 2 * d + t:
                                       (PR_W0 if kind == "w" else PR_A0) + 2 * d + t + 1]
                            dst = S2[:, d, :] if kind == "w" else h[:, 6 + d, :]
                            act(dst[:, 0:NL], lat[:, :], ACT.Sigmoid, bias=bias)
                            act(dst[:, NL:T], cx[:, 0:NC_], ACT.Sigmoid, bias=bias).then_inc(free(), 1)
                    e.wait_ge(kk_raw.sem, kk_raw.upto(l, t + 1))
                    act(e01[:, 0, :], KK, ACT.Square).then_inc(kk_sq(), 1)
                    free, lat, cx = ready(("kk", t))
                    act(e01[:, 0, 0:NL], lat[:, :], ACT.Sqrt, bias=eps[:, 1:2])
                    act(e01[:, 0, NL:T], cx[:, 0:NC_], ACT.Sqrt, bias=eps[:, 1:2]).then_inc(free(), 1)
                    free, lat, cx = ready(("bonus", t))
                    act(e01[:, 1, 0:NL], lat[:, :], ACT.Copy)
                    act(e01[:, 1, NL:T], cx[:, 0:NC_], ACT.Copy).then_inc(free(), 1)
                    e.wait_ge(cum_ready.sem, cum_ready.upto(l, t + 1))
                    act(h[:, 2:4, :], CC, ACT.Exp, scale=-DECAY)
                    act(h[:, 4:6, :], CC, ACT.Exp, scale=DECAY)
                    act(h[:, 0:2, :], S2, ACT.Exp, scale=-DECAY)
                    act(emid[:, :, :], mid[:, :, :], ACT.Exp, scale=-DECAY)
                    act(eend[:, :, :], end[:, :, :], ACT.Exp, scale=-DECAY).then_inc(exps_ready(), 1)

                prep(0)
                for t in range(5):
                    free, lat, cx = ready(("ft1", t))
                    act(Z[:, t, :], lat[:, :], ACT.Copy).then_inc(free(), 1)
                for f in range(2):
                    free, lat, cx = ready(("ft2", f))
                    act(uf[:, f, 0:NL], lat[:, :], ACT.Copy)
                    act(uf[:, f, NL:T], cx[:, 0:128], ACT.Copy).then_inc(free(), 1)

                def attention(blocks, done):
                    seq = [(b, i) for b in blocks for i in range(8)]

                    def pexp(n):
                        b, i = seq[n]
                        m = done + n
                        w = 128 * len(key_tiles(b))
                        e.wait_ge(p_ready.sem, p_ready.upto(l, m + 1))
                        act(Pm[:, m % 3, 0:w], Pm[:, m % 3, 0:w], ACT.Exp, bias=negm[:, (m // 8) % 2, i:i + 1],
                            accum_out=den[:, (m // 8) % 2, i:i + 1]).then_inc(p_exp(), 1)

                    def ptcopy(n):
                        b, i = seq[n]
                        m = done + n
                        w = 128 * len(key_tiles(b))
                        e.wait_ge(pt_ps.sem, pt_ps.upto(l, m + 1))
                        e.wait_ge(pv_done.sem, pv_done.upto(l, max(m - 1, 0)))
                        act(PT[:, m % 2, 0:w], ps[4 + m % 2][:, 0:w], ACT.Copy).then_inc(pt_sb(), 1)

                    for bi, b in enumerate(blocks):
                        lo = 8 * bi
                        for n in range(lo, lo + 10):
                            if n < lo + 8:
                                pexp(n)
                            if n - 2 >= lo:
                                ptcopy(n - 2)
                        e.wait_ge(esk_in.sem, esk_in.upto(l, b + 1))
                        act(esk[:, b % 2, :], esk[:, b % 2, :], ACT.Exp).then_inc(esk_ready(), 1)
                        free, lat, cx = ready(("oT", b))
                        act(qt[:, :, 128 * b:128 * b + 128], lat[:, :].rearrange("p (j t) -> p j t", j=4),
                            ACT.Copy).then_inc(free(), 1)

                attention(ATT_A, 0)

                def recurrence(ht):
                    for d in range(2):
                        e.wait_ge(s0_ps.sem, s0_ps.upto(l, 2 * ht + 2))
                        ck = 0 if d == 0 else LCH - 1
                        act(St[:, d, 0, :], ps[7][:, 128 * d:128 * d + 128], ACT.Copy,
                            scale=emid[:, d, ck:ck + 1]).then_inc(s0_sb(), 1)
                    for g, group in enumerate(GROUPS):
                        base = pair_index(ht, g, 0)
                        gb = 5 * base
                        ng = len(group)
                        for n, (p, d, t) in enumerate(group):
                            e.wait_ge(tok_ps.sem, tok_ps.upto(l, base + n + 1))
                            act(W1A[p][:, :, 64:128], ps[2 * p][:, 0:128].rearrange("p (a t) -> p a t", a=2), ACT.Copy)
                            act(TOK[p], ps[2 * p][:, 128:512].rearrange("p (a t) -> p a t", a=3),
                                ACT.Copy).then_inc(tok_sb(), 1)
                        for lv in range(5):
                            for n, (p, d, t) in enumerate(group):
                                e.wait_ge(xt_ps.sem, xt_ps.upto(l, gb + lv * ng + n + 1))
                                act(Xi[p], ps[2 * p + 1][:, 256:512].rearrange("p (a t) -> p a t", a=2),
                                    ACT.Copy).then_inc(xt_sb(), 1)
                        for n, (p, d, t) in enumerate(group):
                            e.wait_ge(w1_ps.sem, w1_ps.upto(l, base + n + 1))
                            act(W1A[p][:, :, 0:64], ps[2 * p][:, 0:128].rearrange("p (a t) -> p a t", a=2),
                                ACT.Copy).then_inc(w1_sb(), 1)
                        for n, (p, d, t) in enumerate(group):
                            e.wait_ge(ug_ps.sem, ug_ps.upto(l, base + n + 1))
                            act(UG[p], ps[2 * p + 1][:, 256:512].rearrange("p (a t) -> p a t", a=2),
                                ACT.Copy).then_inc(ug_sb(), 1)
                    e.wait_ge(fin_ps.sem, fin_ps.upto(l, ht + 1))
                    if ht == 1:
                        e.wait_ge(fin_st.sem, fin_st.upto(l, 64))
                    act(stout, ps[6][:, 0:256].rearrange("p (a t) -> p a t", a=2), ACT.Copy).then_inc(fin_sb(), 1)

                recurrence(0)
                prep(1)
                attention(ATT_B, 16)
                recurrence(1)

                for t in range(2):
                    taken(e, l, ("mean", t))
                    act(e01[:, t, :], ush[:, 2 + t, :], ACT.Square).then_inc(ysq_ready(), 1)
                for t in range(2):
                    free, lat, cx = ready(("var", t))
                    act(e01[:, t, 0:NL], lat[:, :], ACT.Sqrt, bias=eps[:, 2:3])
                    act(e01[:, t, NL:T], cx[:, 0:NC_], ACT.Sqrt, bias=eps[:, 2:3]).then_inc(free(), 1)
                norm_square(l, 1)
                e.wait_ge(fin_st.sem, fin_st.upto(l, 128))
                norm_root(l, 1)
                norm_shift(l, 1)
                e.wait_ge(kv_stored.sem, kv_stored.upto(l, 32))
                for i in range(FT):
                    i_, lat, cx = acc_item(("gate", i))
                    e.wait_ge(acc_ready.sem, acc_ready.upto(l, i_ + 1))
                    act(hid[:, i, 0:NL], lat[:, :], ACT.Sigmoid)
                    act(hid[:, i, NL:T], cx[:, 0:NC_], ACT.Sigmoid).then_inc(hid_sig(), 1)

            layer_before(e, DEPTH)
            for k in range(KT):
                if k >= 2:
                    e.wait_ge(sq_used.sem, sq_used.upto(DEPTH, k - 1))
                act(S2[:, k % 2, :], x[:, k, :], ACT.Square).then_inc(sq_ready.sem, 1)
            e.wait_ge(acc_ready.sem, acc_ready.upto(DEPTH, 1))
            act(rot[:, 0:NL], ps[0][:, :], ACT.Sqrt, bias=eps[:, 0:1])
            act(rot[:, NL:T], ps[2][:, 0:NC_], ACT.Sqrt, bias=eps[:, 0:1]).then_inc(acc_free[0].sem, 1)
            for t in range(5):
                e.wait_ge(yT_ps, t + 1)
                if t >= 2:
                    e.wait_ge(y_stored[t % 2], 16 * (t // 2))
                for g in range(2):
                    n = 2 * t + g
                    last = act(yout[:, t % 2, 512 * g:512 * g + 512], ps[4 + n % 4][:, :], ACT.Copy)
                last.then_inc(yT_sb, 1)

        @block.vector
        def _(e):
            own = Own(e, dve_own, DVE_CHAIN)
            V = nc.vector
            for s in signals.values():
                if s.primed:
                    e.sem_inc(s.sem)
            e.wait_ge(c_ready, 2)
            V.tensor_tensor(csil[:, :, :].rearrange("p k s -> p s k"), cvec[:, 0:16].rearrange("p (s k) -> p s k", s=2),
                            csil_s.rearrange("p (s k) -> p s k", s=2), MUL).then_inc(c_ready, 1)

            def gains(l, which):
                g = par[:, (PR_NMIX, PR_NFFN)[which]:(PR_NMIX, PR_NFFN)[which] + 8].unsqueeze(2).to_broadcast([128, 8, 2])
                V.scalar_tensor_tensor(gain[:, which, :, :], mod[:, 24 * which + 8:24 * which + 16, :], 1.0, g,
                                       ADD, MUL).then_inc(gain_ready(), 1)
                e.wait_ge(gain_ready.sem, gain_ready.upto(l, which + 1))

            def norm_scale(l, which, n, per_stream):
                taken(e, l, ("norm", which))
                own.after(V.reciprocal(rot, rot))
                for k in range(KT):
                    for s, (a, b) in enumerate(STREAMS):
                        last = V.scalar_tensor_tensor(h[:, k, a:b], x[:, k, a:b], gain[:, n, k, s:s + 1], rot[:, a:b],
                                                      MUL, MUL)
                    last.then_inc(h_scaled() if per_stream else h_scaled.sem, 1)

            e.wait_ge(xT_sb, 10)
            with e.Fori(0, DEPTH) as l:
                own.l, own.n = l, 0

                def ready(name):
                    i, lat, cx = acc_item(name)
                    e.wait_ge(acc_ready.sem, acc_ready.upto(l, i + 1))
                    return acc_free[i % 2], lat, cx

                e.wait_ge(par_ready.sem, par_ready.upto(l, 1))
                e.wait_ge(ada_done.sem, ada_done.upto(l, 8))
                own.after(V.tensor_tensor(mod[:, 0:16, :], ps[4][:, 0:32].rearrange("p (m s) -> p m s", s=2),
                                          par[:, PR_ADA:PR_ADA + 16].unsqueeze(2).to_broadcast([128, 16, 2]), ADD))
                gains(l, 0)
                norm_scale(l, 0, 0, True)
                for m in range(9):
                    taken(e, l, ("rw", m))
                    wl = par[:, PR_SHIFT + m:PR_SHIFT + m + 1]
                    wr = par[:, PR_SHIFT + 18 + m:PR_SHIFT + 19 + m]
                    r_ = raw[:, m % 2, :]
                    V.scalar_tensor_tensor(ush[:, m, 0:NL], r_[:, 0:512], wl, ush[:, m, 0:NL], MUL, ADD)
                    own.after(V.scalar_tensor_tensor(ush[:, m, NL:T], r_[:, 513:641], wl, ush[:, m, NL:T], MUL, ADD))
                    V.scalar_tensor_tensor(ush[:, m, 0:NL], r_[:, 2:514], wr, ush[:, m, 0:NL], MUL, ADD)
                    V.scalar_tensor_tensor(ush[:, m, NL:T], r_[:, 515:643], wr, ush[:, m, NL:T], MUL,
                                           ADD).then_inc(conv_out(), 1)
                e.wait_ge(ld_rope.sem, ld_rope.upto(l, 16))
                for r in range(5):
                    free, lat, cx = ready(("swap", r))
                    dst = qt[:, r, 0:NL] if r < 4 else kt[:, 0:NL]
                    e.wait_ge(rot_done.sem, rot_done.upto(l, r))
                    V.tensor_tensor(rot[:, 0:NL], lat[:, :], rope[:, 1, :], MUL).then_inc(free(), 1)
                    taken(e, l, ("swap", r))
                    e.wait_ge(rot_cos.sem, rot_cos.upto(l, r + 1))
                    V.tensor_tensor(dst, dst, rot[:, 0:NL], ADD).then_inc(rot_done(), 1)
                e.wait_ge(ada_done.sem, ada_done.upto(l, 24))
                own.after(V.tensor_tensor(mod[:, 16:48, :], ps[5][:, 32:96].rearrange("p (m s) -> p m s", s=2),
                                          par[:, PR_ADA + 16:PR_ADA + 48].unsqueeze(2).to_broadcast([128, 32, 2]), ADD))
                gains(l, 1)

                def chunks(v):
                    return v.rearrange("p a (c t) -> p (a c) t", t=CH)

                def prep(t):
                    kb = KK.unsqueeze(1).to_broadcast([128, 2, T])
                    taken(e, l, ("w", t, 0))
                    taken(e, l, ("w", t, 1))
                    V.tensor_tensor_scan(CC[:, 0, :], reset[:, :], S2[:, 0, :], 0.0, MUL, ADD)
                    own.after(V.tensor_tensor_scan(CC[:, 1, :], reset[:, :], S2[:, 1, :], 0.0, MUL, ADD))
                    c0 = CC[:, 0, :].rearrange("p (c t) -> p c t", t=CH)
                    c1 = CC[:, 1, :].rearrange("p (c t) -> p c t", t=CH)
                    V.tensor_copy(end[:, 0, :].unsqueeze(2), c0[:, :, 63:64])
                    V.tensor_copy(mid[:, 0, :].unsqueeze(2), c0[:, :, 31:32])
                    own.after(V.tensor_copy(end[:, 1, :].unsqueeze(2), c1[:, :, 63:64]))
                    own.after(V.tensor_tensor(CC[:, 1, :], S2[:, 1, :], CC[:, 1, :], SUB))
                    own.after(V.tensor_tensor(c1, c1, end[:, 1, :].unsqueeze(2).to_broadcast([128, NCH, CH]), ADD))
                    own.after(V.tensor_copy(mid[:, 1, :].unsqueeze(2), c1[:, :, 32:33]))
                    own.after(V.tensor_tensor(chunks(CC), chunks(CC),
                                              mid[:, :, :].rearrange("p a c -> p (a c)").unsqueeze(2).to_broadcast(
                                                  [128, 2 * NCH, CH]), SUB))
                    own.after(V.tensor_tensor(end[:, :, :], end[:, :, :], mid[:, :, :], SUB))
                    V.tensor_tensor(S2, CC, S2, SUB).then_inc(cum_ready(), 1)
                    taken(e, l, ("kk", t))
                    own.after(V.reciprocal(e01[:, 0, :], e01[:, 0, :]))
                    V.tensor_tensor(KK, KK, e01[:, 0, :], MUL).then_inc(kk_ready(), 1)
                    e.wait_ge(kk_ready.sem, kk_ready.upto(l, t + 1))
                    e.wait_ge(exps_ready.sem, exps_ready.upto(l, t + 1))
                    n = NCH
                    V.tensor_tensor(dec[:, 0, 0:n - 1], eend[:, 0, 0:n - 1], emid[:, 0, 1:n], MUL)
                    V.tensor_copy(dec[:, 0, n - 1:n], eend[:, 0, n - 1:n])
                    V.tensor_copy(dec[:, 1, 0:1], eend[:, 1, 0:1])
                    own.after(V.tensor_tensor(dec[:, 1, 1:n], eend[:, 1, 1:n], emid[:, 1, 0:n - 1], MUL))
                    V.tensor_copy(dec[:, 1, LCH:LCH + 1], eend[:, 1, LCH:LCH + 1])
                    own.after(V.tensor_scalar(CC, h[:, 6:8, :], par[:, PR_KA + t:PR_KA + t + 1], omka[:, t:t + 1],
                                              MUL, ADD))
                    own.after(V.tensor_tensor(CC, CC, ush[:, 2 + t:3 + t, :].to_broadcast([128, 2, T]), MUL))
                    own.after(V.tensor_tensor(h[:, 6:8, :], h[:, 6:8, :], h[:, 4:6, :], MUL))
                    V.tensor_tensor(h[:, 4:6, :], h[:, 4:6, :], CC, MUL)
                    own.after(V.scalar_tensor_tensor(h[:, 6:8, :], h[:, 6:8, :], -1.0, kb, MUL, MUL))
                    e.wait_ge(ar_done.sem, ar_done.upto(l, t + 1))
                    taken(e, l, ("bonus", t))
                    V.tensor_tensor(ush[:, t, :], e01[:, 1, :], ush[:, 4 + t, :], MUL).then_inc(scaled_ready(), 1)
                    e.wait_ge(scaled_ready.sem, scaled_ready.upto(l, t + 1))

                prep(0)

                def attention(blocks, done):
                    seq = [(b, i) for b in blocks for i in range(8)]

                    def softmax_in(n):
                        b, i = seq[n]
                        m = done + n
                        w = 128 * len(key_tiles(b))
                        c0, c1 = mask_cols(b)
                        free, lat, cx = ready(("s", b, i))
                        e.wait_ge(pt_ps.sem, pt_ps.upto(l, max(m - 2, 0)))
                        V.tensor_tensor(Pm[:, m % 3, 0:w], lat[:, 0:w], attmask[:, c0:c1], ADD).then_inc(free(), 1)
                        taken(e, l, ("s", b, i))
                        mx = negm[:, b % 2, i:i + 1]
                        own.after(V.tensor_reduce(mx, Pm[:, m % 3, 0:w], AX.X, MAX))
                        V.tensor_scalar(mx, mx, sink[:, i:i + 1], -1.0, MAX, MUL).then_inc(p_ready(), 1)

                    for bi, b in enumerate(blocks):
                        lo = 8 * bi
                        for n in range(lo, lo + 8):
                            softmax_in(n)
                        e.wait_ge(p_ready.sem, p_ready.upto(l, done + lo + 8))
                        V.tensor_tensor(esk[:, b % 2, :], negm[:, b % 2, :], sink[:, :], ADD).then_inc(esk_in(), 1)
                        e.wait_ge(esk_ready.sem, esk_ready.upto(l, b + 1))
                        own.after(V.tensor_tensor(den[:, b % 2, :], den[:, b % 2, :], esk[:, b % 2, :], ADD))
                        own.after(V.reciprocal(den[:, b % 2, :], den[:, b % 2, :]))
                        e.wait_ge(pv_done.sem, pv_done.upto(l, done + lo + 8))
                        o_ps = ps[6 + b % 2][:, :].rearrange("p (j g c) -> p g j c", j=4, g=2)
                        o_sb = otok[:, b % 2, :].rearrange("p (j g c) -> p g j c", j=4, g=2)
                        for g in range(2):
                            last = V.tensor_tensor(o_sb[:, g, :, :], o_ps[:, g, :, :],
                                                   den[:, b % 2, 4 * g:4 * g + 4].unsqueeze(2).to_broadcast([128, 4, 64]),
                                                   MUL)
                        last.then_inc(o_ready(), 1)

                attention(ATT_A, 0)

                nchain = [0]

                def recurrence(ht):
                    for g, group in enumerate(GROUPS):
                        base = pair_index(ht, g, 0)
                        gb = 5 * base
                        ng = len(group)
                        for hd in range(2):
                            for n, (p, d, t) in enumerate(group):
                                bank = ps[2 * p + 1] if hd == 0 else ps[2 * p]
                                e.wait_ge(prod_ps.sem, prod_ps.upto(l, 2 * base + hd * ng + n + 1))
                                V.tensor_tensor(LP[p][:, hd, :].rearrange("p (a t) -> p a t", a=2),
                                                bank[:, :].rearrange("p (a t) -> p a t", a=2),
                                                masks[:, d:d + 1, :].to_broadcast([128, 2, 256]), MUL).then_inc(
                                                    prod_sb(), 1)
                        eye = mats[:, 0:1, :].to_broadcast([128, 2, 128])
                        for n, (p, d, t) in enumerate(group):
                            e.wait_ge(prod_sb.sem, prod_sb.upto(l, 2 * base + ng + n + 1))
                            own.after(V.tensor_tensor(Yi[p], LP[p][:, :, 256:384],
                                                      lvl[:, 1 - d, 0:1, :].to_broadcast([128, 2, 128]), MUL))
                            V.tensor_tensor(Yi[p], Yi[p], eye, ADD).then_inc(inv0_sb(), 1)
                        for lv in range(1, 6):
                            at = gb + (lv - 1) * ng
                            for n, (p, d, t) in enumerate(group):
                                e.wait_ge(p1_ps.sem, p1_ps.upto(l, at + n + 1))
                                V.tensor_tensor(P1[p], ps[2 * p][:, 0:256].rearrange("p (a t) -> p a t", a=2),
                                                lvl[:, d, lv:lv + 1, :].to_broadcast([128, 2, 128]), MUL).then_inc(
                                                    p1_sb(), 1)
                            for n, (p, d, t) in enumerate(group):
                                e.wait_ge(yu_ps.sem, yu_ps.upto(l, at + n + 1))
                                if lv == 1:
                                    e.wait_ge(inv0_sb.sem, inv0_sb.upto(l, base + n + 1))
                                else:
                                    e.wait_ge(yu_sb.sem, yu_sb.upto(l, at - ng + n + 1))
                                V.tensor_tensor(Yi[p], Yi[p], ps[2 * p + 1][:, 0:256].rearrange(
                                    "p (a t) -> p a t", a=2), ADD).then_inc(yu_sb(), 1)
                        for n, (p, d, t) in enumerate(group):
                            e.wait_ge(qmn_ps.sem, qmn_ps.upto(l, base + n + 1))
                            b0 = ps[2 * p]
                            c = slice(128 * t, 128 * t + 128)
                            if g == 0 and ht == 0 and n == 0:
                                e.wait_ge(mn_zero, 5)
                            V.tensor_tensor(Qt[p], b0[:, 0:128], h[:, 2 + d, c], ADD)
                            for hd in range(2):
                                o = slice(64 * hd, 64 * hd + 64)
                                V.tensor_tensor(MN[o, p, 0, :, o], PS[o, 2 * p:2 * p + 2, 128:192],
                                                mats[o, 0:1, o].to_broadcast([64, 2, 64]), ADD)
                                last = V.tensor_tensor(MN[o, p, 1, :, o],
                                                       PS[o, 2 * p:2 * p + 2, 256:320],
                                                       dec[o, d, 2 * t:2 * t + 2].unsqueeze(2).to_broadcast([64, 2, 64]),
                                                       MUL)
                            last.then_inc(qmn_sb(), 1)
                        for (p, d, t, hf, ck) in chain_steps(group):
                            if needs_state(ck, d):
                                slot, need = PLAN[(ht, g, d, ck)]
                                e.wait_ge(st_ps.sem, st_ps.upto(l, nchain[0] + 1))
                                e.wait_ge(qmn_sb.sem, qmn_sb.upto(l, base + len(group)))
                                V.scalar_tensor_tensor(St[:, d, 1 - slot, :], ps[2 * p][:, 384:512],
                                                       dec[:, d, ck:ck + 1], MN[:, p, 1, hf, :], MUL,
                                                       ADD).then_inc(st_sb(), 1)
                                nchain[0] += 1
                        for n, (p, d, t) in enumerate(y_order(group)):
                            e.wait_ge(y_ps.sem, y_ps.upto(l, base + n + 1))
                            c = slice(128 * t, 128 * t + 128)
                            yc = ush[:, 2 + ht, c]
                            if first_touch(g, d, t):
                                V.tensor_copy(yc, ps[2 * p + 1][:, 0:128]).then_inc(y_sb(), 1)
                            else:
                                e.wait_ge(y_sb.sem, y_sb.upto(l, base + n))
                                V.tensor_tensor(yc, yc, ps[2 * p + 1][:, 0:128], ADD).then_inc(y_sb(), 1)
                        if g == 1:
                            e.wait_ge(y_ps.sem, y_ps.upto(l, base + len(group)))
                            V.memset(St[:, :, 0, :], 0.0).then_inc(ctx_zero(), 1)

                recurrence(0)
                prep(1)
                attention(ATT_B, 16)
                recurrence(1)

                e.wait_ge(y_sb.sem, y_sb.upto(l, y_sb.per))
                for t in range(2):
                    free, lat, cx = ready(("mean", t))
                    y = ush[:, 2 + t, :]
                    V.tensor_tensor(y[:, 0:NL], y[:, 0:NL], lat[:, :], SUB)
                    V.tensor_tensor(y[:, NL:T], y[:, NL:T], cx[:, 0:NC_], SUB).then_inc(free(), 1)
                for t in range(2):
                    y = ush[:, 2 + t, :]
                    taken(e, l, ("var", t))
                    own.after(V.reciprocal(e01[:, t, :], e01[:, t, :]))
                    own.after(V.tensor_tensor(y, y, e01[:, t, :], MUL))
                    own.after(V.tensor_scalar(y, y, par[:, PR_LNG + t:PR_LNG + t + 1], par[:, PR_LNB + t:PR_LNB + t + 1],
                                              MUL, ADD))
                    own.after(V.tensor_tensor(y, y, ush[:, t, :], ADD))
                    free, lat, cx = ready(("g", t))
                    V.tensor_tensor(y[:, 0:NL], y[:, 0:NL], lat[:, :], MUL)
                    V.tensor_tensor(y[:, NL:T], y[:, NL:T], cx[:, 0:NC_], MUL).then_inc(free(), 1)

                def residual(name, m, gate_at):
                    free, lat, cx = ready((name, m))
                    V.scalar_tensor_tensor(x[:, m, 0:NL], lat[:, :], mod[:, gate_at + m, 0:1], x[:, m, 0:NL], MUL, ADD)
                    V.scalar_tensor_tensor(x[:, m, NL:T], cx[:, 0:NC_], mod[:, gate_at + m, 1:2], x[:, m, NL:T], MUL,
                                           ADD).then_inc(free(), 1)

                for m in range(KT):
                    residual("out", m, 16)
                norm_scale(l, 1, 1, True)
                for i in range(FT):
                    gfree, glat, gcx = ready(("gate", i))
                    e.wait_ge(hid_sig.sem, hid_sig.upto(l, i + 1))
                    V.tensor_tensor(hid[:, i, 0:NL], hid[:, i, 0:NL], glat[:, :], MUL)
                    V.tensor_tensor(hid[:, i, NL:T], hid[:, i, NL:T], gcx[:, 0:NC_], MUL).then_inc(gfree(), 1)
                    taken(e, l, ("gate", i))
                    free, lat, cx = ready(("up", i))
                    V.tensor_tensor(hid[:, i, 0:NL], hid[:, i, 0:NL], lat[:, :], MUL)
                    V.tensor_tensor(hid[:, i, NL:T], hid[:, i, NL:T], cx[:, 0:NC_], MUL).then_inc(free(), 1)
                for m in range(KT):
                    residual("f2", m, 40)

            assert own.most == DVE_CHAIN, own.most
            own.l = DEPTH
            own.n = 0
            own.after(V.tensor_copy(gain[:, 2, :, :], cvec[:, 16:24].unsqueeze(2).to_broadcast([128, 8, 2])))
            norm_scale(DEPTH, 0, 2, False)

        bad = [n for n, s in signals.items() if not s.check(n)]
        assert not bad, bad


INS = ["x_prompt", "x_sample", "cache_k", "cache_v", "state_rwkv", "c", "c_ctx", "w_ada", "b_ada", "norm_mix_g",
       "norm_ffn_g", "w_in", "w_out", "attn_sink", "rwkv_shift_w", "rwkv_w0", "rwkv_w_up", "rwkv_a0", "rwkv_a_up",
       "rwkv_g_up", "rwkv_k_k", "rwkv_k_a", "rwkv_r_k", "rwkv_ln_g", "rwkv_ln_b", "ffn_w_in", "ffn_w_out",
       "norm_final_g"]
OUTS = [("y_p", (1, NC_, D)), ("y_s", (1, NL, D)), ("new_k", (1, DEPTH, NC_, 2, HD)),
        ("new_v", (1, DEPTH, NC_, 2, HD)), ("new_s", (1, DEPTH, 2, 4, HD, HD))]


def tables():
    out = {}
    p = np.arange(128)
    mats = np.zeros((128, 5, 128), np.float32)
    mats[p, 0, p] = 1.0
    mats[p, 1, p ^ 16] = 1.0
    mats[:, 2, :] = 1.0 / D
    same_head = (p[:, None] // HD) == (p[None, :] // HD)
    mats[:, 3, :] = same_head
    mats[:, 4, :] = same_head / float(HD)
    out["t_mats"] = mats
    same = (p[:, None] // CH) == (p[None, :] // CH)
    m = np.zeros((128, 2, 2, 128), np.float32)
    i, t = p[:, None], p[None, :]
    m[:, 0, 0], m[:, 0, 1] = same & (i < t), same & (i <= t)
    m[:, 1, 0], m[:, 1, 1] = same & (i > t), same & (i >= t)
    out["t_masks"] = m.reshape(128, 2, 256)
    lv = np.zeros((128, 2, 6, 128), np.float32)
    for n, size in enumerate(LEVELS):
        pair = (p[:, None] // (2 * size)) == (p[None, :] // (2 * size))
        late, early = (p[:, None] // size) % 2 == 1, (p[None, :] // size) % 2 == 0
        lv[:, 0, n] = pair & late & early
        lv[:, 1, n] = lv[:, 0, n].T
    out["t_lvl"] = lv
    am = np.zeros((128, 4, 128), np.float32)
    am[:, 0] = np.where(t >= i, 0.0, -1e30)
    am[:, 3] = np.where(t <= i, 0.0, -1e30)
    out["t_attmask"] = am.reshape(128, 512)
    j = np.arange(T)
    out["t_reset"] = np.broadcast_to((j % CH != 0).astype(np.float32), (128, T)).copy()
    d = np.arange(HD)
    a = 2 * np.pi * np.outer(d, d) / HD
    ch = np.zeros((128, 2, 128), np.float64)
    for g in range(2):
        o = slice(HD * g, HD * g + HD)
        ch[o, 0, o], ch[o, 1, o] = np.cos(a) / 8.0, np.sin(a) / 8.0
    out["t_chan"] = ch.reshape(128, 256).astype(np.float32)
    for n, name in ((NL, ""), (NC_, "x")):
        q = np.arange(n)
        a = 2 * np.pi * (np.outer(q, q) % n) / n
        for f, fn in (("c", np.cos(a)), ("s", -np.sin(a))):
            tab = (fn / math.sqrt(n)).astype(np.float32)
            out["t_dft" + f + name] = tab.reshape(n // 128, 128, n).transpose(1, 0, 2).copy().reshape(
                (128, n // 128, n) if n == NL else (128, n))
    tok = np.arange(NL)
    pos = np.stack([tok // 64, tok % 64]).astype(np.float64)
    inv = 10000.0 ** (-np.arange(16) / 16.0)
    dd = p % HD
    ang = pos[dd // 32] * inv[dd % 16][:, None]
    sign = np.where((dd % 32) < 16, -1.0, 1.0)[:, None]
    out["t_rope"] = np.stack([np.cos(ang), sign * np.sin(ang)], axis=1).astype(np.float32)
    return out


def kernel(**inputs):
    import concourse.bacc as _bacc
    from concourse.bass_utils import run_bass_kernel_spmd as _run

    nc = _bacc.Bacc("TRN2", target_bir_lowering=False, num_devices=1)
    f32 = mybir.dt.float32
    arrays, I, O = {}, {}, {}
    named = [(n, np.ascontiguousarray(inputs[n])) for n in INS] + list(tables().items())
    for name, a in named:
        arrays["in_" + name] = a
        I[name] = nc.dram_tensor("in_" + name, a.shape, f32, kind="ExternalInput").ap()
    for name, shape in OUTS:
        O[name] = nc.dram_tensor("out_" + name, shape, f32, kind="ExternalOutput").ap()
    build(nc, I, O)
    r = _run(nc, [arrays], core_ids=[0])
    return tuple(r.results[0]["out_" + name] for name, _ in OUTS)
```

```python
import math
import numpy as np
import concourse.bass as bass
from concourse import mybir
from contextlib import ExitStack

D = 1024
NC_ = 128
NL = 512
T = NL + NC_
DEPTH = 2
KT = D // 128
DFF = 2816
FT = DFF // 128
HD = 64
IN_W = 2176
CH = 64
NCH = T // CH
LCH = NL // CH
DECAY = 0.6065306597126334
GN_EPS = 64e-5
RMS_EPS = 1e-6
STREAMS = ((0, NL), (NL, T))
LEVELS = (1, 2, 4, 8, 16, 32)
TH = T // 2
SLOTS = 4
SLOT_W = 2048
FH = FT // 2

PR_ADA, PR_NMIX, PR_NFFN, PR_SHIFT, PR_W0, PR_A0, PR_KK, PR_KA, PR_RK, PR_LNG, PR_LNB = (
    0, 48, 56, 64, 91, 95, 99, 101, 103, 105, 107)
NPR = 109

def chunk_order():
    order = [("ada", i) for i in range(8)]
    proj = [("rw", i) for i in range(5)] + [("q", 0), ("q", 1), ("k", 0), ("v", 0), ("fn", 0), ("fn", 1)]
    ada = 8
    for p in proj:
        order.append(p)
        if p[0] in ("rw", "q", "v"):
            order += [("ada", ada), ("ada", ada + 1)]
            ada += 2
    order += [("dftx", 0), ("dftc", 0), ("dfts", 0)]
    order += [("wo", i) for i in range(4)]
    for hf in range(2):
        order += [("f1", FH * hf + i) for i in range(FH)] + [("f2", 2 * m + hf) for m in range(KT)]
    return order


CHUNKS = chunk_order()
CHUNK_AT = {c: i for i, c in enumerate(CHUNKS)}
NCHUNK = len(CHUNKS)
assert NCHUNK % SLOTS == 0
DMAS = {"ada": 1, "rw": 1, "q": 4, "k": 1, "v": 1, "fn": 1, "dftx": 3, "dftc": 1, "dfts": 1, "wo": 3, "f1": 2, "f2": 1}


def ready_counts():
    tot, out = [0] * SLOTS, []
    for i, (kind, _) in enumerate(CHUNKS):
        tot[i % SLOTS] += 16 * DMAS[kind]
        out.append(tot[i % SLOTS])
    return out, tot


READY, READY_TOT = ready_counts()


LAST_ITEM = {("q", i): ("q", 2 * i + 1) for i in range(2)}
LAST_ITEM.update({("rw", i): ("rw", min(2 * i + 1, 8)) for i in range(5)})
LAST_ITEM.update({("k", 0): ("k", 0), ("v", 0): ("v", 0), ("fn", 0): ("fn", 0), ("fn", 1): ("fn", 1)})
LAST_ITEM.update({(t, 0): ("ft2", 1) for t in ("dftx", "dftc", "dfts")})
LAST_ITEM.update({("wo", i): ("out", 2 * i + 1) for i in range(4)})


def ffn_units():
    u = []
    for hf in range(2):
        for i in range(FH * hf, FH * hf + FH):
            u += [(("gate", i), ("f1", i), 0, KT), (("up", i), ("f1", i), 1, KT)]
        u += [(("f2", m, hf), ("f2", 2 * m + hf), 0, FH) for m in range(KT)]
    return u


UNITS = ffn_units()
NUNIT = len(UNITS)
UNIT_OF = {x[0]: n for n, x in enumerate(UNITS)}
LAST_UNIT = {x[1]: n for n, x in enumerate(UNITS)}


def item_order():
    o = [("norm", 0), ("small", 0)]
    o += [("rw", m) for m in range(9)]
    o += [("q", 0), ("q", 1), ("swap", 0), ("q", 2), ("swap", 1), ("q", 3), ("swap", 2),
          ("k", 0), ("swap", 3), ("v", 0), ("swap", 4), ("fn", 0), ("kvT", 0), ("fn", 1)]

    def prep(t):
        return [("w", t, 0), ("w", t, 1), ("a", t, 0), ("a", t, 1), ("kk", t), ("bonus", t)]

    def attn(blocks):
        r = []
        for b in blocks:
            r += [("s", b, i) for i in range(8)] + [("oT", b)]
        return r

    o += prep(0) + [("ft1", i) for i in range(5)] + [("ft2", 0), ("ft2", 1)] + attn(ATT_A)
    o += prep(1) + attn(ATT_B)
    o += [("mean", 0), ("mean", 1), ("var", 0), ("var", 1), ("g", 0), ("g", 1)]
    o += [("out", m) for m in range(KT)] + [("norm", 1)]
    for hf in range(2):
        for i in range(FH * hf, FH * hf + FH):
            o += [("gate", i), ("up", i)]
        o += [("f2", m, hf) for m in range(KT)]
    return o


ATT_A = (0, 1)
ATT_B = (2, 3, 4)
ITEMS = item_order()
ITEM_AT = {x: i for i, x in enumerate(ITEMS)}
NITEM = len(ITEMS)
assert NITEM % 2 == 0 and len(ITEM_AT) == NITEM

def key_tiles(b):
    if b == 4:
        return [("cur", 4)]
    r = []
    if b > 0:
        r.append(("lat", b - 1))
    r += [("lat", b), ("cache", 0)]
    if b < 3:
        r.append(("lat", b + 1))
    return r


def mask_cols(b):
    if b == 4:
        return 128, 256
    return (0 if b > 0 else 128), (512 if b < 3 else 384)


GROUPS = [[(0, 0, 0), (1, 0, 1), (2, 1, 3), (3, 1, 2)],
          [(0, 0, 2), (1, 0, 3), (2, 1, 1), (3, 1, 0)],
          [(0, 0, 4), (2, 1, 4)]]
NPAIR = sum(len(g) for g in GROUPS)


def chain_steps(group):
    out = []
    per_dir = {0: [], 1: []}
    for p, d, t in group:
        for hf in ((0, 1) if d == 0 else (1, 0)):
            per_dir[d].append((p, d, t, hf, 2 * t + hf))
    for a, b in zip(per_dir[0], per_dir[1]):
        out += [a, b]
    return out


def first_touch(g, d, t):
    return (g == 0) or (g == 2 and d == 0)


def needs_state(chunk, d):
    return chunk != (LCH - 1 if d == 0 else 0)


def y_order(group):
    seen, out = {}, []
    for s in chain_steps(group):
        seen[s[0]] = seen.get(s[0], 0) + 1
        if seen[s[0]] == 2:
            out.append(s[:3])
    return out


def state_plan():
    plan, n = {}, 0
    for ht in range(2):
        for g, group in enumerate(GROUPS):
            if g != 1:
                cur = {0: (0, None), 1: (0, None)}
            for (p, d, t, hf, ck) in chain_steps(group):
                plan[(ht, g, d, ck)] = cur[d]
                if needs_state(ck, d):
                    n += 1
                    cur[d] = (1 - cur[d][0], n)
    return plan


class Signal:

    def __init__(self, sem, per_layer, primed=0):
        self.sem, self.per, self.made, self.primed = sem, per_layer, 0, primed

    def __call__(self, n=1):
        self.made += n
        return self.sem

    def upto(self, l, n):
        assert n + self.primed > 0
        return l * self.per + n + self.primed

    def check(self, name, extra=0):
        if self.made - extra != self.per:
            print("SIGNAL", name, "makes", self.made - extra, "per layer, declared", self.per)
        return self.made - extra == self.per


class Own:

    def __init__(self, eng, sem, per_layer):
        self.eng, self.sem, self.per, self.n, self.l, self.most = eng, sem, per_layer, 0, 0, 0

    def after(self, ins):
        self.n += 1
        ins.then_inc(self.sem, 1)
        self.most = max(self.most, self.n)
        self.eng.wait_ge(self.sem, self.l * self.per + self.n)


DVE_CHAIN, POOL_CHAIN = 139, 2


def build(nc, I, O):
    f32 = mybir.dt.float32
    f32r = mybir.dt.float32r
    ALU = mybir.AluOpType
    ACT = mybir.ActivationFunctionType
    AX = mybir.AxisListType
    MUL, ADD, SUB, MAX = ALU.mult, ALU.add, ALU.subtract, ALU.max
    ctx = ExitStack()
    with ctx:
        def sb(name, shape):
            return ctx.enter_context(nc.sbuf_tensor(name, shape, f32))

        signals = {}

        def sig(name, per, primed=0):
            s = Signal(ctx.enter_context(nc.semaphore(name)), per, primed)
            signals[name] = s
            return s

        def sem(name):
            return ctx.enter_context(nc.semaphore(name))

        x = sb("x", [128, KT, T])
        ring = sb("ring", [128, SLOTS, SLOT_W])
        MN = sb("MN", [128, 4, 2, 2, 128])
        St = sb("St", [128, 2, 2, 128])
        masks = sb("masks", [128, 2, 256])
        lvl = sb("lvl", [128, 2, 6, 128])
        attmask = sb("attmask", [128, 512])
        mats = sb("mats", [128, 5, 128])
        reset = sb("reset", [128, T])
        lora = sb("lora", [128, 3, 256])
        prow = sb("prow", [NPR, 128])
        par = sb("par", [128, NPR])
        cvec = sb("cvec", [128, 24])
        csil = sb("csil", [128, KT, 2])
        csil_s = sb("csil_s", [128, 16])
        mod = sb("mod", [128, 48, 2])
        gain = sb("gain", [128, 3, KT, 2])
        sink = sb("sink", [128, 8])
        omka = sb("omka", [128, 2])
        eps = sb("eps", [128, 3])
        mid = sb("mid", [128, 2, NCH])
        end = sb("end", [128, 2, NCH])
        emid = sb("emid", [128, 2, NCH])
        eend = sb("eend", [128, 2, NCH])
        dec = sb("dec", [128, 2, NCH])
        negm = sb("negm", [128, 2, 8])
        den = sb("den", [128, 2, 8])
        esk = sb("esk", [128, 2, 8])
        kcT = sb("kcT", [128, 128])
        ckv = sb("ckv", [128, 2, 128])
        kvout = sb("kvout", [128, 128])
        s0in = sb("s0in", [128, 2, 128])
        with nc.sbuf_tensor("h", [128, KT, T], f32) as h, nc.sbuf_tensor("mix", [128, 25736], f32) as mix:
            pass
        def sbr(name, shape):
            return ctx.enter_context(nc.sbuf_tensor(name, shape, f32r))

        hid_hi = sbr("hid_hi", [128, FH, T])
        h_hi = sbr("h_hi", [128, KT, T])
        h_lo = sbr("h_lo", [128, KT, T])
        hid_lo = sbr("hid_lo", [128, FH, T])
        wsplit = sbr("wsplit", [128, 2, 2, FH * 128])
        tmp = sb("tmp", [128, T])

        ident, swapm, onesD, ones64, mean64 = (mats[:, i, :] for i in range(5))

        def mixv(at, n):
            return mix[:, at:at + n]

        def rows(at, n):
            return mix[:, at:at + n * T].rearrange("p (a t) -> p a t", t=T)

        ush = rows(0, 9)
        qt = rows(5760, 4)
        kt = mixv(8320, T)
        vtok = mixv(8960, T)
        uf = rows(9600, 2)
        S2 = rows(10880, 2)
        CC = rows(12160, 2)
        E0 = 13440
        raw = mix[:, E0:E0 + 1286].rearrange("p (a t) -> p a t", t=643)
        e01 = rows(E0, 2)
        KK = mixv(14726, T)
        rot = mixv(15366, T)
        PB = 16006
        PW = 2432
        pb = [PB + PW * p for p in range(4)]
        assert pb[3] + PW <= 25736
        LP = [mix[:, b:b + 1024].rearrange("p (a t) -> p a t", a=2) for b in pb]
        Yi = [mix[:, b + 1024:b + 1280].rearrange("p (a t) -> p a t", a=2) for b in pb]
        Xi = [mix[:, b + 1280:b + 1536].rearrange("p (a t) -> p a t", a=2) for b in pb]
        P1 = [mix[:, b + 1536:b + 1792].rearrange("p (a t) -> p a t", a=2) for b in pb]
        TOK = [mix[:, b + 1792:b + 2176].rearrange("p (a t) -> p a t", a=3) for b in pb]
        W1A = [mix[:, b + 2176:b + 2432].rearrange("p (a t) -> p a t", a=2) for b in pb]
        UG = P1
        Qt = [mix[:, b + 1280:b + 1408] for b in pb]
        rope = mix[:, PB:PB + 1024].rearrange("p (a t) -> p a t", a=2)
        Z = mix[:, PB:PB + 2560].rearrange("p (a t) -> p a t", a=5)
        Pm = mix[:, PB:PB + 1536].rearrange("p (a t) -> p a t", a=3)
        PT = mix[:, PB + 1536:PB + 2560].rearrange("p (a t) -> p a t", a=2)
        otok = mix[:, PB + 2560:PB + 3584].rearrange("p (a t) -> p a t", a=2)
        mrow = St[0:2, :, :, :].rearrange("p d s c -> p (d s c)")
        stout = rot[:, 0:256].rearrange("p (a t) -> p a t", a=2)
        xin = mix[:, 0:5 * D].rearrange("p (a t) -> p a t", a=5)
        crow = mix[0:24, 5 * D:5 * D + 128]
        yout = mix[:, 0:2 * D].rearrange("p (a t) -> p a t", a=2)

        PS = ctx.enter_context(nc.psum_tensor("PS", [128, 8, 512], f32))
        ps = [PS[:, i, :] for i in range(8)]

        ld_const = sem("ld_const")
        ld_x = [sem(f"ld_x{t}") for t in range(5)]
        ld_tab = sem("ld_tab")
        ld_prow = sig("ld_prow", 16 * 15)
        ld_par = sig("ld_par", 16 * 6)
        ld_rope = sig("ld_rope", 16)
        ld_state = [sig(f"ld_state{t}", 64) for t in range(2)]
        w_ready = [sig(f"w_ready{s}", READY_TOT[s]) for s in range(SLOTS)]
        wh_ready = sig("wh_ready", NUNIT)
        wl_ready = sig("wl_ready", NUNIT, primed=4)
        hl_ready = sig("hl_ready", KT)
        hid_split = sig("hid_split", FT)
        acc_ready = sig("acc_ready", NITEM)
        acc_free = [sig(f"acc_free{i}", NITEM // 2, primed=1) for i in range(2)]
        sq_ready = sig("sq_ready", 2 * KT)
        sq_used = sig("sq_used", 2 * (KT - 1))
        h_scaled = sig("h_scaled", 2 * KT)
        h_ready = sig("h_ready", 2 * KT)
        gain_ready = sig("gain_ready", 2)
        ada_done = sig("ada_done", 24)
        mrow_sb = sig("mrow_sb", 12)
        mcol_ps = sig("mcol_ps", 12)
        par_ready = sig("par_ready", 1, primed=1)
        conv_out = sig("conv_out", 9)
        pads_zero = sig("pads_zero", 1)
        rot_raw = sig("rot_raw", 5)
        rot_cos = sig("rot_cos", 5)
        rot_done = sig("rot_done", 5, primed=1)
        kv_stored = sig("kv_stored", 32)
        lora_in = sig("lora_in", 1)
        kk_raw = sig("kk_raw", 2)
        kk_sq = sig("kk_sq", 2)
        rk_prod = sig("rk_prod", 2)
        cum_ready = sig("cum_ready", 2)
        exps_ready = sig("exps_ready", 2)
        kk_ready = sig("kk_ready", 2)
        ar_done = sig("ar_done", 2)
        scaled_ready = sig("scaled_ready", 2)
        p_ready = sig("p_ready", 40)
        p_exp = sig("p_exp", 40)
        pt_ps = sig("pt_ps", 40, primed=1)
        pt_sb = sig("pt_sb", 40, primed=1)
        pv_done = sig("pv_done", 40, primed=1)
        esk_in = sig("esk_in", 5)
        esk_ready = sig("esk_ready", 5)
        o_ready = sig("o_ready", 5, primed=1)
        mn_zero = sem("mn_zero")
        ctx_zero = sig("ctx_zero", 2)
        n2 = 2 * NPAIR
        s0_ps = sig("s0_ps", 4, primed=1)
        s0_sb = sig("s0_sb", 4)
        tok_ps, tok_sb = sig("tok_ps", n2), sig("tok_sb", n2)
        prod_ps, prod_sb = sig("prod_ps", 2 * n2), sig("prod_sb", 2 * n2)
        inv0_sb = sig("inv0_sb", n2)
        xt_ps, xt_sb = sig("xt_ps", 5 * n2), sig("xt_sb", 5 * n2)
        p1_ps, p1_sb = sig("p1_ps", 5 * n2), sig("p1_sb", 5 * n2)
        yu_ps, yu_sb = sig("yu_ps", 5 * n2), sig("yu_sb", 5 * n2)
        w1_ps, w1_sb = sig("w1_ps", n2), sig("w1_sb", n2)
        ug_ps, ug_sb = sig("ug_ps", n2), sig("ug_sb", n2)
        qmn_ps, qmn_sb = sig("qmn_ps", n2), sig("qmn_sb", n2)
        nstep = 2 * sum(1 for g in GROUPS for s in chain_steps(g) if needs_state(s[4], s[1]))
        st_ps, st_sb = sig("st_ps", nstep), sig("st_sb", nstep)
        y_ps, y_sb = sig("y_ps", n2), sig("y_sb", n2)
        fin_ps, fin_sb, fin_st = sig("fin_ps", 2), sig("fin_sb", 2), sig("fin_st", 128)
        ysq_ready = sig("ysq_ready", 2)
        hid_sig = sig("hid_sig", FT)
        xT_ps, xT_sb, c_ready = sem("xT_ps"), sem("xT_sb"), sem("c_ready")
        yT_ps, yT_sb, y_stored = sem("yT_ps"), sem("yT_sb"), [sem("y_stored0"), sem("y_stored1")]
        dve_own, pool_own = sem("dve_own"), sem("pool_own")
        sp_passed, pool_passed = sem("sp_passed"), sem("pool_passed")

        def acc_item(name):
            i = ITEM_AT[name]
            return i, ps[i % 2], ps[2 + i % 2]

        def pair_index(ht, g, n):
            return ht * NPAIR + sum(len(q) for q in GROUPS[:g]) + n

        def taken(e, l, name, settled=None):
            i = ITEM_AT[name]
            e.wait_ge(acc_free[i % 2].sem, acc_free[i % 2].upto(l, i // 2 + 1))
            if settled:
                settled()

        def layer_before(e, l, settled=None):
            for f in acc_free:
                e.wait_ge(f.sem, f.upto(l, 0))
            if settled:
                settled()

        def unit_weights(u):
            _, ck, g, nk = UNITS[u]
            n = CHUNK_AT[ck]
            raw_w = ring[:, n % SLOTS, 0:(2 if nk == KT else 1) * nk * 128].rearrange("p (k c) -> p k c", k=nk)
            parts = [wsplit[:, u % 2, i, 0:nk * 128].rearrange("p (k c) -> p k c", k=nk) for i in range(2)]
            return n, raw_w[:, :, 128 * g:128 * g + 128], parts[0], parts[1]

        PLAN = state_plan()

        block = ctx.enter_context(nc.Block())

        @block.sync
        def _(e):
            def settled():
                e.sem_inc(sp_passed)

            e.dma_start(crow[0:8, :], I["c"][0].rearrange("(a p) -> a p", p=128)).then_inc(ld_const, 16)
            e.dma_start(crow[8:16, :], I["c_ctx"].rearrange("(a p) -> a p", p=128)).then_inc(ld_const, 16)
            e.dma_start(crow[16:24, :], I["norm_final_g"].rearrange("(a p) -> a p", p=128)).then_inc(ld_const, 16)
            e.dma_start(mats[:, :, :], I["t_mats"]).then_inc(ld_const, 16)
            for t in range(5):
                src_x = I["x_sample"][0, 128 * t:128 * t + 128, :] if t < 4 else I["x_prompt"][0]
                e.dma_start(xin[:, t, :], src_x).then_inc(ld_x[t], 16)
            with e.Fori(0, DEPTH) as l:
                e.wait_ge(par_ready.sem, par_ready.upto(l, 0))
                settled()

                def prm(at, n, src):
                    e.dma_start(prow[at:at + n, :], src.rearrange("(a p) -> a p", p=128)).then_inc(ld_prow(16), 16)

                prm(PR_ADA, 48, I["b_ada"][l])
                prm(PR_NMIX, 8, I["norm_mix_g"][l])
                prm(PR_NFFN, 8, I["norm_ffn_g"][l])
                for j in range(3):
                    prm(PR_SHIFT + 9 * j, 9, I["rwkv_shift_w"][l, j])
                for d in range(2):
                    prm(PR_W0 + 2 * d, 2, I["rwkv_w0"][l, d])
                    prm(PR_A0 + 2 * d, 2, I["rwkv_a0"][l, d])
                prm(PR_KK, 2, I["rwkv_k_k"][l])
                prm(PR_KA, 2, I["rwkv_k_a"][l])
                prm(PR_RK, 2, I["rwkv_r_k"][l].rearrange("h d -> (h d)"))
                prm(PR_LNG, 2, I["rwkv_ln_g"][l])
                prm(PR_LNB, 2, I["rwkv_ln_b"][l])
                for n, (kind, i) in enumerate(CHUNKS):
                    if n == 8:
                        layer_before(e, l, settled)
                        e.dma_start(lora[:, 0, :], I["rwkv_w_up"][l].rearrange("d r c -> (d r) c")).then_inc(ld_par(16), 16)
                        e.dma_start(lora[:, 1, :], I["rwkv_a_up"][l].rearrange("d r c -> (d r) c")).then_inc(ld_par(16), 16)
                        e.dma_start(lora[:, 2, :], I["rwkv_g_up"][l]).then_inc(ld_par(16), 16)
                        e.dma_start(ckv[:, 0, :], I["cache_k"][0, l].rearrange("s h d -> s (h d)")).then_inc(ld_par(16), 16)
                        e.dma_start(ckv[:, 1, :], I["cache_v"][0, l].rearrange("s h d -> s (h d)")).then_inc(ld_par(16), 16)
                        e.dma_start(sink[:, :], I["attn_sink"][l].partition_broadcast(128)).then_inc(ld_par(16), 16)
                        e.dma_start(rope, I["t_rope"]).then_inc(ld_rope(16), 16)
                    old = CHUNKS[n - SLOTS]
                    if old[0] == "ada":
                        e.wait_ge(ada_done.sem, ada_done.upto(l, old[1] + 1))
                    elif old in LAST_UNIT:
                        e.wait_ge(wl_ready.sem, wl_ready.upto(l, LAST_UNIT[old] + 1 - (NUNIT if n < SLOTS else 0)))
                    else:
                        e.wait_ge(acc_ready.sem, acc_ready.upto(l, ITEM_AT[LAST_ITEM[old]] + 1))
                    settled()
                    sl = n % SLOTS
                    dst = ring[:, sl, 0:2048].rearrange("p (k c) -> p k c", k=KT)
                    done = w_ready[sl]

                    def src(w, c0, n_):
                        return w[l, :, c0:c0 + n_].rearrange("(k p) c -> p k c", p=128)

                    if kind == "ada":
                        e.dma_start(dst, src(I["w_ada"], 256 * i, 256)).then_inc(done(16), 16)
                    elif kind == "rw":
                        w_ = 256 if i < 4 else 128
                        e.dma_start(dst[:, :, 0:w_], src(I["w_in"], 768 + 256 * i, w_)).then_inc(done(16), 16)
                    elif kind == "q":
                        for j in range(2):
                            for g in range(2):
                                e.dma_start(dst[:, :, 128 * j + 64 * g:128 * j + 64 * g + 64],
                                            src(I["w_in"], 128 * i + 64 * j + 256 * g, 64)).then_inc(done(16), 16)
                    elif kind in ("k", "v", "fn"):
                        c0 = {"k": 512, "v": 640, "fn": 1920 + 128 * i}[kind]
                        e.dma_start(dst[:, :, 0:128], src(I["w_in"], c0, 128)).then_inc(done(16), 16)
                    elif kind == "dftx":
                        e.dma_start(ring[:, sl, 0:128], I["t_dftcx"]).then_inc(done(16), 16)
                        e.dma_start(ring[:, sl, 128:256], I["t_dftsx"]).then_inc(done(16), 16)
                        e.dma_start(ring[:, sl, 256:512], I["t_chan"]).then_inc(done(16), 16)
                    elif kind in ("dftc", "dfts"):
                        e.dma_start(ring[:, sl, 0:2048].rearrange("p (k c) -> p k c", k=4),
                                    I["t_" + kind]).then_inc(done(16), 16)
                    elif kind == "wo":
                        wo = I["w_out"]
                        c0 = 256 * i
                        for g in range(2):
                            e.dma_start(dst[64 * g:64 * g + 64, 0:4, :],
                                        wo[l, 256 * g:256 * g + 256, c0:c0 + 256].rearrange(
                                            "(k p) c -> p k c", p=64)).then_inc(done(16), 16)
                        e.dma_start(dst[:, 4:8, :], wo[l, 512:1024, c0:c0 + 256].rearrange(
                            "(k p) c -> p k c", p=128)).then_inc(done(16), 16)
                    elif kind == "f1":
                        for g in range(2):
                            e.dma_start(dst[:, :, 128 * g:128 * g + 128],
                                        src(I["ffn_w_in"], DFF * g + 128 * i, 128)).then_inc(done(16), 16)
                    else:
                        m, hf = i // 2, i % 2
                        e.dma_start(ring[:, sl, 0:FH * 128].rearrange("p (k c) -> p k c", k=FH),
                                    I["ffn_w_out"][l, FH * 128 * hf:FH * 128 * (hf + 1),
                                                   128 * m:128 * m + 128].rearrange(
                                        "(k p) c -> p k c", p=128)).then_inc(done(16), 16)
            for t in range(5):
                e.wait_ge(yT_sb, t + 1)
                dst = O["y_s"][0, 128 * t:128 * t + 128, :] if t < 4 else O["y_p"][0]
                e.dma_start(dst, yout[:, t % 2, :]).then_inc(y_stored[t % 2], 16)
            e.wait_ge(y_stored[0], 48)
            e.wait_ge(y_stored[1], 32)

        @block.gpsimd
        def _(e):
            own = Own(e, pool_own, POOL_CHAIN)

            def settled():
                e.sem_inc(pool_passed)

            e.dma_start(masks[:, :, :], I["t_masks"]).then_inc(ld_tab, 16)
            e.dma_start(lvl[:, :, :, :], I["t_lvl"]).then_inc(ld_tab, 16)
            e.dma_start(attmask[:, :], I["t_attmask"]).then_inc(ld_tab, 16)
            e.dma_start(reset[:, :], I["t_reset"]).then_inc(ld_tab, 16)
            nc.gpsimd.memset(MN[:, :, :, :, :], 0.0).then_inc(mn_zero, 1)
            nc.gpsimd.memset(s0in[:, :, :], 0.0).then_inc(mn_zero, 1)
            nc.gpsimd.memset(eps[:, 0:1], RMS_EPS).then_inc(mn_zero, 1)
            nc.gpsimd.memset(eps[:, 1:2], 1e-12).then_inc(mn_zero, 1)
            nc.gpsimd.memset(eps[:, 2:3], GN_EPS).then_inc(mn_zero, 1)
            e.wait_ge(mn_zero, 5)
            e.wait_ge(xT_ps, 11)
            with e.Fori(0, DEPTH) as l:
                own.l, own.n = l, 0
                layer_before(e, l, settled)
                nc.gpsimd.memset(raw[:, :, 0:1], 0.0)
                nc.gpsimd.memset(raw[:, :, 513:514], 0.0)
                nc.gpsimd.memset(raw[:, :, 642:643], 0.0).then_inc(pads_zero(), 1)
                e.wait_ge(ld_rope.sem, ld_rope.upto(l, 16))
                settled()
                for r in range(5):
                    dst = qt[:, r, 0:NL] if r < 4 else kt[:, 0:NL]
                    e.wait_ge(rot_raw.sem, rot_raw.upto(l, r + 1))
                    settled()
                    nc.gpsimd.tensor_tensor(dst, raw[:, r % 2, 0:NL], rope[:, 0, :], MUL).then_inc(rot_cos(), 1)
                taken(e, l, ("kvT", 0), settled)
                e.dma_start(O["new_k"][0, l].rearrange("s h d -> s (h d)"), kvout[:, :]).then_inc(kv_stored(16), 16)
                e.dma_start(O["new_v"][0, l].rearrange("s h d -> s (h d)"), vtok[:, 512:640]).then_inc(kv_stored(16), 16)

                def prep(t):
                    e.wait_ge(conv_out.sem, conv_out.upto(l, 9))
                    settled()
                    e.wait_ge(acc_ready.sem, acc_ready.upto(l, ITEM_AT[("w", t, 0)] + 1))
                    settled()
                    nc.gpsimd.tensor_scalar(KK, ush[:, 2 + t, :], par[:, PR_KK + t:PR_KK + t + 1], None,
                                            MUL).then_inc(kk_raw(), 1)
                    own.after(nc.gpsimd.tensor_tensor(e01[:, 1, :], ush[:, t, :], ush[:, 2 + t, :], MUL))
                    settled()
                    nc.gpsimd.tensor_scalar(e01[:, 1, :], e01[:, 1, :], par[:, PR_RK + t:PR_RK + t + 1], None,
                                            MUL).then_inc(rk_prod(), 1)
                    e.wait_ge(s0_ps.sem, s0_ps.upto(l, 2 * t))
                    settled()
                    for d in range(2):
                        for g in range(2):
                            e.dma_start(s0in[64 * g:64 * g + 64, d, 64 * g:64 * g + 64],
                                        I["state_rwkv"][0, l, d, 2 * t + g]).then_inc(ld_state[t](16), 16)
                    e.wait_ge(exps_ready.sem, exps_ready.upto(l, t + 1))
                    settled()
                    e.wait_ge(kk_ready.sem, kk_ready.upto(l, t + 1))
                    settled()
                    rb = ush[:, t:t + 1, :].to_broadcast([128, 2, T])
                    kb = KK.unsqueeze(1).to_broadcast([128, 2, T])
                    nc.gpsimd.tensor_tensor(h[:, 2:4, :], h[:, 2:4, :], rb, MUL)
                    nc.gpsimd.tensor_tensor(h[:, 0:2, :], h[:, 0:2, :], kb, MUL).then_inc(ar_done(), 1)

                prep(0)
                prep(1)
                for t in range(2):
                    e.wait_ge(fin_sb.sem, fin_sb.upto(l, t + 1))
                    settled()
                    for d in range(2):
                        for g in range(2):
                            e.dma_start(O["new_s"][0, l, d, 2 * t + g],
                                        stout[64 * g:64 * g + 64, d, 64 * g:64 * g + 64]).then_inc(fin_st(16), 16)
                    e.wait_ge(fin_st.sem, fin_st.upto(l, 64 * (t + 1)))
                    settled()
                e.wait_ge(kv_stored.sem, kv_stored.upto(l, 32))
                settled()
                for u in range(NUNIT):
                    n, raw_w, hi, lo = unit_weights(u)
                    e.wait_ge(wh_ready.sem, wh_ready.upto(l, u + 1))
                    settled()
                    nc.gpsimd.tensor_tensor(lo, raw_w, hi, SUB).then_inc(wl_ready(), 1)
            assert own.most == POOL_CHAIN, own.most

        @block.tensor
        def _(e):
            mm = nc.tensor.matmul
            tr = nc.tensor.transpose

            e.wait_ge(ld_const, 16 * 4)
            tr(ps[6][:, 0:24], crow, ident[0:24, 0:24]).then_inc(xT_ps, 1)
            for t in range(5):
                e.wait_ge(ld_x[t], 16)
                for g in range(2):
                    n = 2 * t + g
                    if n >= 2:
                        e.wait_ge(xT_sb, n - 1)
                    for k in range(4):
                        last = tr(ps[4 + n % 2][:, 128 * k:128 * k + 128],
                                  xin[:, t, 512 * g + 128 * k:512 * g + 128 * k + 128], ident)
                    last.then_inc(xT_ps, 1)
            e.wait_ge(c_ready, 3)
            e.wait_ge(xT_sb, 10)

            with e.Fori(0, DEPTH) as l:
                def begin(name):
                    i, lat, cx = acc_item(name)
                    e.wait_ge(acc_free[i % 2].sem, acc_free[i % 2].upto(l, i // 2))
                    return lat, cx

                def chunk(name):
                    n = CHUNK_AT[name]
                    e.wait_ge(w_ready[n % SLOTS].sem, w_ready[n % SLOTS].upto(l, READY[n]))
                    return ring[:, n % SLOTS, :]

                def both(lat, cx, w, k, n, v):
                    mm(lat[:, :], w, v[:, 0:NL], start=(k == 0), stop=(k == n - 1))
                    return mm(cx[:, 0:NC_], w, v[:, NL:T], start=(k == 0), stop=(k == n - 1))

                def norm(which):
                    lat, cx = begin(("norm", which))
                    for k in range(KT):
                        e.wait_ge(sq_ready.sem, sq_ready.upto(l, which * KT + k + 1))
                        last = both(lat, cx, onesD, k, KT, S2[:, k % 2, :])
                        last.then_inc(sq_used() if k < KT - 1 else acc_ready(), 1)

                def ada_rows(j):
                    bank = ps[6 + j % 2]
                    if j >= 2:
                        e.wait_ge(mrow_sb.sem, mrow_sb.upto(l, j - 1))
                    for i in (2 * j, 2 * j + 1):
                        w = chunk(("ada", i))[:, 0:2048].rearrange("p (k c) -> p k c", k=KT)
                        at = 256 * (i % 2)
                        for k in range(KT):
                            last = mm(bank[0:2, at:at + 256], csil[:, k, :], w[:, k, :],
                                      start=(k == 0), stop=(k == KT - 1))
                        last.then_inc(ada_done(), 1)

                def ada_cols(j):
                    e.wait_ge(mrow_sb.sem, mrow_sb.upto(l, j + 1))
                    bank = ps[4] if j < 4 else ps[5]
                    for g in range(4):
                        mt = 4 * j + g
                        last = mm(bank[:, 2 * mt:2 * mt + 2], mrow[:, 128 * g:128 * g + 128], ident[0:2, 0:2],
                                  start=True, stop=True)
                    last.then_inc(mcol_ps(), 1)

                def gemm(name, w):
                    lat, cx = begin(name)
                    for k in range(KT):
                        if name == ("rw", 0):
                            e.wait_ge(h_ready.sem, h_ready.upto(l, k + 1))
                        last = both(lat, cx, w[k], k, KT, h[:, k, :])
                    last.then_inc(acc_ready(), 1)

                ada_rows(0)
                ada_rows(1)
                ada_cols(0)
                norm(0)
                ada_cols(1)
                e.wait_ge(ld_prow.sem, ld_prow.upto(l, ld_prow.per))
                lat, cx = begin(("small", 0))
                tr(lat[:, 0:NPR], prow[:, :], ident[0:NPR, 0:NPR]).then_inc(acc_ready(), 1)
                ada_rows(2)
                ada_rows(3)
                ada_cols(2)
                ada_cols(3)

                def cols(name, g):
                    w = chunk(name)[:, 0:2048].rearrange("p (k c) -> p k c", k=KT)
                    return [w[:, k, 128 * g:128 * g + 128] for k in range(KT)]

                def swap(r):
                    lat, cx = begin(("swap", r))
                    e.wait_ge(rot_raw.sem, rot_raw.upto(l, r + 1))
                    mm(lat[:, :], swapm, raw[:, r % 2, 0:NL], start=True, stop=True).then_inc(acc_ready(), 1)

                for m in range(9):
                    gemm(("rw", m), cols(("rw", m // 2), m % 2))
                    if m % 2 == 0 and m > 0:
                        ada_cols(3 + m // 2)
                    if m % 2 == 1 or m == 8:
                        ada_rows(4 + m // 2)
                gemm(("q", 0), cols(("q", 0), 0))
                ada_cols(8)
                gemm(("q", 1), cols(("q", 0), 1))
                swap(0)
                ada_rows(9)
                gemm(("q", 2), cols(("q", 1), 0))
                ada_cols(9)
                swap(1)
                gemm(("q", 3), cols(("q", 1), 1))
                swap(2)
                ada_rows(10)
                gemm(("k", 0), cols(("k", 0), 0))
                ada_cols(10)
                swap(3)
                gemm(("v", 0), cols(("v", 0), 0))
                swap(4)
                ada_rows(11)
                gemm(("fn", 0), cols(("fn", 0), 0))
                ada_cols(11)
                lat, cx = begin(("kvT", 0))
                taken(e, l, ("v", 0))
                for t in range(4):
                    tr(lat[:, 128 * t:128 * t + 128], KK[:, 128 * t:128 * t + 128], ident)
                tr(cx[:, 0:128], KK[:, NL:T], ident)
                tr(cx[:, 128:256], kt[:, NL:T], ident)
                e.wait_ge(ld_par.sem, ld_par.upto(l, ld_par.per))
                tr(cx[:, 256:384], ckv[:, 0, :], ident).then_inc(acc_ready(), 1)
                gemm(("fn", 1), cols(("fn", 1), 0))

                def prep(t):
                    if t == 0:
                        e.wait_ge(lora_in.sem, lora_in.upto(l, 1))
                    for kind, which, src in (("w", 0, 7), ("a", 1, 8)):
                        for d in range(2):
                            lat, cx = begin((kind, t, d))
                            both(lat, cx, lora[64 * d:64 * d + 64, which, 128 * t:128 * t + 128], 0, 1,
                                 ush[64 * d:64 * d + 64, src, :]).then_inc(acc_ready(), 1)
                    lat, cx = begin(("kk", t))
                    e.wait_ge(kk_sq.sem, kk_sq.upto(l, t + 1))
                    both(lat, cx, ones64, 0, 1, e01[:, 0, :]).then_inc(acc_ready(), 1)
                    lat, cx = begin(("bonus", t))
                    e.wait_ge(rk_prod.sem, rk_prod.upto(l, t + 1))
                    both(lat, cx, ones64, 0, 1, e01[:, 1, :]).then_inc(acc_ready(), 1)

                prep(0)

                taken(e, l, ("fn", 0))
                taken(e, l, ("fn", 1))
                tx_ = chunk(("dftx", 0))
                for t in range(5):
                    lat, cx = begin(("ft1", t))
                    for f in range(2):
                        last = mm(lat[:, 256 * f:256 * f + 256], uf[:, f, 128 * t:128 * t + 128], tx_[:, 256:512],
                                  start=True, stop=True)
                    last.then_inc(acc_ready(), 1)
                tc_, ts_ = chunk(("dftc", 0)), chunk(("dfts", 0))
                for f in range(2):
                    lat, cx = begin(("ft2", f))
                    if f == 0:
                        taken(e, l, ("ft1", 3))
                        taken(e, l, ("ft1", 4))
                    for t in range(4):
                        mm(lat[:, :], Z[:, t, 256 * f:256 * f + 128], tc_[:, 512 * t:512 * t + 512],
                           start=(t == 0), stop=False)
                        mm(lat[:, :], Z[:, t, 256 * f + 128:256 * f + 256], ts_[:, 512 * t:512 * t + 512],
                           start=False, stop=(t == 3))
                    mm(cx[:, 0:128], Z[:, 4, 256 * f:256 * f + 128], tx_[:, 0:128], start=True, stop=False)
                    mm(cx[:, 0:128], Z[:, 4, 256 * f + 128:256 * f + 256], tx_[:, 128:256],
                       start=False, stop=True).then_inc(acc_ready(), 1)

                def attention(blocks, done):
                    seq = [(b, i) for b in blocks for i in range(8)]

                    def scores(n):
                        b, i = seq[n]
                        j, g = i % 4, i // 4
                        rowsl = slice(64 * g, 64 * g + 64)
                        q = qt[rowsl, j, 128 * b:128 * b + 128]
                        lat, cx = begin(("s", b, i))
                        at = 0
                        for kind, t in key_tiles(b):
                            src = kcT[rowsl, :] if kind == "cache" else kt[rowsl, 128 * t:128 * t + 128]
                            last = mm(lat[:, at:at + 128], q, src, start=True, stop=True)
                            at += 128
                        last.then_inc(acc_ready(), 1)

                    def transposes(n):
                        b, i = seq[n]
                        m = done + n
                        e.wait_ge(p_exp.sem, p_exp.upto(l, m + 1))
                        e.wait_ge(pt_sb.sem, pt_sb.upto(l, max(m - 1, 0)))
                        for c in range(len(key_tiles(b))):
                            last = tr(ps[4 + m % 2][:, 128 * c:128 * c + 128], Pm[:, m % 3, 128 * c:128 * c + 128],
                                      ident)
                        last.then_inc(pt_ps(), 1)

                    def values(n):
                        b, i = seq[n]
                        m = done + n
                        j, g = i % 4, i // 4
                        nb = m // 8
                        if i == 0:
                            e.wait_ge(o_ready.sem, o_ready.upto(l, max(nb - 1, 0)))
                        e.wait_ge(pt_sb.sem, pt_sb.upto(l, m + 1))
                        tiles = key_tiles(b)
                        for c, (kind, t) in enumerate(tiles):
                            v = (ckv[:, 1, 64 * g:64 * g + 64] if kind == "cache"
                                 else vtok[:, 128 * t + 64 * g:128 * t + 64 * g + 64])
                            last = mm(ps[6 + nb % 2][:, 128 * j + 64 * g:128 * j + 64 * g + 64],
                                      PT[:, m % 2, 128 * c:128 * c + 128], v,
                                      start=(c == 0), stop=(c == len(tiles) - 1))
                        last.then_inc(pv_done(), 1)
                        if i == 7:
                            pending.append(b)

                    def out_transposes():
                        b = pending.pop(0)
                        nb = b
                        lat, cx = begin(("oT", b))
                        e.wait_ge(o_ready.sem, o_ready.upto(l, nb + 1))
                        for j in range(4):
                            last = tr(lat[:, 128 * j:128 * j + 128], otok[:, nb % 2, 128 * j:128 * j + 128], ident)
                        last.then_inc(acc_ready(), 1)

                    pending = []
                    for bi, b in enumerate(blocks):
                        lo = 8 * bi
                        for n in range(lo, lo + 8 + 3):
                            if n < lo + 8:
                                scores(n)
                            if lo <= n - 2 < lo + 8:
                                transposes(n - 2)
                            if lo <= n - 3 < lo + 8:
                                values(n - 3)
                        out_transposes()

                e.wait_ge(rot_done.sem, rot_done.upto(l, 5))
                taken(e, l, ("kvT", 0))
                e.wait_ge(par_ready.sem, par_ready.upto(l, 1))
                attention(ATT_A, 0)

                nchain = [0]

                def recurrence(ht, items_before, heads_before):
                    for q_ in range(2):
                        e.wait_ge(acc_free[q_].sem, acc_free[q_].upto(l, (items_before + 1 - q_) // 2))
                    e.wait_ge(scaled_ready.sem, scaled_ready.upto(l, ht + 1))
                    e.wait_ge(ar_done.sem, ar_done.upto(l, ht + 1))
                    e.wait_ge(ld_state[ht].sem, ld_state[ht].upto(l, 64))
                    for d in range(2):
                        tr(ps[7][:, 128 * d:128 * d + 128], s0in[:, d, :], ident).then_inc(s0_ps(), 1)
                    for g, group in enumerate(GROUPS):
                        base = pair_index(ht, g, 0)
                        A_, R_, K_, B_ = 0, 2, 4, 6
                        for n, (p, d, t) in enumerate(group):
                            if g > 0:
                                e.wait_ge(st_sb.sem, st_sb.upto(l, nchain[0]))
                                e.wait_ge(y_sb.sem, y_sb.upto(l, base))
                            c = slice(128 * t, 128 * t + 128)
                            b0 = ps[2 * p]
                            tr(b0[:, 0:128], h[:, A_ + d, c], ident)
                            tr(b0[:, 128:256], h[:, K_ + d, c], ident)
                            tr(b0[:, 256:384], h[:, B_ + d, c], ident)
                            tr(b0[:, 384:512], ush[:, 4 + ht, c], ident).then_inc(tok_ps(), 1)
                        for hd in range(2):
                            hs = slice(64 * hd, 64 * hd + 64)
                            for n, (p, d, t) in enumerate(group):
                                c = slice(128 * t, 128 * t + 128)
                                bank = ps[2 * p + 1] if hd == 0 else ps[2 * p]
                                if hd == 0 and g == 0 and p == 3:
                                    e.wait_ge(s0_sb.sem, s0_sb.upto(l, 2 * ht + 2))
                                if hd == 1:
                                    e.wait_ge(tok_sb.sem, tok_sb.upto(l, base + n + 1))
                                ar = h[hs, d:d + 3:2, c]
                                mm(bank[:, 0:256], h[hs, K_ + d, c], ar, start=True, stop=True)
                                mm(bank[:, 256:512], h[hs, B_ + d, c], ar, start=True, stop=True).then_inc(
                                    prod_ps(), 1)

                        def flip(level, n, p):
                            b = ps[2 * p + 1]
                            for hd in range(2):
                                last = tr(b[:, 256 + 128 * hd:384 + 128 * hd], Yi[p][:, hd, :], ident)
                            last.then_inc(xt_ps(), 1)

                        gb = 5 * base
                        ng = len(group)
                        for n, (p, d, t) in enumerate(group):
                            e.wait_ge(inv0_sb.sem, inv0_sb.upto(l, base + n + 1))
                            flip(0, n, p)
                        for lv in range(1, 6):
                            at = gb + (lv - 1) * ng
                            for n, (p, d, t) in enumerate(group):
                                e.wait_ge(xt_sb.sem, xt_sb.upto(l, at + n + 1))
                                for hd in range(2):
                                    last = mm(ps[2 * p][:, 128 * hd:128 * hd + 128], LP[p][:, hd, 256:384],
                                              Xi[p][:, hd, :], start=True, stop=True)
                                last.then_inc(p1_ps(), 1)
                            for n, (p, d, t) in enumerate(group):
                                e.wait_ge(p1_sb.sem, p1_sb.upto(l, at + n + 1))
                                for hd in range(2):
                                    last = mm(ps[2 * p + 1][:, 128 * hd:128 * hd + 128], P1[p][:, hd, :],
                                              Yi[p][:, hd, :], start=True, stop=True)
                                last.then_inc(yu_ps(), 1)
                            if lv < 5:
                                for n, (p, d, t) in enumerate(group):
                                    e.wait_ge(yu_sb.sem, yu_sb.upto(l, at + n + 1))
                                    flip(lv, n, p)
                        for n, (p, d, t) in enumerate(group):
                            for hd in range(2):
                                last = mm(ps[2 * p][:, 64 * hd:64 * hd + 64], LP[p][:, hd, 0:128],
                                          TOK[p][:, 2, 64 * hd:64 * hd + 64], start=True, stop=True)
                            last.then_inc(w1_ps(), 1)
                        for n, (p, d, t) in enumerate(group):
                            e.wait_ge(yu_sb.sem, yu_sb.upto(l, gb + 4 * ng + n + 1))
                            e.wait_ge(w1_sb.sem, w1_sb.upto(l, base + n + 1))
                            for hd in range(2):
                                last = mm(ps[2 * p + 1][:, 256 + 128 * hd:384 + 128 * hd], Yi[p][:, hd, :],
                                          W1A[p][:, hd, :], start=True, stop=True)
                            last.then_inc(ug_ps(), 1)
                        for n, (p, d, t) in enumerate(group):
                            e.wait_ge(ug_sb.sem, ug_sb.upto(l, base + n + 1))
                            b0 = ps[2 * p]
                            for hd in range(2):
                                o = slice(64 * hd, 64 * hd + 64)
                                mm(b0[o, 0:128], UG[p][:, hd, 64:128], LP[p][:, hd, 384:512], start=True, stop=True)
                                for hf in range(2):
                                    r = slice(64 * hf, 64 * hf + 64)
                                    bh = ps[2 * p + hf]
                                    mm(bh[o, 128:192], UG[p][r, hd, 64:128], TOK[p][r, 1, o], start=True, stop=True)
                                    mm(bh[o, 256:320], TOK[p][r, 0, o], TOK[p][r, 2, o], start=True, stop=False)
                                    last = mm(bh[o, 256:320], TOK[p][r, 1, o], UG[p][r, hd, 0:64],
                                              start=False, stop=True)
                            last.then_inc(qmn_ps(), 1)
                        for n, (p, d, t) in enumerate(group):
                            b1 = ps[2 * p + 1]
                            e.wait_ge(qmn_sb.sem, qmn_sb.upto(l, base + n + 1))
                            for hd in range(2):
                                o = slice(64 * hd, 64 * hd + 64)
                                mm(b1[o, 0:128], TOK[p][:, 2, o], LP[p][:, hd, 128:256], start=True, stop=False,
                                   skip_group_check=True)
                                mm(b1[o, 0:128], UG[p][:, hd, 0:64], LP[p][:, hd, 384:512], start=False, stop=False,
                                   skip_group_check=True)
                        seen = {}
                        for (p, d, t, hf, ck) in chain_steps(group):
                            n = [q[0] for q in group].index(p)
                            e.wait_ge(qmn_sb.sem, qmn_sb.upto(l, base + n + 1))
                            slot, need = PLAN[(ht, g, d, ck)]
                            if need is None and g == 2:
                                e.wait_ge(ctx_zero.sem, ctx_zero.upto(l, ht + 1))
                            elif need is None:
                                e.wait_ge(s0_sb.sem, s0_sb.upto(l, 2 * ht + d + 1))
                            else:
                                e.wait_ge(st_sb.sem, st_sb.upto(l, need))
                            S = St[:, d, slot, :]
                            last = mm(ps[2 * p + 1][:, 64 * hf:64 * hf + 64], S, Qt[p][:, 64 * hf:64 * hf + 64],
                                      start=False, stop=True, skip_group_check=True)
                            seen[p] = seen.get(p, 0) + 1
                            if seen[p] == 2:
                                last.then_inc(y_ps(), 1)
                            if needs_state(ck, d):
                                mm(ps[2 * p][:, 384:512], MN[:, p, 0, hf, :], S, start=True, stop=True).then_inc(
                                    st_ps(), 1)
                                nchain[0] += 1
                    e.wait_ge(st_sb.sem, st_sb.upto(l, nchain[0]))
                    e.wait_ge(y_sb.sem, y_sb.upto(l, pair_index(ht, 2, 2)))
                    for d in range(2):
                        last = tr(ps[6][:, 128 * d:128 * d + 128], St[:, d, 0, :], ident)
                    last.then_inc(fin_ps(), 1)
                    e.wait_ge(fin_sb.sem, fin_sb.upto(l, ht + 1))

                recurrence(0, ITEM_AT[("w", 1, 0)], 16)
                prep(1)
                attention(ATT_B, 16)
                recurrence(1, ITEM_AT[("mean", 0)], 40)

                for t in range(2):
                    lat, cx = begin(("mean", t))
                    both(lat, cx, mean64, 0, 1, ush[:, 2 + t, :]).then_inc(acc_ready(), 1)
                for t in range(2):
                    lat, cx = begin(("var", t))
                    e.wait_ge(ysq_ready.sem, ysq_ready.upto(l, t + 1))
                    both(lat, cx, mean64, 0, 1, e01[:, t, :]).then_inc(acc_ready(), 1)
                for t in range(2):
                    lat, cx = begin(("g", t))
                    both(lat, cx, lora[:, 2, 128 * t:128 * t + 128], 0, 1, ush[:, 6, :]).then_inc(acc_ready(), 1)

                taken(e, l, ("ft2", 0))
                taken(e, l, ("ft2", 1))
                for b in (3, 4):
                    taken(e, l, ("oT", b))
                src_of = {0: qt[:, 0, :], 1: qt[:, 1, :], 2: qt[:, 2, :], 3: qt[:, 3, :],
                          4: ush[:, 2, :], 5: ush[:, 3, :], 6: uf[:, 0, :], 7: uf[:, 1, :]}
                for m in range(KT):
                    w = cols(("wo", m // 2), m % 2)
                    lat, cx = begin(("out", m))
                    for n, k in enumerate((0, 1, 2, 3, 6, 7, 4, 5)):
                        if m == 0 and k in (4, 5):
                            taken(e, l, ("g", k - 4))
                        last = both(lat, cx, w[k], n, KT, src_of[k])
                    last.then_inc(acc_ready(), 1)
                norm(1)
                def unit(u, order, total, first=0):
                    name, ck, g, nk = UNITS[u]
                    if first == 0:
                        begin(name)
                        e.wait_ge(wl_ready.sem, wl_ready.upto(l, u + 1))
                    i, lat, cx = acc_item(name)
                    hi, lo = (h_hi, h_lo) if nk == KT else (hid_hi, hid_lo)
                    for n, (k, p) in enumerate(order, first):
                        if u == 0 and p == 0:
                            e.wait_ge(h_ready.sem, h_ready.upto(l, KT + k + 1))
                        if u == 0 and p == 2:
                            e.wait_ge(hl_ready.sem, hl_ready.upto(l, k + 1))
                        if name[:2] == ("f2", 0) and p == 0:
                            e.wait_ge(hid_split.sem, hid_split.upto(l, FH * name[2] + k + 1))
                        w = wsplit[:, u % 2, 1 if p == 1 else 0, 128 * k:128 * k + 128]
                        v = (lo if p == 2 else hi)[:, k, :]
                        mm(lat[:, 0:TH], w, v[:, 0:TH], start=(n == 0), stop=(n == total - 1))
                        last = mm(cx[:, 0:TH], w, v[:, TH:T], start=(n == 0), stop=(n == total - 1))
                    if first + len(order) == total:
                        last.then_inc(acc_ready(), 1)

                on_high = [(k, p) for k in range(KT) for p in (0, 1)]
                on_low = [(k, 2) for k in range(KT)]
                unit(0, on_high, 3 * KT)
                unit(1, on_high, 3 * KT)
                unit(0, on_low, 3 * KT, len(on_high))
                unit(1, on_low, 3 * KT, len(on_high))
                for u in range(2, NUNIT):
                    nk = UNITS[u][3]
                    unit(u, [(k, p) for k in range(nk) for p in range(3)], 3 * nk)

            lat, cx = ps[0], ps[2]
            layer_before(e, DEPTH)
            for k in range(KT):
                e.wait_ge(sq_ready.sem, sq_ready.upto(DEPTH, k + 1))
                mm(lat[:, :], onesD, S2[:, k % 2, 0:NL], start=(k == 0), stop=(k == KT - 1))
                mm(cx[:, 0:NC_], onesD, S2[:, k % 2, NL:T], start=(k == 0), stop=(k == KT - 1)).then_inc(
                    sq_used.sem if k < KT - 1 else acc_ready.sem, 1)
            e.wait_ge(h_scaled.sem, h_scaled.upto(DEPTH, KT))
            for t in range(5):
                for g in range(2):
                    n = 2 * t + g
                    if n >= 4:
                        e.wait_ge(yT_sb, n // 2 - 1)
                    for k in range(4):
                        last = tr(ps[4 + n % 4][:, 128 * k:128 * k + 128],
                                  h[:, 4 * g + k, 128 * t:128 * t + 128], ident)
                last.then_inc(yT_ps, 1)

        @block.scalar
        def _(e):
            
            act = nc.scalar.activation
            e.wait_ge(mn_zero, 5)
            e.wait_ge(xT_ps, 1)
            act(cvec[:, :], ps[6][:, 0:24], ACT.Copy).then_inc(c_ready, 1)
            e.wait_ge(c_ready, 1)
            act(csil_s[:, :], cvec[:, 0:16], ACT.Sigmoid).then_inc(c_ready, 1)
            for n in range(10):
                t, g = n // 2, n % 2
                e.wait_ge(xT_ps, n + 2)
                c = slice(128 * t, 128 * t + 128)
                act(x[:, 4 * g:4 * g + 4, c], ps[4 + n % 2][:, :].rearrange("p (k t) -> p k t", k=4),
                    ACT.Copy).then_inc(xT_sb, 1)

            def norm_square(l, which):
                for k in range(KT):
                    if which == 1:
                        taken(e, l, ("out", k))
                    if k >= 2:
                        e.wait_ge(sq_used.sem, sq_used.upto(l, which * (KT - 1) + k - 1))
                    act(S2[:, k % 2, :], x[:, k, :], ACT.Square).then_inc(sq_ready(), 1)

            def norm_root(l, which):
                i, lat, cx = acc_item(("norm", which))
                e.wait_ge(acc_ready.sem, acc_ready.upto(l, i + 1))
                act(rot[:, 0:NL], lat[:, :], ACT.Sqrt, bias=eps[:, 0:1])
                act(rot[:, NL:T], cx[:, 0:NC_], ACT.Sqrt, bias=eps[:, 0:1]).then_inc(acc_free[i % 2](), 1)

            def norm_shift(l, which):
                dst = h_hi if which else h
                for k in range(KT):
                    e.wait_ge(h_scaled.sem, h_scaled.upto(l, which * KT + k + 1))
                    for s, (a, b) in enumerate(STREAMS):
                        last = act(dst[:, k, a:b], h[:, k, a:b], ACT.Identity,
                                   bias=mod[:, 24 * which + k, s:s + 1])
                    last.then_inc(h_ready(), 1)

            e.wait_ge(xT_sb, 10)
            with e.Fori(0, DEPTH) as l:

                def ready(name):
                    i, lat, cx = acc_item(name)
                    e.wait_ge(acc_ready.sem, acc_ready.upto(l, i + 1))
                    return acc_free[i % 2], lat, cx

                layer_before(e, l)
                norm_square(l, 0)
                norm_root(l, 0)
                free, lat, cx = ready(("small", 0))
                act(par[:, :], lat[:, 0:NPR], ACT.Copy).then_inc(free(), 1)
                taken(e, l, ("small", 0))
                act(omka[:, :], par[:, PR_KA:PR_KA + 2], ACT.Copy, scale=-1.0, bias=1.0).then_inc(par_ready(), 1)
                norm_shift(l, 0)
                e.wait_ge(pads_zero.sem, pads_zero.upto(l, 1))

                def ada_rows(j):
                    e.wait_ge(ada_done.sem, ada_done.upto(l, 2 * j + 2))
                    e.wait_ge(mcol_ps.sem, mcol_ps.upto(l, j))
                    act(mrow, ps[6 + j % 2][0:2, :], ACT.Copy).then_inc(mrow_sb(), 1)

                for m in range(9):
                    free, lat, cx = ready(("rw", m))
                    if m >= 2:
                        e.wait_ge(conv_out.sem, conv_out.upto(l, m - 1))
                    act(raw[:, m % 2, 1:513], lat[:, :], ACT.Copy)
                    act(raw[:, m % 2, 514:642], cx[:, 0:NC_], ACT.Copy)
                    w1 = par[:, PR_SHIFT + 9 + m:PR_SHIFT + 10 + m]
                    act(ush[:, m, 0:NL], lat[:, :], ACT.Copy, scale=w1)
                    act(ush[:, m, NL:T], cx[:, 0:NC_], ACT.Copy, scale=w1).then_inc(free(), 1)
                    if m % 2 == 1 or m == 8:
                        ada_rows(4 + m // 2)
                for r, name in enumerate((("q", 0), ("q", 1), ("q", 2), ("q", 3), ("k", 0))):
                    free, lat, cx = ready(name)
                    sc = 0.125 if r < 4 else 1.0
                    dst = qt[:, r, NL:T] if r < 4 else kt[:, NL:T]
                    if r < 2:
                        e.wait_ge(conv_out.sem, conv_out.upto(l, 9))
                    else:
                        e.wait_ge(rot_cos.sem, rot_cos.upto(l, r - 1))
                        e.wait_ge(acc_ready.sem, acc_ready.upto(l, ITEM_AT[("swap", r - 2)] + 1))
                    act(raw[:, r % 2, 0:NL], lat[:, :], ACT.Copy, scale=sc).then_inc(rot_raw(), 1)
                    act(dst, cx[:, 0:NC_], ACT.Copy, scale=sc).then_inc(free(), 1)
                    if r in (1, 3):
                        ada_rows(9 + r // 2)
                free, lat, cx = ready(("v", 0))
                act(KK[:, 0:NL], lat[:, :], ACT.Copy)
                act(KK[:, NL:T], cx[:, 0:NC_], ACT.Copy).then_inc(free(), 1)
                ada_rows(11)

                def fcopy(f):
                    free, lat, cx = ready(("fn", f))
                    act(uf[:, f, 0:NL], lat[:, :], ACT.Copy)
                    act(uf[:, f, NL:T], cx[:, 0:NC_], ACT.Copy).then_inc(free(), 1)

                fcopy(0)
                free, lat, cx = ready(("kvT", 0))
                act(vtok[:, 0:NL], lat[:, :], ACT.Copy)
                act(vtok[:, NL:T], cx[:, 0:128], ACT.Copy)
                act(kcT[:, :], cx[:, 256:384], ACT.Copy)
                act(kvout[:, :], cx[:, 128:256], ACT.Copy).then_inc(free(), 1)
                e.wait_ge(conv_out.sem, conv_out.upto(l, 9))
                act(ush[:, 6, :], ush[:, 6, :], ACT.Sigmoid)
                act(ush[:, 7, :], ush[:, 7, :], ACT.Tanh).then_inc(lora_in(), 1)
                fcopy(1)

                def prep(t):
                    for kind, slot0 in (("w", None), ("a", 6)):
                        for d in range(2):
                            free, lat, cx = ready((kind, t, d))
                            bias = par[:, (PR_W0 if kind == "w" else PR_A0) + 2 * d + t:
                                       (PR_W0 if kind == "w" else PR_A0) + 2 * d + t + 1]
                            dst = S2[:, d, :] if kind == "w" else h[:, 6 + d, :]
                            act(dst[:, 0:NL], lat[:, :], ACT.Sigmoid, bias=bias)
                            act(dst[:, NL:T], cx[:, 0:NC_], ACT.Sigmoid, bias=bias).then_inc(free(), 1)
                    e.wait_ge(kk_raw.sem, kk_raw.upto(l, t + 1))
                    act(e01[:, 0, :], KK, ACT.Square).then_inc(kk_sq(), 1)
                    free, lat, cx = ready(("kk", t))
                    act(e01[:, 0, 0:NL], lat[:, :], ACT.Sqrt, bias=eps[:, 1:2])
                    act(e01[:, 0, NL:T], cx[:, 0:NC_], ACT.Sqrt, bias=eps[:, 1:2]).then_inc(free(), 1)
                    free, lat, cx = ready(("bonus", t))
                    act(e01[:, 1, 0:NL], lat[:, :], ACT.Copy)
                    act(e01[:, 1, NL:T], cx[:, 0:NC_], ACT.Copy).then_inc(free(), 1)
                    e.wait_ge(cum_ready.sem, cum_ready.upto(l, t + 1))
                    act(h[:, 2:4, :], CC, ACT.Exp, scale=-DECAY)
                    act(h[:, 4:6, :], CC, ACT.Exp, scale=DECAY)
                    act(h[:, 0:2, :], S2, ACT.Exp, scale=-DECAY)
                    act(emid[:, :, :], mid[:, :, :], ACT.Exp, scale=-DECAY)
                    act(eend[:, :, :], end[:, :, :], ACT.Exp, scale=-DECAY).then_inc(exps_ready(), 1)

                prep(0)
                for t in range(5):
                    free, lat, cx = ready(("ft1", t))
                    act(Z[:, t, :], lat[:, :], ACT.Copy).then_inc(free(), 1)
                for f in range(2):
                    free, lat, cx = ready(("ft2", f))
                    act(uf[:, f, 0:NL], lat[:, :], ACT.Copy)
                    act(uf[:, f, NL:T], cx[:, 0:128], ACT.Copy).then_inc(free(), 1)

                def attention(blocks, done):
                    seq = [(b, i) for b in blocks for i in range(8)]

                    def pexp(n):
                        b, i = seq[n]
                        m = done + n
                        w = 128 * len(key_tiles(b))
                        e.wait_ge(p_ready.sem, p_ready.upto(l, m + 1))
                        act(Pm[:, m % 3, 0:w], Pm[:, m % 3, 0:w], ACT.Exp, bias=negm[:, (m // 8) % 2, i:i + 1],
                            accum_out=den[:, (m // 8) % 2, i:i + 1]).then_inc(p_exp(), 1)

                    def ptcopy(n):
                        b, i = seq[n]
                        m = done + n
                        w = 128 * len(key_tiles(b))
                        e.wait_ge(pt_ps.sem, pt_ps.upto(l, m + 1))
                        e.wait_ge(pv_done.sem, pv_done.upto(l, max(m - 1, 0)))
                        act(PT[:, m % 2, 0:w], ps[4 + m % 2][:, 0:w], ACT.Copy).then_inc(pt_sb(), 1)

                    for bi, b in enumerate(blocks):
                        lo = 8 * bi
                        for n in range(lo, lo + 10):
                            if n < lo + 8:
                                pexp(n)
                            if n - 2 >= lo:
                                ptcopy(n - 2)
                        e.wait_ge(esk_in.sem, esk_in.upto(l, b + 1))
                        act(esk[:, b % 2, :], esk[:, b % 2, :], ACT.Exp).then_inc(esk_ready(), 1)
                        free, lat, cx = ready(("oT", b))
                        act(qt[:, :, 128 * b:128 * b + 128], lat[:, :].rearrange("p (j t) -> p j t", j=4),
                            ACT.Copy).then_inc(free(), 1)

                attention(ATT_A, 0)

                def recurrence(ht):
                    for d in range(2):
                        e.wait_ge(s0_ps.sem, s0_ps.upto(l, 2 * ht + 2))
                        ck = 0 if d == 0 else LCH - 1
                        act(St[:, d, 0, :], ps[7][:, 128 * d:128 * d + 128], ACT.Copy,
                            scale=emid[:, d, ck:ck + 1]).then_inc(s0_sb(), 1)
                    for g, group in enumerate(GROUPS):
                        base = pair_index(ht, g, 0)
                        gb = 5 * base
                        ng = len(group)
                        for n, (p, d, t) in enumerate(group):
                            e.wait_ge(tok_ps.sem, tok_ps.upto(l, base + n + 1))
                            act(W1A[p][:, :, 64:128], ps[2 * p][:, 0:128].rearrange("p (a t) -> p a t", a=2), ACT.Copy)
                            act(TOK[p], ps[2 * p][:, 128:512].rearrange("p (a t) -> p a t", a=3),
                                ACT.Copy).then_inc(tok_sb(), 1)
                        for lv in range(5):
                            for n, (p, d, t) in enumerate(group):
                                e.wait_ge(xt_ps.sem, xt_ps.upto(l, gb + lv * ng + n + 1))
                                act(Xi[p], ps[2 * p + 1][:, 256:512].rearrange("p (a t) -> p a t", a=2),
                                    ACT.Copy).then_inc(xt_sb(), 1)
                        for n, (p, d, t) in enumerate(group):
                            e.wait_ge(w1_ps.sem, w1_ps.upto(l, base + n + 1))
                            act(W1A[p][:, :, 0:64], ps[2 * p][:, 0:128].rearrange("p (a t) -> p a t", a=2),
                                ACT.Copy).then_inc(w1_sb(), 1)
                        for n, (p, d, t) in enumerate(group):
                            e.wait_ge(ug_ps.sem, ug_ps.upto(l, base + n + 1))
                            act(UG[p], ps[2 * p + 1][:, 256:512].rearrange("p (a t) -> p a t", a=2),
                                ACT.Copy).then_inc(ug_sb(), 1)
                    e.wait_ge(fin_ps.sem, fin_ps.upto(l, ht + 1))
                    if ht == 1:
                        e.wait_ge(fin_st.sem, fin_st.upto(l, 64))
                    act(stout, ps[6][:, 0:256].rearrange("p (a t) -> p a t", a=2), ACT.Copy).then_inc(fin_sb(), 1)

                recurrence(0)
                prep(1)
                attention(ATT_B, 16)
                recurrence(1)

                for t in range(2):
                    taken(e, l, ("mean", t))
                    act(e01[:, t, :], ush[:, 2 + t, :], ACT.Square).then_inc(ysq_ready(), 1)
                for t in range(2):
                    free, lat, cx = ready(("var", t))
                    act(e01[:, t, 0:NL], lat[:, :], ACT.Sqrt, bias=eps[:, 2:3])
                    act(e01[:, t, NL:T], cx[:, 0:NC_], ACT.Sqrt, bias=eps[:, 2:3]).then_inc(free(), 1)
                norm_square(l, 1)
                e.wait_ge(fin_st.sem, fin_st.upto(l, 128))
                norm_root(l, 1)

                def weight_high(u):
                    if u >= 2:
                        e.wait_ge(acc_ready.sem, acc_ready.upto(l, ITEM_AT[UNITS[u - 2][0]] + 1))
                    n, raw_w, hi, lo = unit_weights(u)
                    e.wait_ge(w_ready[n % SLOTS].sem, w_ready[n % SLOTS].upto(l, READY[n]))
                    act(hi, raw_w, ACT.Copy).then_inc(wh_ready(), 1)

                weight_high(0)
                weight_high(1)
                e.wait_ge(kv_stored.sem, kv_stored.upto(l, 32))
                norm_shift(l, 1)
                for u in range(2, NUNIT + 2):
                    if u < NUNIT:
                        weight_high(u)
                    name = UNITS[u - 2][0]
                    if name[0] == "gate":
                        i = name[1]
                        i_, lat, cx = acc_item(name)
                        e.wait_ge(acc_ready.sem, acc_ready.upto(l, i_ + 1))
                        if i > 0:
                            e.wait_ge(hid_split.sem, hid_split.upto(l, i))
                        act(tmp[:, 0:TH], lat[:, 0:TH], ACT.Sigmoid)
                        act(tmp[:, TH:T], cx[:, 0:TH], ACT.Sigmoid).then_inc(hid_sig(), 1)

            layer_before(e, DEPTH)
            for k in range(KT):
                if k >= 2:
                    e.wait_ge(sq_used.sem, sq_used.upto(DEPTH, k - 1))
                act(S2[:, k % 2, :], x[:, k, :], ACT.Square).then_inc(sq_ready.sem, 1)
            e.wait_ge(acc_ready.sem, acc_ready.upto(DEPTH, 1))
            act(rot[:, 0:NL], ps[0][:, :], ACT.Sqrt, bias=eps[:, 0:1])
            act(rot[:, NL:T], ps[2][:, 0:NC_], ACT.Sqrt, bias=eps[:, 0:1]).then_inc(acc_free[0].sem, 1)
            for t in range(5):
                e.wait_ge(yT_ps, t + 1)
                if t >= 2:
                    e.wait_ge(y_stored[t % 2], 16 * (t // 2))
                for g in range(2):
                    n = 2 * t + g
                    last = act(yout[:, t % 2, 512 * g:512 * g + 512], ps[4 + n % 4][:, :], ACT.Copy)
                last.then_inc(yT_sb, 1)

        @block.vector
        def _(e):
            own = Own(e, dve_own, DVE_CHAIN)
            V = nc.vector
            for s in signals.values():
                if s.primed:
                    e.sem_inc(s.sem, s.primed)
            e.wait_ge(c_ready, 2)
            V.tensor_tensor(csil[:, :, :].rearrange("p k s -> p s k"), cvec[:, 0:16].rearrange("p (s k) -> p s k", s=2),
                            csil_s.rearrange("p (s k) -> p s k", s=2), MUL).then_inc(c_ready, 1)

            e.wait_ge(ld_tab, 64)

            def gains(l, which):
                g = par[:, (PR_NMIX, PR_NFFN)[which]:(PR_NMIX, PR_NFFN)[which] + 8].unsqueeze(2).to_broadcast([128, 8, 2])
                V.scalar_tensor_tensor(gain[:, which, :, :], mod[:, 24 * which + 8:24 * which + 16, :], 1.0, g,
                                       ADD, MUL).then_inc(gain_ready(), 1)
                e.wait_ge(gain_ready.sem, gain_ready.upto(l, which + 1))

            def norm_scale(l, which, n, per_stream):
                taken(e, l, ("norm", which))
                own.after(V.reciprocal(rot, rot))
                for k in range(KT):
                    for s, (a, b) in enumerate(STREAMS):
                        last = V.scalar_tensor_tensor(h[:, k, a:b], x[:, k, a:b], gain[:, n, k, s:s + 1], rot[:, a:b],
                                                      MUL, MUL)
                    last.then_inc(h_scaled() if per_stream else h_scaled.sem, 1)
                if which == 1:
                    for k in range(KT):
                        low_part(l, k)

            def low_part(l, k):
                e.wait_ge(h_ready.sem, h_ready.upto(l, KT + k + 1))
                for s, (a, b) in enumerate(STREAMS):
                    last = V.scalar_tensor_tensor(h_lo[:, k, a:b], h[:, k, a:b], mod[:, 24 + k, s:s + 1],
                                                  h_hi[:, k, a:b], ADD, SUB)
                last.then_inc(hl_ready(), 1)

            e.wait_ge(xT_sb, 10)
            with e.Fori(0, DEPTH) as l:
                own.l, own.n = l, 0

                def ready(name):
                    i, lat, cx = acc_item(name)
                    e.wait_ge(acc_ready.sem, acc_ready.upto(l, i + 1))
                    return acc_free[i % 2], lat, cx

                layer_before(e, l)
                for j in range(4):
                    e.wait_ge(ada_done.sem, ada_done.upto(l, 2 * j + 2))
                    if j >= 1:
                        e.wait_ge(mcol_ps.sem, mcol_ps.upto(l, j))
                    V.tensor_copy(mrow, ps[6 + j % 2][0:2, :]).then_inc(mrow_sb(), 1)
                e.wait_ge(par_ready.sem, par_ready.upto(l, 1))
                e.wait_ge(mcol_ps.sem, mcol_ps.upto(l, 4))
                own.after(V.tensor_tensor(mod[:, 0:16, :], ps[4][:, 0:32].rearrange("p (m s) -> p m s", s=2),
                                          par[:, PR_ADA:PR_ADA + 16].unsqueeze(2).to_broadcast([128, 16, 2]), ADD))
                gains(l, 0)
                norm_scale(l, 0, 0, True)
                for m in range(9):
                    taken(e, l, ("rw", m))
                    wl = par[:, PR_SHIFT + m:PR_SHIFT + m + 1]
                    wr = par[:, PR_SHIFT + 18 + m:PR_SHIFT + 19 + m]
                    r_ = raw[:, m % 2, :]
                    V.scalar_tensor_tensor(ush[:, m, 0:NL], r_[:, 0:512], wl, ush[:, m, 0:NL], MUL, ADD)
                    own.after(V.scalar_tensor_tensor(ush[:, m, NL:T], r_[:, 513:641], wl, ush[:, m, NL:T], MUL, ADD))
                    V.scalar_tensor_tensor(ush[:, m, 0:NL], r_[:, 2:514], wr, ush[:, m, 0:NL], MUL, ADD)
                    V.scalar_tensor_tensor(ush[:, m, NL:T], r_[:, 515:643], wr, ush[:, m, NL:T], MUL,
                                           ADD).then_inc(conv_out(), 1)
                e.wait_ge(ld_rope.sem, ld_rope.upto(l, 16))
                for r in range(5):
                    free, lat, cx = ready(("swap", r))
                    dst = qt[:, r, 0:NL] if r < 4 else kt[:, 0:NL]
                    e.wait_ge(rot_done.sem, rot_done.upto(l, r))
                    V.tensor_tensor(rot[:, 0:NL], lat[:, :], rope[:, 1, :], MUL).then_inc(free(), 1)
                    taken(e, l, ("swap", r))
                    e.wait_ge(rot_cos.sem, rot_cos.upto(l, r + 1))
                    V.tensor_tensor(dst, dst, rot[:, 0:NL], ADD).then_inc(rot_done(), 1)
                e.wait_ge(mcol_ps.sem, mcol_ps.upto(l, 12))
                own.after(V.tensor_tensor(mod[:, 16:48, :], ps[5][:, 32:96].rearrange("p (m s) -> p m s", s=2),
                                          par[:, PR_ADA + 16:PR_ADA + 48].unsqueeze(2).to_broadcast([128, 32, 2]), ADD))
                gains(l, 1)

                def chunks(v):
                    return v.rearrange("p a (c t) -> p (a c) t", t=CH)

                def prep(t):
                    kb = KK.unsqueeze(1).to_broadcast([128, 2, T])
                    taken(e, l, ("w", t, 0))
                    taken(e, l, ("w", t, 1))
                    V.tensor_tensor_scan(CC[:, 0, :], reset[:, :], S2[:, 0, :], 0.0, MUL, ADD)
                    own.after(V.tensor_tensor_scan(CC[:, 1, :], reset[:, :], S2[:, 1, :], 0.0, MUL, ADD))
                    c0 = CC[:, 0, :].rearrange("p (c t) -> p c t", t=CH)
                    c1 = CC[:, 1, :].rearrange("p (c t) -> p c t", t=CH)
                    V.tensor_copy(end[:, 0, :].unsqueeze(2), c0[:, :, 63:64])
                    V.tensor_copy(mid[:, 0, :].unsqueeze(2), c0[:, :, 31:32])
                    own.after(V.tensor_copy(end[:, 1, :].unsqueeze(2), c1[:, :, 63:64]))
                    own.after(V.tensor_tensor(CC[:, 1, :], S2[:, 1, :], CC[:, 1, :], SUB))
                    own.after(V.tensor_tensor(c1, c1, end[:, 1, :].unsqueeze(2).to_broadcast([128, NCH, CH]), ADD))
                    own.after(V.tensor_copy(mid[:, 1, :].unsqueeze(2), c1[:, :, 32:33]))
                    own.after(V.tensor_tensor(chunks(CC), chunks(CC),
                                              mid[:, :, :].rearrange("p a c -> p (a c)").unsqueeze(2).to_broadcast(
                                                  [128, 2 * NCH, CH]), SUB))
                    own.after(V.tensor_tensor(end[:, :, :], end[:, :, :], mid[:, :, :], SUB))
                    V.tensor_tensor(S2, CC, S2, SUB).then_inc(cum_ready(), 1)
                    taken(e, l, ("kk", t))
                    own.after(V.reciprocal(e01[:, 0, :], e01[:, 0, :]))
                    V.tensor_tensor(KK, KK, e01[:, 0, :], MUL).then_inc(kk_ready(), 1)
                    e.wait_ge(kk_ready.sem, kk_ready.upto(l, t + 1))
                    e.wait_ge(exps_ready.sem, exps_ready.upto(l, t + 1))
                    n = NCH
                    V.tensor_tensor(dec[:, 0, 0:n - 1], eend[:, 0, 0:n - 1], emid[:, 0, 1:n], MUL)
                    V.tensor_copy(dec[:, 0, n - 1:n], eend[:, 0, n - 1:n])
                    V.tensor_copy(dec[:, 1, 0:1], eend[:, 1, 0:1])
                    own.after(V.tensor_tensor(dec[:, 1, 1:n], eend[:, 1, 1:n], emid[:, 1, 0:n - 1], MUL))
                    V.tensor_copy(dec[:, 1, LCH:LCH + 1], eend[:, 1, LCH:LCH + 1])
                    own.after(V.tensor_scalar(CC, h[:, 6:8, :], par[:, PR_KA + t:PR_KA + t + 1], omka[:, t:t + 1],
                                              MUL, ADD))
                    own.after(V.tensor_tensor(CC, CC, ush[:, 2 + t:3 + t, :].to_broadcast([128, 2, T]), MUL))
                    own.after(V.tensor_tensor(h[:, 6:8, :], h[:, 6:8, :], h[:, 4:6, :], MUL))
                    V.tensor_tensor(h[:, 4:6, :], h[:, 4:6, :], CC, MUL)
                    own.after(V.scalar_tensor_tensor(h[:, 6:8, :], h[:, 6:8, :], -1.0, kb, MUL, MUL))
                    e.wait_ge(ar_done.sem, ar_done.upto(l, t + 1))
                    taken(e, l, ("bonus", t))
                    V.tensor_tensor(ush[:, t, :], e01[:, 1, :], ush[:, 4 + t, :], MUL).then_inc(scaled_ready(), 1)
                    e.wait_ge(scaled_ready.sem, scaled_ready.upto(l, t + 1))

                prep(0)

                def attention(blocks, done):
                    seq = [(b, i) for b in blocks for i in range(8)]

                    def softmax_in(n):
                        b, i = seq[n]
                        m = done + n
                        w = 128 * len(key_tiles(b))
                        c0, c1 = mask_cols(b)
                        free, lat, cx = ready(("s", b, i))
                        e.wait_ge(pt_ps.sem, pt_ps.upto(l, max(m - 2, 0)))
                        V.tensor_tensor(Pm[:, m % 3, 0:w], lat[:, 0:w], attmask[:, c0:c1], ADD).then_inc(free(), 1)
                        taken(e, l, ("s", b, i))
                        mx = negm[:, b % 2, i:i + 1]
                        own.after(V.tensor_reduce(mx, Pm[:, m % 3, 0:w], AX.X, MAX))
                        V.tensor_scalar(mx, mx, sink[:, i:i + 1], -1.0, MAX, MUL).then_inc(p_ready(), 1)

                    for bi, b in enumerate(blocks):
                        lo = 8 * bi
                        for n in range(lo, lo + 8):
                            softmax_in(n)
                        e.wait_ge(p_ready.sem, p_ready.upto(l, done + lo + 8))
                        V.tensor_tensor(esk[:, b % 2, :], negm[:, b % 2, :], sink[:, :], ADD).then_inc(esk_in(), 1)
                        e.wait_ge(esk_ready.sem, esk_ready.upto(l, b + 1))
                        own.after(V.tensor_tensor(den[:, b % 2, :], den[:, b % 2, :], esk[:, b % 2, :], ADD))
                        own.after(V.reciprocal(den[:, b % 2, :], den[:, b % 2, :]))
                        e.wait_ge(pv_done.sem, pv_done.upto(l, done + lo + 8))
                        o_ps = ps[6 + b % 2][:, :].rearrange("p (j g c) -> p g j c", j=4, g=2)
                        o_sb = otok[:, b % 2, :].rearrange("p (j g c) -> p g j c", j=4, g=2)
                        for g in range(2):
                            last = V.tensor_tensor(o_sb[:, g, :, :], o_ps[:, g, :, :],
                                                   den[:, b % 2, 4 * g:4 * g + 4].unsqueeze(2).to_broadcast([128, 4, 64]),
                                                   MUL)
                        last.then_inc(o_ready(), 1)

                attention(ATT_A, 0)

                nchain = [0]

                def recurrence(ht):
                    for g, group in enumerate(GROUPS):
                        base = pair_index(ht, g, 0)
                        gb = 5 * base
                        ng = len(group)
                        for hd in range(2):
                            for n, (p, d, t) in enumerate(group):
                                bank = ps[2 * p + 1] if hd == 0 else ps[2 * p]
                                e.wait_ge(prod_ps.sem, prod_ps.upto(l, 2 * base + hd * ng + n + 1))
                                V.tensor_tensor(LP[p][:, hd, :].rearrange("p (a t) -> p a t", a=2),
                                                bank[:, :].rearrange("p (a t) -> p a t", a=2),
                                                masks[:, d:d + 1, :].to_broadcast([128, 2, 256]), MUL).then_inc(
                                                    prod_sb(), 1)
                        eye = mats[:, 0:1, :].to_broadcast([128, 2, 128])
                        for n, (p, d, t) in enumerate(group):
                            e.wait_ge(prod_sb.sem, prod_sb.upto(l, 2 * base + ng + n + 1))
                            own.after(V.tensor_tensor(Yi[p], LP[p][:, :, 256:384],
                                                      lvl[:, 1 - d, 0:1, :].to_broadcast([128, 2, 128]), MUL))
                            V.tensor_tensor(Yi[p], Yi[p], eye, ADD).then_inc(inv0_sb(), 1)
                        for lv in range(1, 6):
                            at = gb + (lv - 1) * ng
                            for n, (p, d, t) in enumerate(group):
                                e.wait_ge(p1_ps.sem, p1_ps.upto(l, at + n + 1))
                                V.tensor_tensor(P1[p], ps[2 * p][:, 0:256].rearrange("p (a t) -> p a t", a=2),
                                                lvl[:, d, lv:lv + 1, :].to_broadcast([128, 2, 128]), MUL).then_inc(
                                                    p1_sb(), 1)
                            for n, (p, d, t) in enumerate(group):
                                e.wait_ge(yu_ps.sem, yu_ps.upto(l, at + n + 1))
                                if lv == 1:
                                    e.wait_ge(inv0_sb.sem, inv0_sb.upto(l, base + n + 1))
                                else:
                                    e.wait_ge(yu_sb.sem, yu_sb.upto(l, at - ng + n + 1))
                                V.tensor_tensor(Yi[p], Yi[p], ps[2 * p + 1][:, 0:256].rearrange(
                                    "p (a t) -> p a t", a=2), ADD).then_inc(yu_sb(), 1)
                        for n, (p, d, t) in enumerate(group):
                            e.wait_ge(qmn_ps.sem, qmn_ps.upto(l, base + n + 1))
                            b0 = ps[2 * p]
                            c = slice(128 * t, 128 * t + 128)
                            if g == 0 and ht == 0 and n == 0:
                                e.wait_ge(mn_zero, 5)
                            V.tensor_tensor(Qt[p], b0[:, 0:128], h[:, 2 + d, c], ADD)
                            for hd in range(2):
                                o = slice(64 * hd, 64 * hd + 64)
                                V.tensor_tensor(MN[o, p, 0, :, o], PS[o, 2 * p:2 * p + 2, 128:192],
                                                mats[o, 0:1, o].to_broadcast([64, 2, 64]), ADD)
                                last = V.tensor_tensor(MN[o, p, 1, :, o],
                                                       PS[o, 2 * p:2 * p + 2, 256:320],
                                                       dec[o, d, 2 * t:2 * t + 2].unsqueeze(2).to_broadcast([64, 2, 64]),
                                                       MUL)
                            last.then_inc(qmn_sb(), 1)
                        for (p, d, t, hf, ck) in chain_steps(group):
                            if needs_state(ck, d):
                                slot, need = PLAN[(ht, g, d, ck)]
                                e.wait_ge(st_ps.sem, st_ps.upto(l, nchain[0] + 1))
                                e.wait_ge(qmn_sb.sem, qmn_sb.upto(l, base + len(group)))
                                V.scalar_tensor_tensor(St[:, d, 1 - slot, :], ps[2 * p][:, 384:512],
                                                       dec[:, d, ck:ck + 1], MN[:, p, 1, hf, :], MUL,
                                                       ADD).then_inc(st_sb(), 1)
                                nchain[0] += 1
                        for n, (p, d, t) in enumerate(y_order(group)):
                            e.wait_ge(y_ps.sem, y_ps.upto(l, base + n + 1))
                            c = slice(128 * t, 128 * t + 128)
                            yc = ush[:, 2 + ht, c]
                            if first_touch(g, d, t):
                                V.tensor_copy(yc, ps[2 * p + 1][:, 0:128]).then_inc(y_sb(), 1)
                            else:
                                e.wait_ge(y_sb.sem, y_sb.upto(l, base + n))
                                V.tensor_tensor(yc, yc, ps[2 * p + 1][:, 0:128], ADD).then_inc(y_sb(), 1)
                        if g == 1:
                            e.wait_ge(y_ps.sem, y_ps.upto(l, base + len(group)))
                            V.memset(St[:, :, 0, :], 0.0).then_inc(ctx_zero(), 1)

                recurrence(0)
                prep(1)
                attention(ATT_B, 16)
                recurrence(1)

                e.wait_ge(y_sb.sem, y_sb.upto(l, y_sb.per))
                for t in range(2):
                    free, lat, cx = ready(("mean", t))
                    y = ush[:, 2 + t, :]
                    V.tensor_tensor(y[:, 0:NL], y[:, 0:NL], lat[:, :], SUB)
                    V.tensor_tensor(y[:, NL:T], y[:, NL:T], cx[:, 0:NC_], SUB).then_inc(free(), 1)
                for t in range(2):
                    y = ush[:, 2 + t, :]
                    taken(e, l, ("var", t))
                    own.after(V.reciprocal(e01[:, t, :], e01[:, t, :]))
                    own.after(V.tensor_tensor(y, y, e01[:, t, :], MUL))
                    own.after(V.tensor_scalar(y, y, par[:, PR_LNG + t:PR_LNG + t + 1], par[:, PR_LNB + t:PR_LNB + t + 1],
                                              MUL, ADD))
                    own.after(V.tensor_tensor(y, y, ush[:, t, :], ADD))
                    free, lat, cx = ready(("g", t))
                    V.tensor_tensor(y[:, 0:NL], y[:, 0:NL], lat[:, :], MUL)
                    V.tensor_tensor(y[:, NL:T], y[:, NL:T], cx[:, 0:NC_], MUL).then_inc(free(), 1)

                def residual(name, m, gate_at, split):
                    free, lat, cx = ready(name)
                    for a, b, bank, at in ((0, split, lat, 0), (split, NL, cx, 0), (NL, T, cx, NL - split)):
                        if a < b:
                            s = 1 if a == NL else 0
                            last = V.scalar_tensor_tensor(x[:, m, a:b], bank[:, at:at + b - a],
                                                          mod[:, gate_at + m, s:s + 1], x[:, m, a:b], MUL, ADD)
                    last.then_inc(free(), 1)

                for m in range(KT):
                    residual(("out", m), m, 16, NL)
                norm_scale(l, 1, 1, True)
                for hf in range(2):
                    for i in range(FH * hf, FH * hf + FH):
                        gfree, glat, gcx = ready(("gate", i))
                        e.wait_ge(hid_sig.sem, hid_sig.upto(l, i + 1))
                        V.tensor_tensor(tmp[:, 0:TH], tmp[:, 0:TH], glat[:, 0:TH], MUL)
                        V.tensor_tensor(tmp[:, TH:T], tmp[:, TH:T], gcx[:, 0:TH], MUL).then_inc(gfree(), 1)
                        taken(e, l, ("gate", i))
                        free, lat, cx = ready(("up", i))
                        V.tensor_tensor(tmp[:, 0:TH], tmp[:, 0:TH], lat[:, 0:TH], MUL)
                        V.tensor_tensor(tmp[:, TH:T], tmp[:, TH:T], cx[:, 0:TH], MUL).then_inc(free(), 1)
                        taken(e, l, ("up", i))
                        own.after(V.tensor_copy(hid_hi[:, i % FH, :], tmp[:, :]))
                        V.tensor_tensor(hid_lo[:, i % FH, :], tmp[:, :], hid_hi[:, i % FH, :], SUB).then_inc(hid_split(), 1)
                    for m in range(KT):
                        residual(("f2", m, hf), m, 40, TH)

            assert own.most == DVE_CHAIN, own.most
            own.l = DEPTH
            own.n = 0
            own.after(V.tensor_copy(gain[:, 2, :, :], cvec[:, 16:24].unsqueeze(2).to_broadcast([128, 8, 2])))
            norm_scale(DEPTH, 0, 2, False)

        bad = [n for n, s in signals.items() if not s.check(n)]
        assert not bad, bad


INS = ["x_prompt", "x_sample", "cache_k", "cache_v", "state_rwkv", "c", "c_ctx", "w_ada", "b_ada", "norm_mix_g",
       "norm_ffn_g", "w_in", "w_out", "attn_sink", "rwkv_shift_w", "rwkv_w0", "rwkv_w_up", "rwkv_a0", "rwkv_a_up",
       "rwkv_g_up", "rwkv_k_k", "rwkv_k_a", "rwkv_r_k", "rwkv_ln_g", "rwkv_ln_b", "ffn_w_in", "ffn_w_out",
       "norm_final_g"]
OUTS = [("y_p", (1, NC_, D)), ("y_s", (1, NL, D)), ("new_k", (1, DEPTH, NC_, 2, HD)),
        ("new_v", (1, DEPTH, NC_, 2, HD)), ("new_s", (1, DEPTH, 2, 4, HD, HD))]


def tables():
    out = {}
    p = np.arange(128)
    mats = np.zeros((128, 5, 128), np.float32)
    mats[p, 0, p] = 1.0
    mats[p, 1, p ^ 16] = 1.0
    mats[:, 2, :] = 1.0 / D
    same_head = (p[:, None] // HD) == (p[None, :] // HD)
    mats[:, 3, :] = same_head
    mats[:, 4, :] = same_head / float(HD)
    out["t_mats"] = mats
    same = (p[:, None] // CH) == (p[None, :] // CH)
    m = np.zeros((128, 2, 2, 128), np.float32)
    i, t = p[:, None], p[None, :]
    m[:, 0, 0], m[:, 0, 1] = same & (i < t), same & (i <= t)
    m[:, 1, 0], m[:, 1, 1] = same & (i > t), same & (i >= t)
    out["t_masks"] = m.reshape(128, 2, 256)
    lv = np.zeros((128, 2, 6, 128), np.float32)
    for n, size in enumerate(LEVELS):
        pair = (p[:, None] // (2 * size)) == (p[None, :] // (2 * size))
        late, early = (p[:, None] // size) % 2 == 1, (p[None, :] // size) % 2 == 0
        lv[:, 0, n] = pair & late & early
        lv[:, 1, n] = lv[:, 0, n].T
    out["t_lvl"] = lv
    am = np.zeros((128, 4, 128), np.float32)
    am[:, 0] = np.where(t >= i, 0.0, -1e30)
    am[:, 3] = np.where(t <= i, 0.0, -1e30)
    out["t_attmask"] = am.reshape(128, 512)
    j = np.arange(T)
    out["t_reset"] = np.broadcast_to((j % CH != 0).astype(np.float32), (128, T)).copy()
    d = np.arange(HD)
    a = 2 * np.pi * np.outer(d, d) / HD
    ch = np.zeros((128, 2, 128), np.float64)
    for g in range(2):
        o = slice(HD * g, HD * g + HD)
        ch[o, 0, o], ch[o, 1, o] = np.cos(a) / 8.0, np.sin(a) / 8.0
    out["t_chan"] = ch.reshape(128, 256).astype(np.float32)
    for n, name in ((NL, ""), (NC_, "x")):
        q = np.arange(n)
        a = 2 * np.pi * (np.outer(q, q) % n) / n
        for f, fn in (("c", np.cos(a)), ("s", -np.sin(a))):
            tab = (fn / math.sqrt(n)).astype(np.float32)
            out["t_dft" + f + name] = tab.reshape(n // 128, 128, n).transpose(1, 0, 2).copy().reshape(
                (128, n // 128, n) if n == NL else (128, n))
    tok = np.arange(NL)
    pos = np.stack([tok // 64, tok % 64]).astype(np.float64)
    inv = 10000.0 ** (-np.arange(16) / 16.0)
    dd = p % HD
    ang = pos[dd // 32] * inv[dd % 16][:, None]
    sign = np.where((dd % 32) < 16, -1.0, 1.0)[:, None]
    out["t_rope"] = np.stack([np.cos(ang), sign * np.sin(ang)], axis=1).astype(np.float32)
    return out


def kernel(**inputs):
    import concourse.bacc as _bacc
    from concourse.bass_utils import run_bass_kernel_spmd as _run

    nc = _bacc.Bacc("TRN2", target_bir_lowering=False, num_devices=1)
    f32 = mybir.dt.float32
    arrays, I, O = {}, {}, {}
    named = [(n, np.ascontiguousarray(inputs[n])) for n in INS] + list(tables().items())
    for name, a in named:
        arrays["in_" + name] = a
        I[name] = nc.dram_tensor("in_" + name, a.shape, f32, kind="ExternalInput").ap()
    for name, shape in OUTS:
        O[name] = nc.dram_tensor("out_" + name, shape, f32, kind="ExternalOutput").ap()
    build(nc, I, O)
    r = _run(nc, [arrays], core_ids=[0])
    return tuple(r.results[0]["out_" + name] for name, _ in OUTS)
```

```python
import math
import numpy as np
import concourse.bass as bass
from concourse import mybir
from contextlib import ExitStack

D = 1024
NC_ = 128
NL = 512
T = NL + NC_
DEPTH = 2
KT = D // 128
DFF = 2816
FT = DFF // 128
HD = 64
IN_W = 2176
CH = 64
NCH = T // CH
LCH = NL // CH
DECAY = 0.6065306597126334
GN_EPS = 64e-5
RMS_EPS = 1e-6
STREAMS = ((0, NL), (NL, T))
LEVELS = (1, 2, 4, 8, 16, 32)
S2_AT, ROPE_END = 10880, 17030
TH = T // 2
SLOTS = 4
SLOT_W = 2048
FH = FT // 2

PR_ADA, PR_NMIX, PR_NFFN, PR_SHIFT, PR_W0, PR_A0, PR_KK, PR_KA, PR_RK, PR_LNG, PR_LNB = (
    0, 48, 56, 64, 91, 95, 99, 101, 103, 105, 107)
NPR = 109

def chunk_order():
    order = [("ada", i) for i in range(8)]
    proj = [("rw", i) for i in range(5)] + [("q", 0), ("q", 1), ("k", 0), ("v", 0), ("fn", 0), ("fn", 1)]
    ada = 8
    for p in proj:
        order.append(p)
        if p[0] in ("rw", "q", "v"):
            order += [("ada", ada), ("ada", ada + 1)]
            ada += 2
    order += [("dftx", 0), ("dftc", 0), ("dfts", 0)]
    order += [("wo", i) for i in range(4)]
    for hf in range(2):
        order += [("f1", FH * hf + i) for i in range(FH)] + [("f2", 2 * m + hf) for m in range(KT)]
    return order


CHUNKS = chunk_order()
CHUNK_AT = {c: i for i, c in enumerate(CHUNKS)}
NCHUNK = len(CHUNKS)
assert NCHUNK % SLOTS == 0
DMAS = {"ada": 1, "rw": 1, "q": 4, "k": 1, "v": 1, "fn": 1, "dftx": 3, "dftc": 1, "dfts": 1, "wo": 3, "f1": 2, "f2": 1}


def ready_counts():
    tot, out = [0] * SLOTS, []
    for i, (kind, _) in enumerate(CHUNKS):
        tot[i % SLOTS] += 16 * DMAS[kind]
        out.append(tot[i % SLOTS])
    return out, tot


READY, READY_TOT = ready_counts()


LAST_ITEM = {("wo", i): ("out", 2 * i + 1) for i in range(4)}
LAST_ITEM.update({(t, 0): ("ft2", 1) for t in ("dftx", "dftc", "dfts")})


def split_units():
    u = [(("rw", m), ("rw", m // 2), m % 2, KT) for m in range(9)]
    u += [(("q", j), ("q", j // 2), j % 2, KT) for j in range(4)]
    u += [(x, x, 0, KT) for x in (("k", 0), ("v", 0), ("fn", 0), ("fn", 1))]
    for hf in range(2):
        for i in range(FH * hf, FH * hf + FH):
            u += [(("gate", i), ("f1", i), 0, KT), (("up", i), ("f1", i), 1, KT)]
        u += [(("f2", m, hf), ("f2", 2 * m + hf), 0, FH) for m in range(KT)]
    return u


UNITS = split_units()
NUNIT = len(UNITS)
UNIT_OF = {x[0]: n for n, x in enumerate(UNITS)}
NPROJ = UNIT_OF[("gate", 0)]
LAST_UNIT = {x[1]: n for n, x in enumerate(UNITS)}


def item_order():
    o = [("norm", 0), ("small", 0)]
    o += [("rw", m) for m in range(9)]
    o += [("q", 0), ("q", 1), ("swap", 0), ("q", 2), ("swap", 1), ("q", 3), ("swap", 2),
          ("k", 0), ("swap", 3), ("v", 0), ("swap", 4), ("fn", 0), ("kvT", 0), ("ckT", 0), ("fn", 1)]

    def prep(t):
        return [("w", t, 0), ("w", t, 1), ("a", t, 0), ("a", t, 1), ("kk", t), ("bonus", t)]

    def attn(blocks):
        r = []
        for b in blocks:
            r += [("s", b, i) for i in range(8)]
        return r

    o += prep(0) + [("ft1", i) for i in range(5)] + [("ft2", 0), ("ft2", 1)] + attn(ATT_A)
    o += prep(1) + attn(ATT_B)
    o += [("mean", 0), ("mean", 1), ("var", 0), ("var", 1), ("g", 0), ("g", 1)]
    o += [("out", m) for m in range(KT)] + [("norm", 1)]
    for hf in range(2):
        for i in range(FH * hf, FH * hf + FH):
            o += [("gate", i), ("up", i)]
        o += [("f2", m, hf) for m in range(KT)]
    return o


ATT_A = (0, 1)
ATT_B = (2, 3, 4)
ITEMS = item_order()
ITEM_AT = {x: i for i, x in enumerate(ITEMS)}
NITEM = len(ITEMS)
assert NITEM % 2 == 0 and len(ITEM_AT) == NITEM

def key_tiles(b):
    if b == 4:
        return [("lat", 4)]
    near = [("lat", t) for t in (b - 1, b, b + 1) if 0 <= t <= 3]
    return [("cache", 0)] + near if b == 3 else near + [("cache", 0)]


def key_runs(b):
    near = [t for kind, t in key_tiles(b) if kind == "lat"]
    runs = [("lat", near[0], len(near))]
    if b < 4:
        runs.insert(0 if b == 3 else 1, ("cache", 0, 1))
    return runs


def mask_cols(b):
    if b == 4:
        return 0, 128
    return {0: (256, 640), 3: (0, 384)}.get(b, (128, 640))


GROUPS = [[(0, 0, 0), (1, 0, 1), (2, 1, 3), (3, 1, 2)],
          [(0, 0, 2), (1, 0, 3), (2, 1, 1), (3, 1, 0)],
          [(0, 0, 4), (2, 1, 4)]]
NPAIR = sum(len(g) for g in GROUPS)


def chain_steps(group):
    out = []
    per_dir = {0: [], 1: []}
    for p, d, t in group:
        for hf in ((0, 1) if d == 0 else (1, 0)):
            per_dir[d].append((p, d, t, hf, 2 * t + hf))
    for a, b in zip(per_dir[0], per_dir[1]):
        out += [a, b]
    return out


def first_touch(g, d, t):
    return (g == 0) or (g == 2 and d == 0)


def needs_state(chunk, d):
    return chunk != (LCH - 1 if d == 0 else 0)


def y_order(group):
    seen, out = {}, []
    for s in chain_steps(group):
        seen[s[0]] = seen.get(s[0], 0) + 1
        if seen[s[0]] == 2:
            out.append(s[:3])
    return out


def state_plan():
    plan, n = {}, 0
    for ht in range(2):
        for g, group in enumerate(GROUPS):
            if g != 1:
                cur = {0: (0, None), 1: (0, None)}
            for (p, d, t, hf, ck) in chain_steps(group):
                plan[(ht, g, d, ck)] = cur[d]
                if needs_state(ck, d):
                    n += 1
                    cur[d] = (1 - cur[d][0], n)
    return plan


class Signal:

    def __init__(self, sem, per_layer, primed=0):
        self.sem, self.per, self.made, self.primed = sem, per_layer, 0, primed

    def __call__(self, n=1):
        self.made += n
        return self.sem

    def upto(self, l, n):
        assert n + self.primed > 0
        return l * self.per + n + self.primed

    def check(self, name, extra=0):
        if self.made - extra != self.per:
            print("SIGNAL", name, "makes", self.made - extra, "per layer, declared", self.per)
        return self.made - extra == self.per


class Own:

    def __init__(self, eng, sem, per_layer):
        self.eng, self.sem, self.per, self.n, self.l, self.most = eng, sem, per_layer, 0, 0, 0

    def after(self, ins):
        self.n += 1
        ins.then_inc(self.sem, 1)
        self.most = max(self.most, self.n)
        self.eng.wait_ge(self.sem, self.l * self.per + self.n)


DVE_CHAIN, POOL_CHAIN = 173, 2


def build(nc, I, O):
    f32 = mybir.dt.float32
    f32r = mybir.dt.float32r
    ALU = mybir.AluOpType
    ACT = mybir.ActivationFunctionType
    AX = mybir.AxisListType
    MUL, ADD, SUB, MAX = ALU.mult, ALU.add, ALU.subtract, ALU.max
    ctx = ExitStack()
    with ctx:
        def sb(name, shape):
            return ctx.enter_context(nc.sbuf_tensor(name, shape, f32))

        signals = {}

        def sig(name, per, primed=0):
            s = Signal(ctx.enter_context(nc.semaphore(name)), per, primed)
            signals[name] = s
            return s

        def sem(name):
            return ctx.enter_context(nc.semaphore(name))

        x = sb("x", [128, KT, T])
        ring = sb("ring", [128, SLOTS, SLOT_W])
        MN = sb("MN", [128, 4, 2, 2, 128])
        St = sb("St", [128, 2, 2, 128])
        masks = sb("masks", [128, 2, 256])
        lvl = sb("lvl", [128, 2, 6, 128])
        attmask = sb("attmask", [128, 640])
        mats = sb("mats", [128, 5, 128])
        reset = sb("reset", [128, T])
        lora = sb("lora", [128, 3, 256])
        prow = sb("prow", [NPR, 128])
        par = sb("par", [128, NPR])
        cvec = sb("cvec", [128, 24])
        csil = sb("csil", [128, KT, 2])
        csil_s = sb("csil_s", [128, 16])
        mod = sb("mod", [128, 48, 2])
        gain = sb("gain", [128, 3, KT, 2])
        sink = sb("sink", [128, 8])
        omka = sb("omka", [128, 2])
        eps = sb("eps", [128, 3])
        mid = sb("mid", [128, 2, NCH])
        end = sb("end", [128, 2, NCH])
        emid = sb("emid", [128, 2, NCH])
        eend = sb("eend", [128, 2, NCH])
        dec = sb("dec", [128, 2, NCH])
        negm = sb("negm", [128, 2, 8])
        den = sb("den", [128, 2, 8])
        esk = sb("esk", [128, 2, 8])
        kcT = sb("kcT", [128, 128])
        ckv = sb("ckv", [128, 2, 128])
        kvout = sb("kvout", [128, 128])
        s0in = sb("s0in", [128, 2, 128])
        with nc.sbuf_tensor("h", [128, KT, T], f32) as h, nc.sbuf_tensor("mix", [128, 25736], f32) as mix:
            pass
        def sbr(name, shape):
            return ctx.enter_context(nc.sbuf_tensor(name, shape, f32r))

        with ExitStack() as part:
            def sbp(name, shape):
                return part.enter_context(nc.sbuf_tensor(name, shape, f32r))

            in_lo = sbp("in_lo", [128, KT, T])
            sbp("gap0", [128, S2_AT])
            win0 = sbp("win0", [128, 2, KT * 128])
            sbp("gap1", [128, ROPE_END - S2_AT - 2 * KT * 128])
            in_hi = sbp("in_hi", [128, KT, T])
            win1 = sbp("win1", [128, 2, KT * 128])
        hid_hi = sbr("hid_hi", [128, FH, T])
        h_hi = sbr("h_hi", [128, KT, T])
        h_lo = sbr("h_lo", [128, KT, T])
        hid_lo = sbr("hid_lo", [128, FH, T])
        wsplit = sbr("wsplit", [128, 2, 2, FH * 128])
        tmp = sb("tmp", [128, T])

        ident, swapm, onesD, ones64, mean64 = (mats[:, i, :] for i in range(5))

        def mixv(at, n):
            return mix[:, at:at + n]

        def rows(at, n):
            return mix[:, at:at + n * T].rearrange("p (a t) -> p a t", t=T)

        ush = rows(0, 9)
        qt = rows(5760, 4)
        kt = mixv(8320, T)
        vtok = mixv(8960, T)
        uf = rows(9600, 2)
        S2 = rows(S2_AT, 2)
        CC = rows(12160, 2)
        E0 = 13440
        raw = mix[:, E0:E0 + 1286].rearrange("p (a t) -> p a t", t=643)
        e01 = rows(E0, 2)
        KK = mixv(14726, T)
        rot = mixv(15366, T)
        PB = 16006
        PW = 2432
        pb = [PB + PW * p for p in range(4)]
        assert pb[3] + PW <= 25736
        LP = [mix[:, b:b + 1024].rearrange("p (a t) -> p a t", a=2) for b in pb]
        Yi = [mix[:, b + 1024:b + 1280].rearrange("p (a t) -> p a t", a=2) for b in pb]
        Xi = [mix[:, b + 1280:b + 1536].rearrange("p (a t) -> p a t", a=2) for b in pb]
        P1 = [mix[:, b + 1536:b + 1792].rearrange("p (a t) -> p a t", a=2) for b in pb]
        TOK = [mix[:, b + 1792:b + 2176].rearrange("p (a t) -> p a t", a=3) for b in pb]
        W1A = [mix[:, b + 2176:b + 2432].rearrange("p (a t) -> p a t", a=2) for b in pb]
        UG = P1
        Qt = [mix[:, b + 1280:b + 1408] for b in pb]
        rope = mix[:, PB:PB + 1024].rearrange("p (a t) -> p a t", a=2)
        Z = mix[:, PB:PB + 2560].rearrange("p (a t) -> p a t", a=5)
        Pm = mix[:, PB:PB + 2048].rearrange("p (a t) -> p a t", a=4)
        PT = mix[:, PB + 2048:PB + 6144].rearrange("p (s c j t) -> p s c j t", s=2, c=4, j=4)
        mrow = St[0:2, :, :, :].rearrange("p d s c -> p (d s c)")
        stout = rot[:, 0:256].rearrange("p (a t) -> p a t", a=2)
        xin = mix[:, 0:5 * D].rearrange("p (a t) -> p a t", a=5)
        crow = mix[0:24, 5 * D:5 * D + 128]
        yout = mix[:, 0:2 * D].rearrange("p (a t) -> p a t", a=2)

        PS = ctx.enter_context(nc.psum_tensor("PS", [128, 8, 512], f32))
        ps = [PS[:, i, :] for i in range(8)]

        ld_const = sem("ld_const")
        ld_x = [sem(f"ld_x{t}") for t in range(5)]
        ld_tab = sem("ld_tab")
        ld_prow = sig("ld_prow", 16 * 15)
        ld_par = sig("ld_par", 16 * 6)
        ld_rope = sig("ld_rope", 16)
        ld_state = [sig(f"ld_state{t}", 64) for t in range(2)]
        w_ready = [sig(f"w_ready{s}", READY_TOT[s]) for s in range(SLOTS)]
        wh_ready = sig("wh_ready", NUNIT)
        wl_ready = sig("wl_ready", NUNIT, primed=4)
        hl_ready = sig("hl_ready", 2 * KT)
        hid_split = sig("hid_split", FT)
        acc_ready = sig("acc_ready", NITEM)
        acc_free = [sig(f"acc_free{i}", NITEM // 2, primed=1) for i in range(2)]
        sq_ready = sig("sq_ready", 2 * KT)
        sq_used = sig("sq_used", 2 * (KT - 1))
        h_scaled = sig("h_scaled", 2 * KT)
        h_ready = sig("h_ready", 2 * KT)
        gain_ready = sig("gain_ready", 2)
        ada_done = sig("ada_done", 24)
        mrow_sb = sig("mrow_sb", 12)
        mcol_ps = sig("mcol_ps", 12)
        par_ready = sig("par_ready", 1, primed=1)
        conv_out = sig("conv_out", 9)
        pads_zero = sig("pads_zero", 1)
        rot_raw = sig("rot_raw", 5)
        rot_cos = sig("rot_cos", 5)
        rot_done = sig("rot_done", 5, primed=1)
        kv_stored = sig("kv_stored", 32)
        lora_in = sig("lora_in", 1)
        kk_raw = sig("kk_raw", 2)
        kk_sq = sig("kk_sq", 2)
        rk_prod = sig("rk_prod", 2)
        cum_ready = sig("cum_ready", 2)
        exps_ready = sig("exps_ready", 2)
        kk_ready = sig("kk_ready", 2)
        ar_done = sig("ar_done", 2)
        scaled_ready = sig("scaled_ready", 2)
        p_ready = sig("p_ready", 40)
        p_exp = sig("p_exp", 40)
        den_ready = sig("den_ready", 40)
        p_scaled = sig("p_scaled", 40)
        pt_ps = sig("pt_ps", 40, primed=1)
        pt_sb = sig("pt_sb", 40, primed=1)
        pv_done = sig("pv_done", 10)
        o_sb = sig("o_sb", 5)
        mn_zero = sem("mn_zero")
        ctx_zero = sig("ctx_zero", 2)
        n2 = 2 * NPAIR
        s0_ps = sig("s0_ps", 4, primed=1)
        s0_sb = sig("s0_sb", 4)
        tok_ps, tok_sb = sig("tok_ps", n2), sig("tok_sb", n2)
        prod_ps, prod_sb = sig("prod_ps", 2 * n2), sig("prod_sb", 2 * n2)
        inv0_sb = sig("inv0_sb", n2)
        xt_ps, xt_sb = sig("xt_ps", 5 * n2), sig("xt_sb", 5 * n2)
        p1_ps, p1_sb = sig("p1_ps", 5 * n2), sig("p1_sb", 5 * n2)
        yu_ps, yu_sb = sig("yu_ps", 5 * n2), sig("yu_sb", 5 * n2)
        w1_ps, w1_sb = sig("w1_ps", n2), sig("w1_sb", n2)
        ug_ps, ug_sb = sig("ug_ps", n2), sig("ug_sb", n2)
        qmn_ps, qmn_sb = sig("qmn_ps", n2), sig("qmn_sb", n2)
        nstep = 2 * sum(1 for g in GROUPS for s in chain_steps(g) if needs_state(s[4], s[1]))
        st_ps, st_sb = sig("st_ps", nstep), sig("st_sb", nstep)
        y_ps, y_sb = sig("y_ps", n2), sig("y_sb", n2)
        fin_ps, fin_sb, fin_st = sig("fin_ps", 2), sig("fin_sb", 2), sig("fin_st", 128)
        ysq_ready = sig("ysq_ready", 2)
        hid_sig = sig("hid_sig", FT)
        xT_ps, xT_sb, c_ready = sem("xT_ps"), sem("xT_sb"), sem("c_ready")
        yT_ps, yT_sb, y_stored = sem("yT_ps"), sem("yT_sb"), [sem("y_stored0"), sem("y_stored1")]
        dve_own, pool_own = sem("dve_own"), sem("pool_own")
        sp_passed, pool_passed = sem("sp_passed"), sem("pool_passed")

        def acc_item(name):
            i = ITEM_AT[name]
            return i, ps[i % 2], ps[2 + i % 2]

        def pair_index(ht, g, n):
            return ht * NPAIR + sum(len(q) for q in GROUPS[:g]) + n

        def taken(e, l, name, settled=None):
            i = ITEM_AT[name]
            e.wait_ge(acc_free[i % 2].sem, acc_free[i % 2].upto(l, i // 2 + 1))
            if settled:
                settled()

        def layer_before(e, l, settled=None):
            for f in acc_free:
                e.wait_ge(f.sem, f.upto(l, 0))
            if settled:
                settled()

        def unit_weights(u):
            _, ck, g, nk = UNITS[u]
            n = CHUNK_AT[ck]
            raw_w = ring[:, n % SLOTS, 0:(2 if nk == KT else 1) * nk * 128].rearrange("p (k c) -> p k c", k=nk)
            slot = (win0, win1)[u % 2] if u < NPROJ else wsplit[:, u % 2, :, :]
            parts = [slot[:, i, 0:nk * 128].rearrange("p (k c) -> p k c", k=nk) for i in range(2)]
            return n, raw_w[:, :, 128 * g:128 * g + 128], parts[0], parts[1]

        PLAN = state_plan()

        block = ctx.enter_context(nc.Block())

        @block.sync
        def _(e):
            def settled():
                e.sem_inc(sp_passed)

            e.dma_start(crow[0:8, :], I["c"][0].rearrange("(a p) -> a p", p=128)).then_inc(ld_const, 16)
            e.dma_start(crow[8:16, :], I["c_ctx"].rearrange("(a p) -> a p", p=128)).then_inc(ld_const, 16)
            e.dma_start(crow[16:24, :], I["norm_final_g"].rearrange("(a p) -> a p", p=128)).then_inc(ld_const, 16)
            e.dma_start(mats[:, :, :], I["t_mats"]).then_inc(ld_const, 16)
            for t in range(5):
                src_x = I["x_sample"][0, 128 * t:128 * t + 128, :] if t < 4 else I["x_prompt"][0]
                e.dma_start(xin[:, t, :], src_x).then_inc(ld_x[t], 16)
            with e.Fori(0, DEPTH) as l:
                e.wait_ge(par_ready.sem, par_ready.upto(l, 0))
                settled()

                def prm(at, n, src):
                    e.dma_start(prow[at:at + n, :], src.rearrange("(a p) -> a p", p=128)).then_inc(ld_prow(16), 16)

                prm(PR_ADA, 48, I["b_ada"][l])
                prm(PR_NMIX, 8, I["norm_mix_g"][l])
                prm(PR_NFFN, 8, I["norm_ffn_g"][l])
                for j in range(3):
                    prm(PR_SHIFT + 9 * j, 9, I["rwkv_shift_w"][l, j])
                for d in range(2):
                    prm(PR_W0 + 2 * d, 2, I["rwkv_w0"][l, d])
                    prm(PR_A0 + 2 * d, 2, I["rwkv_a0"][l, d])
                prm(PR_KK, 2, I["rwkv_k_k"][l])
                prm(PR_KA, 2, I["rwkv_k_a"][l])
                prm(PR_RK, 2, I["rwkv_r_k"][l].rearrange("h d -> (h d)"))
                prm(PR_LNG, 2, I["rwkv_ln_g"][l])
                prm(PR_LNB, 2, I["rwkv_ln_b"][l])
                for n, (kind, i) in enumerate(CHUNKS):
                    if n == 8:
                        layer_before(e, l, settled)
                        e.dma_start(lora[:, 0, :], I["rwkv_w_up"][l].rearrange("d r c -> (d r) c")).then_inc(ld_par(16), 16)
                        e.dma_start(lora[:, 1, :], I["rwkv_a_up"][l].rearrange("d r c -> (d r) c")).then_inc(ld_par(16), 16)
                        e.dma_start(lora[:, 2, :], I["rwkv_g_up"][l]).then_inc(ld_par(16), 16)
                        e.dma_start(ckv[:, 0, :], I["cache_k"][0, l].rearrange("s h d -> s (h d)")).then_inc(ld_par(16), 16)
                        e.dma_start(ckv[:, 1, :], I["cache_v"][0, l].rearrange("s h d -> s (h d)")).then_inc(ld_par(16), 16)
                        e.dma_start(sink[:, :], I["attn_sink"][l].partition_broadcast(128)).then_inc(ld_par(16), 16)
                        e.dma_start(rope, I["t_rope"]).then_inc(ld_rope(16), 16)
                    old = CHUNKS[n - SLOTS]
                    if old[0] == "ada":
                        e.wait_ge(ada_done.sem, ada_done.upto(l, old[1] + 1))
                    elif old in LAST_UNIT:
                        e.wait_ge(wl_ready.sem, wl_ready.upto(l, LAST_UNIT[old] + 1 - (NUNIT if n < SLOTS else 0)))
                    else:
                        e.wait_ge(acc_ready.sem, acc_ready.upto(l, ITEM_AT[LAST_ITEM[old]] + 1))
                    settled()
                    sl = n % SLOTS
                    dst = ring[:, sl, 0:2048].rearrange("p (k c) -> p k c", k=KT)
                    done = w_ready[sl]

                    def src(w, c0, n_):
                        return w[l, :, c0:c0 + n_].rearrange("(k p) c -> p k c", p=128)

                    if kind == "ada":
                        e.dma_start(dst, src(I["w_ada"], 256 * i, 256)).then_inc(done(16), 16)
                    elif kind == "rw":
                        w_ = 256 if i < 4 else 128
                        e.dma_start(dst[:, :, 0:w_], src(I["w_in"], 768 + 256 * i, w_)).then_inc(done(16), 16)
                    elif kind == "q":
                        for j in range(2):
                            for g in range(2):
                                e.dma_start(dst[:, :, 128 * j + 64 * g:128 * j + 64 * g + 64],
                                            src(I["w_in"], 128 * i + 64 * j + 256 * g, 64)).then_inc(done(16), 16)
                    elif kind in ("k", "v", "fn"):
                        c0 = {"k": 512, "v": 640, "fn": 1920 + 128 * i}[kind]
                        e.dma_start(dst[:, :, 0:128], src(I["w_in"], c0, 128)).then_inc(done(16), 16)
                    elif kind == "dftx":
                        e.dma_start(ring[:, sl, 0:128], I["t_dftcx"]).then_inc(done(16), 16)
                        e.dma_start(ring[:, sl, 128:256], I["t_dftsx"]).then_inc(done(16), 16)
                        e.dma_start(ring[:, sl, 256:512], I["t_chan"]).then_inc(done(16), 16)
                    elif kind in ("dftc", "dfts"):
                        e.dma_start(ring[:, sl, 0:2048].rearrange("p (k c) -> p k c", k=4),
                                    I["t_" + kind]).then_inc(done(16), 16)
                    elif kind == "wo":
                        wo = I["w_out"]
                        c0 = 256 * i
                        for g in range(2):
                            e.dma_start(dst[64 * g:64 * g + 64, 0:4, :],
                                        wo[l, 256 * g:256 * g + 256, c0:c0 + 256].rearrange(
                                            "(k p) c -> p k c", p=64)).then_inc(done(16), 16)
                        e.dma_start(dst[:, 4:8, :], wo[l, 512:1024, c0:c0 + 256].rearrange(
                            "(k p) c -> p k c", p=128)).then_inc(done(16), 16)
                    elif kind == "f1":
                        for g in range(2):
                            e.dma_start(dst[:, :, 128 * g:128 * g + 128],
                                        src(I["ffn_w_in"], DFF * g + 128 * i, 128)).then_inc(done(16), 16)
                    else:
                        m, hf = i // 2, i % 2
                        e.dma_start(ring[:, sl, 0:FH * 128].rearrange("p (k c) -> p k c", k=FH),
                                    I["ffn_w_out"][l, FH * 128 * hf:FH * 128 * (hf + 1),
                                                   128 * m:128 * m + 128].rearrange(
                                        "(k p) c -> p k c", p=128)).then_inc(done(16), 16)
            for t in range(5):
                e.wait_ge(yT_sb, t + 1)
                dst = O["y_s"][0, 128 * t:128 * t + 128, :] if t < 4 else O["y_p"][0]
                e.dma_start(dst, yout[:, t % 2, :]).then_inc(y_stored[t % 2], 16)
            e.wait_ge(y_stored[0], 48)
            e.wait_ge(y_stored[1], 32)

        @block.gpsimd
        def _(e):
            own = Own(e, pool_own, POOL_CHAIN)

            def settled():
                e.sem_inc(pool_passed)

            e.dma_start(masks[:, :, :], I["t_masks"]).then_inc(ld_tab, 16)
            e.dma_start(lvl[:, :, :, :], I["t_lvl"]).then_inc(ld_tab, 16)
            e.dma_start(attmask[:, :], I["t_attmask"]).then_inc(ld_tab, 16)
            e.dma_start(reset[:, :], I["t_reset"]).then_inc(ld_tab, 16)
            nc.gpsimd.memset(MN[:, :, :, :, :], 0.0).then_inc(mn_zero, 1)
            nc.gpsimd.memset(s0in[:, :, :], 0.0).then_inc(mn_zero, 1)
            nc.gpsimd.memset(eps[:, 0:1], RMS_EPS).then_inc(mn_zero, 1)
            nc.gpsimd.memset(eps[:, 1:2], 1e-12).then_inc(mn_zero, 1)
            nc.gpsimd.memset(eps[:, 2:3], GN_EPS).then_inc(mn_zero, 1)
            e.wait_ge(mn_zero, 5)
            e.wait_ge(xT_ps, 11)
            with e.Fori(0, DEPTH) as l:
                own.l, own.n = l, 0
                layer_before(e, l, settled)
                nc.gpsimd.memset(raw[:, :, 0:1], 0.0)
                nc.gpsimd.memset(raw[:, :, 513:514], 0.0)
                nc.gpsimd.memset(raw[:, :, 642:643], 0.0).then_inc(pads_zero(), 1)

                def weight_low(u):
                    n, raw_w, hi, lo = unit_weights(u)
                    e.wait_ge(wh_ready.sem, wh_ready.upto(l, u + 1))
                    settled()
                    nc.gpsimd.tensor_tensor(lo, raw_w, hi, SUB).then_inc(wl_ready(), 1)

                for u in range(UNIT_OF[("q", 2)]):
                    weight_low(u)
                e.wait_ge(ld_rope.sem, ld_rope.upto(l, 16))
                settled()
                for r in range(5):
                    weight_low(UNIT_OF[("q", 2)] + r)
                    dst = qt[:, r, 0:NL] if r < 4 else kt[:, 0:NL]
                    e.wait_ge(rot_raw.sem, rot_raw.upto(l, r + 1))
                    settled()
                    nc.gpsimd.tensor_tensor(dst, raw[:, r % 2, 0:NL], rope[:, 0, :], MUL).then_inc(rot_cos(), 1)
                weight_low(NPROJ - 1)
                taken(e, l, ("kvT", 0), settled)
                e.dma_start(O["new_k"][0, l].rearrange("s h d -> s (h d)"), kvout[:, :]).then_inc(kv_stored(16), 16)
                e.dma_start(O["new_v"][0, l].rearrange("s h d -> s (h d)"), vtok[:, 512:640]).then_inc(kv_stored(16), 16)

                def prep(t):
                    e.wait_ge(conv_out.sem, conv_out.upto(l, 9))
                    settled()
                    e.wait_ge(acc_ready.sem, acc_ready.upto(l, ITEM_AT[("w", t, 0)] + 1))
                    settled()
                    nc.gpsimd.tensor_scalar(KK, ush[:, 2 + t, :], par[:, PR_KK + t:PR_KK + t + 1], None,
                                            MUL).then_inc(kk_raw(), 1)
                    own.after(nc.gpsimd.tensor_tensor(e01[:, 1, :], ush[:, t, :], ush[:, 2 + t, :], MUL))
                    settled()
                    nc.gpsimd.tensor_scalar(e01[:, 1, :], e01[:, 1, :], par[:, PR_RK + t:PR_RK + t + 1], None,
                                            MUL).then_inc(rk_prod(), 1)
                    e.wait_ge(s0_ps.sem, s0_ps.upto(l, 2 * t))
                    settled()
                    for d in range(2):
                        for g in range(2):
                            e.dma_start(s0in[64 * g:64 * g + 64, d, 64 * g:64 * g + 64],
                                        I["state_rwkv"][0, l, d, 2 * t + g]).then_inc(ld_state[t](16), 16)
                    e.wait_ge(exps_ready.sem, exps_ready.upto(l, t + 1))
                    settled()
                    e.wait_ge(kk_ready.sem, kk_ready.upto(l, t + 1))
                    settled()
                    rb = ush[:, t:t + 1, :].to_broadcast([128, 2, T])
                    kb = KK.unsqueeze(1).to_broadcast([128, 2, T])
                    nc.gpsimd.tensor_tensor(h[:, 2:4, :], h[:, 2:4, :], rb, MUL)
                    nc.gpsimd.tensor_tensor(h[:, 0:2, :], h[:, 0:2, :], kb, MUL).then_inc(ar_done(), 1)

                prep(0)
                prep(1)
                for t in range(2):
                    e.wait_ge(fin_sb.sem, fin_sb.upto(l, t + 1))
                    settled()
                    for d in range(2):
                        for g in range(2):
                            e.dma_start(O["new_s"][0, l, d, 2 * t + g],
                                        stout[64 * g:64 * g + 64, d, 64 * g:64 * g + 64]).then_inc(fin_st(16), 16)
                    e.wait_ge(fin_st.sem, fin_st.upto(l, 64 * (t + 1)))
                    settled()
                e.wait_ge(kv_stored.sem, kv_stored.upto(l, 32))
                settled()
                for u in range(NPROJ, NUNIT):
                    weight_low(u)
            assert own.most == POOL_CHAIN, own.most

        @block.tensor
        def _(e):
            mm = nc.tensor.matmul
            tr = nc.tensor.transpose

            e.wait_ge(ld_const, 16 * 4)
            tr(ps[6][:, 0:24], crow, ident[0:24, 0:24]).then_inc(xT_ps, 1)
            for t in range(5):
                e.wait_ge(ld_x[t], 16)
                for g in range(2):
                    n = 2 * t + g
                    if n >= 2:
                        e.wait_ge(xT_sb, n - 1)
                    for k in range(4):
                        last = tr(ps[4 + n % 2][:, 128 * k:128 * k + 128],
                                  xin[:, t, 512 * g + 128 * k:512 * g + 128 * k + 128], ident)
                    last.then_inc(xT_ps, 1)
            e.wait_ge(c_ready, 3)
            e.wait_ge(xT_sb, 10)

            with e.Fori(0, DEPTH) as l:
                def begin(name):
                    i, lat, cx = acc_item(name)
                    e.wait_ge(acc_free[i % 2].sem, acc_free[i % 2].upto(l, i // 2))
                    return lat, cx

                def chunk(name):
                    n = CHUNK_AT[name]
                    e.wait_ge(w_ready[n % SLOTS].sem, w_ready[n % SLOTS].upto(l, READY[n]))
                    return ring[:, n % SLOTS, :]

                def both(lat, cx, w, k, n, v):
                    mm(lat[:, :], w, v[:, 0:NL], start=(k == 0), stop=(k == n - 1))
                    return mm(cx[:, 0:NC_], w, v[:, NL:T], start=(k == 0), stop=(k == n - 1))

                def norm(which):
                    lat, cx = begin(("norm", which))
                    for k in range(KT):
                        e.wait_ge(sq_ready.sem, sq_ready.upto(l, which * KT + k + 1))
                        last = both(lat, cx, onesD, k, KT, S2[:, k % 2, :])
                        last.then_inc(sq_used() if k < KT - 1 else acc_ready(), 1)

                def ada_rows(j):
                    bank = ps[6 + j % 2]
                    if j >= 2:
                        e.wait_ge(mrow_sb.sem, mrow_sb.upto(l, j - 1))
                    for i in (2 * j, 2 * j + 1):
                        w = chunk(("ada", i))[:, 0:2048].rearrange("p (k c) -> p k c", k=KT)
                        at = 256 * (i % 2)
                        for k in range(KT):
                            last = mm(bank[0:2, at:at + 256], csil[:, k, :], w[:, k, :],
                                      start=(k == 0), stop=(k == KT - 1))
                        last.then_inc(ada_done(), 1)

                def ada_cols(j):
                    e.wait_ge(mrow_sb.sem, mrow_sb.upto(l, j + 1))
                    bank = ps[4] if j < 4 else ps[5]
                    for g in range(4):
                        mt = 4 * j + g
                        last = mm(bank[:, 2 * mt:2 * mt + 2], mrow[:, 128 * g:128 * g + 128], ident[0:2, 0:2],
                                  start=True, stop=True)
                    last.then_inc(mcol_ps(), 1)

                def unit(u, order, total, first=0):
                    name, ck, g, nk = UNITS[u]
                    if first == 0:
                        begin(name)
                        e.wait_ge(wl_ready.sem, wl_ready.upto(l, u + 1))
                    i, lat, cx = acc_item(name)
                    which = 0 if u < NPROJ else 1
                    hi, lo = ((in_hi, in_lo) if which == 0 else (h_hi, h_lo)) if nk == KT else (hid_hi, hid_lo)
                    w_hi, w_lo = unit_weights(u)[2:]
                    for n, (k, p) in enumerate(order, first):
                        if u in (0, NPROJ) and p == 0:
                            e.wait_ge(h_ready.sem, h_ready.upto(l, which * KT + k + 1))
                        if u in (0, NPROJ) and p == 2:
                            e.wait_ge(hl_ready.sem, hl_ready.upto(l, which * KT + k + 1))
                        if name[:2] == ("f2", 0) and p == 0:
                            e.wait_ge(hid_split.sem, hid_split.upto(l, FH * name[2] + k + 1))
                        w = (w_lo if p == 1 else w_hi)[:, k, :]
                        v = (lo if p == 2 else hi)[:, k, :]
                        mm(lat[:, 0:TH], w, v[:, 0:TH], start=(n == 0), stop=(n == total - 1))
                        last = mm(cx[:, 0:TH], w, v[:, TH:T], start=(n == 0), stop=(n == total - 1))
                    if first + len(order) == total:
                        last.then_inc(acc_ready(), 1)

                def first_two(u):
                    on_high = [(k, p) for k in range(KT) for p in (0, 1)]
                    on_low = [(k, 2) for k in range(KT)]
                    unit(u, on_high, 3 * KT)
                    unit(u + 1, on_high, 3 * KT)
                    unit(u, on_low, 3 * KT, len(on_high))
                    unit(u + 1, on_low, 3 * KT, len(on_high))

                def whole(u):
                    nk = UNITS[u][3]
                    unit(u, [(k, p) for k in range(nk) for p in range(3)], 3 * nk)

                ada_rows(0)
                ada_rows(1)
                ada_cols(0)
                norm(0)
                ada_cols(1)
                e.wait_ge(ld_prow.sem, ld_prow.upto(l, ld_prow.per))
                lat, cx = begin(("small", 0))
                tr(lat[:, 0:NPR], prow[:, :], ident[0:NPR, 0:NPR]).then_inc(acc_ready(), 1)
                ada_rows(2)
                ada_rows(3)
                ada_cols(2)
                ada_cols(3)

                def cols(name, g):
                    w = chunk(name)[:, 0:2048].rearrange("p (k c) -> p k c", k=KT)
                    return [w[:, k, 128 * g:128 * g + 128] for k in range(KT)]

                def swap(r):
                    lat, cx = begin(("swap", r))
                    e.wait_ge(rot_raw.sem, rot_raw.upto(l, r + 1))
                    mm(lat[:, :], swapm, raw[:, r % 2, 0:NL], start=True, stop=True).then_inc(acc_ready(), 1)

                first_two(0)
                ada_rows(4)
                for m in range(2, 9):
                    whole(UNIT_OF[("rw", m)])
                    if m % 2 == 0:
                        ada_cols(3 + m // 2)
                    if m % 2 == 1 or m == 8:
                        ada_rows(4 + m // 2)
                whole(UNIT_OF[("q", 0)])
                ada_cols(8)
                whole(UNIT_OF[("q", 1)])
                swap(0)
                ada_rows(9)
                whole(UNIT_OF[("q", 2)])
                ada_cols(9)
                swap(1)
                whole(UNIT_OF[("q", 3)])
                swap(2)
                ada_rows(10)
                whole(UNIT_OF[("k", 0)])
                ada_cols(10)
                swap(3)
                whole(UNIT_OF[("v", 0)])
                swap(4)
                ada_rows(11)
                whole(UNIT_OF[("fn", 0)])
                ada_cols(11)
                lat, cx = begin(("kvT", 0))
                taken(e, l, ("v", 0))
                for t in range(4):
                    tr(lat[:, 128 * t:128 * t + 128], KK[:, 128 * t:128 * t + 128], ident)
                tr(cx[:, 0:128], KK[:, NL:T], ident)
                tr(cx[:, 128:256], kt[:, NL:T], ident).then_inc(acc_ready(), 1)
                lat, cx = begin(("ckT", 0))
                e.wait_ge(ld_par.sem, ld_par.upto(l, ld_par.per))
                tr(lat[:, 0:128], ckv[:, 0, :], ident).then_inc(acc_ready(), 1)
                whole(UNIT_OF[("fn", 1)])

                def prep(t):
                    if t == 0:
                        e.wait_ge(lora_in.sem, lora_in.upto(l, 1))
                    for kind, which, src in (("w", 0, 7), ("a", 1, 8)):
                        for d in range(2):
                            lat, cx = begin((kind, t, d))
                            both(lat, cx, lora[64 * d:64 * d + 64, which, 128 * t:128 * t + 128], 0, 1,
                                 ush[64 * d:64 * d + 64, src, :]).then_inc(acc_ready(), 1)
                    lat, cx = begin(("kk", t))
                    e.wait_ge(kk_sq.sem, kk_sq.upto(l, t + 1))
                    both(lat, cx, ones64, 0, 1, e01[:, 0, :]).then_inc(acc_ready(), 1)
                    lat, cx = begin(("bonus", t))
                    e.wait_ge(rk_prod.sem, rk_prod.upto(l, t + 1))
                    both(lat, cx, ones64, 0, 1, e01[:, 1, :]).then_inc(acc_ready(), 1)

                prep(0)

                taken(e, l, ("fn", 0))
                taken(e, l, ("fn", 1))
                tx_ = chunk(("dftx", 0))
                for t in range(5):
                    lat, cx = begin(("ft1", t))
                    for f in range(2):
                        last = mm(lat[:, 256 * f:256 * f + 256], uf[:, f, 128 * t:128 * t + 128], tx_[:, 256:512],
                                  start=True, stop=True)
                    last.then_inc(acc_ready(), 1)
                tc_, ts_ = chunk(("dftc", 0)), chunk(("dfts", 0))
                for f in range(2):
                    lat, cx = begin(("ft2", f))
                    if f == 0:
                        taken(e, l, ("ft1", 3))
                        taken(e, l, ("ft1", 4))
                    for t in range(4):
                        mm(lat[:, :], Z[:, t, 256 * f:256 * f + 128], tc_[:, 512 * t:512 * t + 512],
                           start=(t == 0), stop=False)
                        mm(lat[:, :], Z[:, t, 256 * f + 128:256 * f + 256], ts_[:, 512 * t:512 * t + 512],
                           start=False, stop=(t == 3))
                    mm(cx[:, 0:128], Z[:, 4, 256 * f:256 * f + 128], tx_[:, 0:128], start=True, stop=False)
                    mm(cx[:, 0:128], Z[:, 4, 256 * f + 128:256 * f + 256], tx_[:, 128:256],
                       start=False, stop=True).then_inc(acc_ready(), 1)

                def attention(blocks, done):
                    seq = [(b, i) for b in blocks for i in range(8)]

                    def scores(n):
                        b, i = seq[n]
                        j, g = i % 4, i // 4
                        rowsl = slice(64 * g, 64 * g + 64)
                        q = qt[rowsl, j, 128 * b:128 * b + 128]
                        lat, cx = begin(("s", b, i))
                        at = 0
                        for kind, t, nt in key_runs(b):
                            w = 128 * nt
                            src = kcT[rowsl, :] if kind == "cache" else kt[rowsl, 128 * t:128 * t + w]
                            last = mm(lat[:, at:at + w], q, src, start=True, stop=True)
                            at += w
                        last.then_inc(acc_ready(), 1)

                    def transposes(n):
                        b, i = seq[n]
                        m = done + n
                        e.wait_ge(p_scaled.sem, p_scaled.upto(l, m + 1))
                        e.wait_ge(pt_sb.sem, pt_sb.upto(l, max(m - 1, 0)))
                        for c in range(len(key_tiles(b))):
                            last = tr(ps[4 + m % 2][:, 128 * c:128 * c + 128], Pm[:, m % 4, 128 * c:128 * c + 128],
                                      ident)
                        last.then_inc(pt_ps(), 1)

                    def values(q):
                        b, i = seq[4 * q]
                        g = i // 4
                        G = done // 4 + q
                        nb = G // 2
                        if g == 0 and nb >= 2:
                            e.wait_ge(o_sb.sem, o_sb.upto(l, nb - 1))
                        e.wait_ge(pt_sb.sem, pt_sb.upto(l, 4 * G + 4))
                        tiles = key_tiles(b)
                        for c, (kind, t) in enumerate(tiles):
                            v = (ckv[:, 1, 64 * g:64 * g + 64] if kind == "cache"
                                 else vtok[:, 128 * t + 64 * g:128 * t + 64 * g + 64])
                            last = mm(ps[6 + nb % 2][64 * g:64 * g + 64, :], v,
                                      PT[:, G % 2, c, :, :].rearrange("p j t -> p (j t)"),
                                      start=(c == 0), stop=(c == len(tiles) - 1))
                        last.then_inc(pv_done(), 1)

                    nh = len(seq)
                    for n in range(nh + 4):
                        if n < nh:
                            scores(n)
                        if 0 <= n - 2 < nh:
                            transposes(n - 2)
                        if n >= 7 and n % 4 == 3:
                            values((n - 7) // 4)

                e.wait_ge(rot_done.sem, rot_done.upto(l, 5))
                taken(e, l, ("kvT", 0))
                taken(e, l, ("ckT", 0))
                e.wait_ge(par_ready.sem, par_ready.upto(l, 1))
                attention(ATT_A, 0)

                nchain = [0]

                def recurrence(ht, items_before, blocks_before):
                    for q_ in range(2):
                        e.wait_ge(acc_free[q_].sem, acc_free[q_].upto(l, (items_before + 1 - q_) // 2))
                    e.wait_ge(o_sb.sem, o_sb.upto(l, blocks_before))
                    e.wait_ge(scaled_ready.sem, scaled_ready.upto(l, ht + 1))
                    e.wait_ge(ar_done.sem, ar_done.upto(l, ht + 1))
                    e.wait_ge(ld_state[ht].sem, ld_state[ht].upto(l, 64))
                    for d in range(2):
                        tr(ps[7][:, 128 * d:128 * d + 128], s0in[:, d, :], ident).then_inc(s0_ps(), 1)
                    for g, group in enumerate(GROUPS):
                        base = pair_index(ht, g, 0)
                        A_, R_, K_, B_ = 0, 2, 4, 6
                        for n, (p, d, t) in enumerate(group):
                            if g > 0:
                                e.wait_ge(st_sb.sem, st_sb.upto(l, nchain[0]))
                                e.wait_ge(y_sb.sem, y_sb.upto(l, base))
                            c = slice(128 * t, 128 * t + 128)
                            b0 = ps[2 * p]
                            tr(b0[:, 0:128], h[:, A_ + d, c], ident)
                            tr(b0[:, 128:256], h[:, K_ + d, c], ident)
                            tr(b0[:, 256:384], h[:, B_ + d, c], ident)
                            tr(b0[:, 384:512], ush[:, 4 + ht, c], ident).then_inc(tok_ps(), 1)
                        for hd in range(2):
                            hs = slice(64 * hd, 64 * hd + 64)
                            for n, (p, d, t) in enumerate(group):
                                c = slice(128 * t, 128 * t + 128)
                                bank = ps[2 * p + 1] if hd == 0 else ps[2 * p]
                                if hd == 0 and g == 0 and p == 3:
                                    e.wait_ge(s0_sb.sem, s0_sb.upto(l, 2 * ht + 2))
                                if hd == 1:
                                    e.wait_ge(tok_sb.sem, tok_sb.upto(l, base + n + 1))
                                ar = h[hs, d:d + 3:2, c]
                                mm(bank[:, 0:256], h[hs, K_ + d, c], ar, start=True, stop=True)
                                mm(bank[:, 256:512], h[hs, B_ + d, c], ar, start=True, stop=True).then_inc(
                                    prod_ps(), 1)

                        def flip(level, n, p):
                            b = ps[2 * p + 1]
                            for hd in range(2):
                                last = tr(b[:, 256 + 128 * hd:384 + 128 * hd], Yi[p][:, hd, :], ident)
                            last.then_inc(xt_ps(), 1)

                        gb = 5 * base
                        ng = len(group)
                        for n, (p, d, t) in enumerate(group):
                            e.wait_ge(inv0_sb.sem, inv0_sb.upto(l, base + n + 1))
                            flip(0, n, p)
                        for lv in range(1, 6):
                            at = gb + (lv - 1) * ng
                            for n, (p, d, t) in enumerate(group):
                                e.wait_ge(xt_sb.sem, xt_sb.upto(l, at + n + 1))
                                for hd in range(2):
                                    last = mm(ps[2 * p][:, 128 * hd:128 * hd + 128], LP[p][:, hd, 256:384],
                                              Xi[p][:, hd, :], start=True, stop=True)
                                last.then_inc(p1_ps(), 1)
                            for n, (p, d, t) in enumerate(group):
                                e.wait_ge(p1_sb.sem, p1_sb.upto(l, at + n + 1))
                                for hd in range(2):
                                    last = mm(ps[2 * p + 1][:, 128 * hd:128 * hd + 128], P1[p][:, hd, :],
                                              Yi[p][:, hd, :], start=True, stop=True)
                                last.then_inc(yu_ps(), 1)
                            if lv < 5:
                                for n, (p, d, t) in enumerate(group):
                                    e.wait_ge(yu_sb.sem, yu_sb.upto(l, at + n + 1))
                                    flip(lv, n, p)
                        for n, (p, d, t) in enumerate(group):
                            for hd in range(2):
                                last = mm(ps[2 * p][:, 64 * hd:64 * hd + 64], LP[p][:, hd, 0:128],
                                          TOK[p][:, 2, 64 * hd:64 * hd + 64], start=True, stop=True)
                            last.then_inc(w1_ps(), 1)
                        for n, (p, d, t) in enumerate(group):
                            e.wait_ge(yu_sb.sem, yu_sb.upto(l, gb + 4 * ng + n + 1))
                            e.wait_ge(w1_sb.sem, w1_sb.upto(l, base + n + 1))
                            for hd in range(2):
                                last = mm(ps[2 * p + 1][:, 256 + 128 * hd:384 + 128 * hd], Yi[p][:, hd, :],
                                          W1A[p][:, hd, :], start=True, stop=True)
                            last.then_inc(ug_ps(), 1)
                        for n, (p, d, t) in enumerate(group):
                            e.wait_ge(ug_sb.sem, ug_sb.upto(l, base + n + 1))
                            b0 = ps[2 * p]
                            for hd in range(2):
                                o = slice(64 * hd, 64 * hd + 64)
                                mm(b0[o, 0:128], UG[p][:, hd, 64:128], LP[p][:, hd, 384:512], start=True, stop=True)
                                for hf in range(2):
                                    r = slice(64 * hf, 64 * hf + 64)
                                    bh = ps[2 * p + hf]
                                    mm(bh[o, 128:192], UG[p][r, hd, 64:128], TOK[p][r, 1, o], start=True, stop=True)
                                    mm(bh[o, 256:320], TOK[p][r, 0, o], TOK[p][r, 2, o], start=True, stop=False)
                                    last = mm(bh[o, 256:320], TOK[p][r, 1, o], UG[p][r, hd, 0:64],
                                              start=False, stop=True)
                            last.then_inc(qmn_ps(), 1)
                        for n, (p, d, t) in enumerate(group):
                            b1 = ps[2 * p + 1]
                            e.wait_ge(qmn_sb.sem, qmn_sb.upto(l, base + n + 1))
                            for hd in range(2):
                                o = slice(64 * hd, 64 * hd + 64)
                                mm(b1[o, 0:128], TOK[p][:, 2, o], LP[p][:, hd, 128:256], start=True, stop=False,
                                   skip_group_check=True)
                                mm(b1[o, 0:128], UG[p][:, hd, 0:64], LP[p][:, hd, 384:512], start=False, stop=False,
                                   skip_group_check=True)
                        seen = {}
                        for (p, d, t, hf, ck) in chain_steps(group):
                            n = [q[0] for q in group].index(p)
                            e.wait_ge(qmn_sb.sem, qmn_sb.upto(l, base + n + 1))
                            slot, need = PLAN[(ht, g, d, ck)]
                            if need is None and g == 2:
                                e.wait_ge(ctx_zero.sem, ctx_zero.upto(l, ht + 1))
                            elif need is None:
                                e.wait_ge(s0_sb.sem, s0_sb.upto(l, 2 * ht + d + 1))
                            else:
                                e.wait_ge(st_sb.sem, st_sb.upto(l, need))
                            S = St[:, d, slot, :]
                            last = mm(ps[2 * p + 1][:, 64 * hf:64 * hf + 64], S, Qt[p][:, 64 * hf:64 * hf + 64],
                                      start=False, stop=True, skip_group_check=True)
                            seen[p] = seen.get(p, 0) + 1
                            if seen[p] == 2:
                                last.then_inc(y_ps(), 1)
                            if needs_state(ck, d):
                                mm(ps[2 * p][:, 384:512], MN[:, p, 0, hf, :], S, start=True, stop=True).then_inc(
                                    st_ps(), 1)
                                nchain[0] += 1
                    e.wait_ge(st_sb.sem, st_sb.upto(l, nchain[0]))
                    e.wait_ge(y_sb.sem, y_sb.upto(l, pair_index(ht, 2, 2)))
                    for d in range(2):
                        last = tr(ps[6][:, 128 * d:128 * d + 128], St[:, d, 0, :], ident)
                    last.then_inc(fin_ps(), 1)
                    e.wait_ge(fin_sb.sem, fin_sb.upto(l, ht + 1))

                recurrence(0, ITEM_AT[("w", 1, 0)], 2)
                prep(1)
                attention(ATT_B, 16)
                recurrence(1, ITEM_AT[("mean", 0)], 5)

                for t in range(2):
                    lat, cx = begin(("mean", t))
                    both(lat, cx, mean64, 0, 1, ush[:, 2 + t, :]).then_inc(acc_ready(), 1)
                for t in range(2):
                    lat, cx = begin(("var", t))
                    e.wait_ge(ysq_ready.sem, ysq_ready.upto(l, t + 1))
                    both(lat, cx, mean64, 0, 1, e01[:, t, :]).then_inc(acc_ready(), 1)
                for t in range(2):
                    lat, cx = begin(("g", t))
                    both(lat, cx, lora[:, 2, 128 * t:128 * t + 128], 0, 1, ush[:, 6, :]).then_inc(acc_ready(), 1)

                taken(e, l, ("ft2", 0))
                taken(e, l, ("ft2", 1))
                e.wait_ge(o_sb.sem, o_sb.upto(l, 5))
                src_of = {0: qt[:, 0, :], 1: qt[:, 1, :], 2: qt[:, 2, :], 3: qt[:, 3, :],
                          4: ush[:, 2, :], 5: ush[:, 3, :], 6: uf[:, 0, :], 7: uf[:, 1, :]}
                def out(m, ks, first):
                    w = cols(("wo", m // 2), m % 2)
                    lat, cx = begin(("out", m)) if first == 0 else acc_item(("out", m))[1:]
                    for n, k in enumerate(ks, first):
                        last = both(lat, cx, w[k], n, KT, src_of[k])
                    if first + len(ks) == KT:
                        last.then_inc(acc_ready(), 1)

                early, late = (0, 1, 2, 3, 6, 7), (4, 5)
                out(0, early, 0)
                out(1, early, 0)
                taken(e, l, ("g", 0))
                taken(e, l, ("g", 1))
                out(0, late, len(early))
                out(1, late, len(early))
                for m in range(2, KT):
                    out(m, early + late, 0)
                norm(1)
                first_two(NPROJ)
                for u in range(NPROJ + 2, NUNIT):
                    whole(u)

            lat, cx = ps[0], ps[2]
            layer_before(e, DEPTH)
            for k in range(KT):
                e.wait_ge(sq_ready.sem, sq_ready.upto(DEPTH, k + 1))
                mm(lat[:, :], onesD, S2[:, k % 2, 0:NL], start=(k == 0), stop=(k == KT - 1))
                mm(cx[:, 0:NC_], onesD, S2[:, k % 2, NL:T], start=(k == 0), stop=(k == KT - 1)).then_inc(
                    sq_used.sem if k < KT - 1 else acc_ready.sem, 1)
            e.wait_ge(h_scaled.sem, h_scaled.upto(DEPTH, KT))
            for t in range(5):
                for g in range(2):
                    n = 2 * t + g
                    if n >= 4:
                        e.wait_ge(yT_sb, n // 2 - 1)
                    for k in range(4):
                        last = tr(ps[4 + n % 4][:, 128 * k:128 * k + 128],
                                  h[:, 4 * g + k, 128 * t:128 * t + 128], ident)
                last.then_inc(yT_ps, 1)

        @block.scalar
        def _(e):

            act = nc.scalar.activation
            e.wait_ge(mn_zero, 5)
            e.wait_ge(xT_ps, 1)
            act(cvec[:, :], ps[6][:, 0:24], ACT.Copy).then_inc(c_ready, 1)
            e.wait_ge(c_ready, 1)
            act(csil_s[:, :], cvec[:, 0:16], ACT.Sigmoid).then_inc(c_ready, 1)
            for n in range(10):
                t, g = n // 2, n % 2
                e.wait_ge(xT_ps, n + 2)
                c = slice(128 * t, 128 * t + 128)
                act(x[:, 4 * g:4 * g + 4, c], ps[4 + n % 2][:, :].rearrange("p (k t) -> p k t", k=4),
                    ACT.Copy).then_inc(xT_sb, 1)

            def norm_square(l, which):
                for k in range(KT):
                    if which == 1:
                        taken(e, l, ("out", k))
                    if k >= 2:
                        e.wait_ge(sq_used.sem, sq_used.upto(l, which * (KT - 1) + k - 1))
                    act(S2[:, k % 2, :], x[:, k, :], ACT.Square).then_inc(sq_ready(), 1)

            def norm_root(l, which):
                i, lat, cx = acc_item(("norm", which))
                e.wait_ge(acc_ready.sem, acc_ready.upto(l, i + 1))
                act(rot[:, 0:NL], lat[:, :], ACT.Sqrt, bias=eps[:, 0:1])
                act(rot[:, NL:T], cx[:, 0:NC_], ACT.Sqrt, bias=eps[:, 0:1]).then_inc(acc_free[i % 2](), 1)

            def norm_shift(l, which):
                dst = h_hi if which else in_hi
                for k in range(KT):
                    e.wait_ge(h_scaled.sem, h_scaled.upto(l, which * KT + k + 1))
                    for s, (a, b) in enumerate(STREAMS):
                        last = act(dst[:, k, a:b], h[:, k, a:b], ACT.Identity,
                                   bias=mod[:, 24 * which + k, s:s + 1])
                    last.then_inc(h_ready(), 1)

            e.wait_ge(xT_sb, 10)
            with e.Fori(0, DEPTH) as l:

                def ready(name):
                    i, lat, cx = acc_item(name)
                    e.wait_ge(acc_ready.sem, acc_ready.upto(l, i + 1))
                    return acc_free[i % 2], lat, cx

                layer_before(e, l)
                norm_square(l, 0)
                norm_root(l, 0)
                free, lat, cx = ready(("small", 0))
                act(par[:, :], lat[:, 0:NPR], ACT.Copy).then_inc(free(), 1)
                taken(e, l, ("small", 0))
                act(omka[:, :], par[:, PR_KA:PR_KA + 2], ACT.Copy, scale=-1.0, bias=1.0).then_inc(par_ready(), 1)
                def weight_high(u):
                    if u >= 2:
                        e.wait_ge(acc_ready.sem, acc_ready.upto(l, ITEM_AT[UNITS[u - 2][0]] + 1))
                    n, raw_w, hi, lo = unit_weights(u)
                    e.wait_ge(w_ready[n % SLOTS].sem, w_ready[n % SLOTS].upto(l, READY[n]))
                    act(hi, raw_w, ACT.Copy).then_inc(wh_ready(), 1)

                weight_high(0)
                weight_high(1)
                norm_shift(l, 0)
                e.wait_ge(pads_zero.sem, pads_zero.upto(l, 1))

                def ada_rows(j):
                    e.wait_ge(ada_done.sem, ada_done.upto(l, 2 * j + 2))
                    e.wait_ge(mcol_ps.sem, mcol_ps.upto(l, j))
                    act(mrow, ps[6 + j % 2][0:2, :], ACT.Copy).then_inc(mrow_sb(), 1)

                for m in range(9):
                    weight_high(m + 2)
                    free, lat, cx = ready(("rw", m))
                    if m >= 2:
                        e.wait_ge(conv_out.sem, conv_out.upto(l, m - 1))
                    act(raw[:, m % 2, 1:TH + 1], lat[:, 0:TH], ACT.Copy)
                    act(raw[:, m % 2, TH + 1:NL + 1], cx[:, 0:NL - TH], ACT.Copy)
                    act(raw[:, m % 2, NL + 2:T + 2], cx[:, NL - TH:TH], ACT.Copy)
                    w1 = par[:, PR_SHIFT + 9 + m:PR_SHIFT + 10 + m]
                    act(ush[:, m, 0:TH], lat[:, 0:TH], ACT.Copy, scale=w1)
                    act(ush[:, m, TH:T], cx[:, 0:TH], ACT.Copy, scale=w1).then_inc(free(), 1)
                    if m % 2 == 1 or m == 8:
                        ada_rows(4 + m // 2)
                for r, name in enumerate((("q", 0), ("q", 1), ("q", 2), ("q", 3), ("k", 0))):
                    weight_high(UNIT_OF[name] + 2)
                    free, lat, cx = ready(name)
                    sc = 0.125 if r < 4 else 1.0
                    dst = qt[:, r, NL:T] if r < 4 else kt[:, NL:T]
                    if r < 2:
                        e.wait_ge(conv_out.sem, conv_out.upto(l, 9))
                    else:
                        e.wait_ge(rot_cos.sem, rot_cos.upto(l, r - 1))
                        e.wait_ge(acc_ready.sem, acc_ready.upto(l, ITEM_AT[("swap", r - 2)] + 1))
                    act(raw[:, r % 2, 0:TH], lat[:, 0:TH], ACT.Copy, scale=sc)
                    act(raw[:, r % 2, TH:NL], cx[:, 0:NL - TH], ACT.Copy, scale=sc).then_inc(rot_raw(), 1)
                    act(dst, cx[:, NL - TH:TH], ACT.Copy, scale=sc).then_inc(free(), 1)
                    if r in (1, 3):
                        ada_rows(9 + r // 2)
                weight_high(UNIT_OF[("v", 0)] + 2)
                free, lat, cx = ready(("v", 0))
                act(KK[:, 0:TH], lat[:, 0:TH], ACT.Copy)
                act(KK[:, TH:T], cx[:, 0:TH], ACT.Copy).then_inc(free(), 1)
                ada_rows(11)

                def fcopy(f):
                    free, lat, cx = ready(("fn", f))
                    act(uf[:, f, 0:TH], lat[:, 0:TH], ACT.Copy)
                    act(uf[:, f, TH:T], cx[:, 0:TH], ACT.Copy).then_inc(free(), 1)

                fcopy(0)
                free, lat, cx = ready(("kvT", 0))
                act(vtok[:, 0:NL], lat[:, :], ACT.Copy)
                act(vtok[:, NL:T], cx[:, 0:128], ACT.Copy)
                act(kvout[:, :], cx[:, 128:256], ACT.Copy).then_inc(free(), 1)
                free, lat, cx = ready(("ckT", 0))
                act(kcT[:, :], lat[:, 0:128], ACT.Copy).then_inc(free(), 1)
                e.wait_ge(conv_out.sem, conv_out.upto(l, 9))
                act(ush[:, 6, :], ush[:, 6, :], ACT.Sigmoid)
                act(ush[:, 7, :], ush[:, 7, :], ACT.Tanh).then_inc(lora_in(), 1)
                fcopy(1)

                def prep(t):
                    for kind, slot0 in (("w", None), ("a", 6)):
                        for d in range(2):
                            free, lat, cx = ready((kind, t, d))
                            bias = par[:, (PR_W0 if kind == "w" else PR_A0) + 2 * d + t:
                                       (PR_W0 if kind == "w" else PR_A0) + 2 * d + t + 1]
                            dst = S2[:, d, :] if kind == "w" else h[:, 6 + d, :]
                            act(dst[:, 0:NL], lat[:, :], ACT.Sigmoid, bias=bias)
                            act(dst[:, NL:T], cx[:, 0:NC_], ACT.Sigmoid, bias=bias).then_inc(free(), 1)
                    e.wait_ge(kk_raw.sem, kk_raw.upto(l, t + 1))
                    act(e01[:, 0, :], KK, ACT.Square).then_inc(kk_sq(), 1)
                    free, lat, cx = ready(("kk", t))
                    act(e01[:, 0, 0:NL], lat[:, :], ACT.Sqrt, bias=eps[:, 1:2])
                    act(e01[:, 0, NL:T], cx[:, 0:NC_], ACT.Sqrt, bias=eps[:, 1:2]).then_inc(free(), 1)
                    free, lat, cx = ready(("bonus", t))
                    act(e01[:, 1, 0:NL], lat[:, :], ACT.Copy)
                    act(e01[:, 1, NL:T], cx[:, 0:NC_], ACT.Copy).then_inc(free(), 1)

                def prep_exp(t):
                    e.wait_ge(cum_ready.sem, cum_ready.upto(l, t + 1))
                    act(h[:, 2:4, :], CC, ACT.Exp, scale=-DECAY)
                    act(h[:, 4:6, :], CC, ACT.Exp, scale=DECAY)
                    act(h[:, 0:2, :], S2, ACT.Exp, scale=-DECAY)
                    act(emid[:, :, :], mid[:, :, :], ACT.Exp, scale=-DECAY)
                    act(eend[:, :, :], end[:, :, :], ACT.Exp, scale=-DECAY).then_inc(exps_ready(), 1)

                prep(0)
                for t in range(5):
                    free, lat, cx = ready(("ft1", t))
                    act(Z[:, t, :], lat[:, :], ACT.Copy).then_inc(free(), 1)
                for f in range(2):
                    free, lat, cx = ready(("ft2", f))
                    act(uf[:, f, 0:NL], lat[:, :], ACT.Copy)
                    act(uf[:, f, NL:T], cx[:, 0:128], ACT.Copy).then_inc(free(), 1)

                def attention(blocks, done, t):
                    seq = [(b, i) for b in blocks for i in range(8)]

                    def pexp(n):
                        b, i = seq[n]
                        m = done + n
                        w = 128 * len(key_tiles(b))
                        e.wait_ge(p_ready.sem, p_ready.upto(l, m + 1))
                        mx = negm[:, b % 2, i:i + 1]
                        act(Pm[:, m % 4, 0:w], Pm[:, m % 4, 0:w], ACT.Exp, bias=mx,
                            accum_out=den[:, b % 2, i:i + 1])
                        act(esk[:, b % 2, i:i + 1], sink[:, i:i + 1], ACT.Exp, bias=mx).then_inc(p_exp(), 1)

                    def pscale(n):
                        b, i = seq[n]
                        m = done + n
                        w = 128 * len(key_tiles(b))
                        e.wait_ge(den_ready.sem, den_ready.upto(l, m + 1))
                        act(Pm[:, m % 4, 0:w], Pm[:, m % 4, 0:w], ACT.Copy,
                            scale=den[:, b % 2, i:i + 1]).then_inc(p_scaled(), 1)

                    def ptcopy(n):
                        b, i = seq[n]
                        m = done + n
                        nt = len(key_tiles(b))
                        e.wait_ge(pt_ps.sem, pt_ps.upto(l, m + 1))
                        if m >= 8:
                            e.wait_ge(pv_done.sem, pv_done.upto(l, m // 4 - 1))
                        act(PT[:, (m // 4) % 2, 0:nt, i % 4, :],
                            ps[4 + m % 2][:, 0:128 * nt].rearrange("p (c t) -> p c t", c=nt),
                            ACT.Copy).then_inc(pt_sb(), 1)

                    nh = len(seq)
                    for n in range(nh + 5):
                        if n == 8:
                            prep_exp(t)
                        if n < nh:
                            pexp(n)
                        if 0 <= n - 1 < nh:
                            pscale(n - 1)
                        if 0 <= n - 3 < nh:
                            ptcopy(n - 3)
                        if n >= 12 and (n - 5) % 8 == 7:
                            b, i = seq[n - 5]
                            nb = (done + n - 5) // 8
                            e.wait_ge(pv_done.sem, pv_done.upto(l, 2 * nb + 2))
                            act(qt[:, :, 128 * b:128 * b + 128],
                                ps[6 + nb % 2][:, :].rearrange("p (j t) -> p j t", j=4), ACT.Copy).then_inc(o_sb(), 1)

                attention(ATT_A, 0, 0)

                def recurrence(ht):
                    for d in range(2):
                        e.wait_ge(s0_ps.sem, s0_ps.upto(l, 2 * ht + 2))
                        ck = 0 if d == 0 else LCH - 1
                        act(St[:, d, 0, :], ps[7][:, 128 * d:128 * d + 128], ACT.Copy,
                            scale=emid[:, d, ck:ck + 1]).then_inc(s0_sb(), 1)
                    for g, group in enumerate(GROUPS):
                        base = pair_index(ht, g, 0)
                        gb = 5 * base
                        ng = len(group)
                        for n, (p, d, t) in enumerate(group):
                            e.wait_ge(tok_ps.sem, tok_ps.upto(l, base + n + 1))
                            act(W1A[p][:, :, 64:128], ps[2 * p][:, 0:128].rearrange("p (a t) -> p a t", a=2), ACT.Copy)
                            act(TOK[p], ps[2 * p][:, 128:512].rearrange("p (a t) -> p a t", a=3),
                                ACT.Copy).then_inc(tok_sb(), 1)
                        for lv in range(5):
                            for n, (p, d, t) in enumerate(group):
                                e.wait_ge(xt_ps.sem, xt_ps.upto(l, gb + lv * ng + n + 1))
                                act(Xi[p], ps[2 * p + 1][:, 256:512].rearrange("p (a t) -> p a t", a=2),
                                    ACT.Copy).then_inc(xt_sb(), 1)
                        for n, (p, d, t) in enumerate(group):
                            e.wait_ge(w1_ps.sem, w1_ps.upto(l, base + n + 1))
                            act(W1A[p][:, :, 0:64], ps[2 * p][:, 0:128].rearrange("p (a t) -> p a t", a=2),
                                ACT.Copy).then_inc(w1_sb(), 1)
                        for n, (p, d, t) in enumerate(group):
                            e.wait_ge(ug_ps.sem, ug_ps.upto(l, base + n + 1))
                            act(UG[p], ps[2 * p + 1][:, 256:512].rearrange("p (a t) -> p a t", a=2),
                                ACT.Copy).then_inc(ug_sb(), 1)
                    e.wait_ge(fin_ps.sem, fin_ps.upto(l, ht + 1))
                    if ht == 1:
                        e.wait_ge(fin_st.sem, fin_st.upto(l, 64))
                    act(stout, ps[6][:, 0:256].rearrange("p (a t) -> p a t", a=2), ACT.Copy).then_inc(fin_sb(), 1)

                recurrence(0)
                prep(1)
                attention(ATT_B, 16, 1)
                recurrence(1)

                for t in range(2):
                    taken(e, l, ("mean", t))
                    act(e01[:, t, :], ush[:, 2 + t, :], ACT.Square).then_inc(ysq_ready(), 1)
                for t in range(2):
                    free, lat, cx = ready(("var", t))
                    act(e01[:, t, 0:NL], lat[:, :], ACT.Sqrt, bias=eps[:, 2:3])
                    act(e01[:, t, NL:T], cx[:, 0:NC_], ACT.Sqrt, bias=eps[:, 2:3]).then_inc(free(), 1)
                norm_square(l, 1)
                e.wait_ge(fin_st.sem, fin_st.upto(l, 128))
                norm_root(l, 1)

                weight_high(NPROJ)
                weight_high(NPROJ + 1)
                e.wait_ge(kv_stored.sem, kv_stored.upto(l, 32))
                norm_shift(l, 1)
                for u in range(NPROJ + 2, NUNIT + 2):
                    if u < NUNIT:
                        weight_high(u)
                    name = UNITS[u - 2][0]
                    if name[0] == "gate":
                        i = name[1]
                        i_, lat, cx = acc_item(name)
                        e.wait_ge(acc_ready.sem, acc_ready.upto(l, i_ + 1))
                        if i > 0:
                            e.wait_ge(hid_split.sem, hid_split.upto(l, i))
                        act(tmp[:, 0:TH], lat[:, 0:TH], ACT.Sigmoid)
                        act(tmp[:, TH:T], cx[:, 0:TH], ACT.Sigmoid).then_inc(hid_sig(), 1)

            layer_before(e, DEPTH)
            for k in range(KT):
                if k >= 2:
                    e.wait_ge(sq_used.sem, sq_used.upto(DEPTH, k - 1))
                act(S2[:, k % 2, :], x[:, k, :], ACT.Square).then_inc(sq_ready.sem, 1)
            e.wait_ge(acc_ready.sem, acc_ready.upto(DEPTH, 1))
            act(rot[:, 0:NL], ps[0][:, :], ACT.Sqrt, bias=eps[:, 0:1])
            act(rot[:, NL:T], ps[2][:, 0:NC_], ACT.Sqrt, bias=eps[:, 0:1]).then_inc(acc_free[0].sem, 1)
            for t in range(5):
                e.wait_ge(yT_ps, t + 1)
                if t >= 2:
                    e.wait_ge(y_stored[t % 2], 16 * (t // 2))
                for g in range(2):
                    n = 2 * t + g
                    last = act(yout[:, t % 2, 512 * g:512 * g + 512], ps[4 + n % 4][:, :], ACT.Copy)
                last.then_inc(yT_sb, 1)

        @block.vector
        def _(e):
            own = Own(e, dve_own, DVE_CHAIN)
            V = nc.vector
            for s in signals.values():
                if s.primed:
                    e.sem_inc(s.sem, s.primed)
            e.wait_ge(c_ready, 2)
            V.tensor_tensor(csil[:, :, :].rearrange("p k s -> p s k"), cvec[:, 0:16].rearrange("p (s k) -> p s k", s=2),
                            csil_s.rearrange("p (s k) -> p s k", s=2), MUL).then_inc(c_ready, 1)

            e.wait_ge(ld_tab, 64)

            def gains(l, which):
                g = par[:, (PR_NMIX, PR_NFFN)[which]:(PR_NMIX, PR_NFFN)[which] + 8].unsqueeze(2).to_broadcast([128, 8, 2])
                V.scalar_tensor_tensor(gain[:, which, :, :], mod[:, 24 * which + 8:24 * which + 16, :], 1.0, g,
                                       ADD, MUL).then_inc(gain_ready(), 1)
                e.wait_ge(gain_ready.sem, gain_ready.upto(l, which + 1))

            def norm_scale(l, which, n, per_stream):
                taken(e, l, ("norm", which))
                own.after(V.reciprocal(rot, rot))
                for k in range(KT):
                    for s, (a, b) in enumerate(STREAMS):
                        last = V.scalar_tensor_tensor(h[:, k, a:b], x[:, k, a:b], gain[:, n, k, s:s + 1], rot[:, a:b],
                                                      MUL, MUL)
                    last.then_inc(h_scaled() if per_stream else h_scaled.sem, 1)
                if per_stream:
                    for k in range(KT):
                        low_part(l, which, k)

            def low_part(l, which, k):
                hi, lo = (h_hi, h_lo) if which else (in_hi, in_lo)
                e.wait_ge(h_ready.sem, h_ready.upto(l, which * KT + k + 1))
                for s, (a, b) in enumerate(STREAMS):
                    last = V.scalar_tensor_tensor(lo[:, k, a:b], h[:, k, a:b], mod[:, 24 * which + k, s:s + 1],
                                                  hi[:, k, a:b], ADD, SUB)
                last.then_inc(hl_ready(), 1)

            e.wait_ge(xT_sb, 10)
            with e.Fori(0, DEPTH) as l:
                own.l, own.n = l, 0

                def ready(name):
                    i, lat, cx = acc_item(name)
                    e.wait_ge(acc_ready.sem, acc_ready.upto(l, i + 1))
                    return acc_free[i % 2], lat, cx

                layer_before(e, l)
                for j in range(4):
                    e.wait_ge(ada_done.sem, ada_done.upto(l, 2 * j + 2))
                    if j >= 1:
                        e.wait_ge(mcol_ps.sem, mcol_ps.upto(l, j))
                    V.tensor_copy(mrow, ps[6 + j % 2][0:2, :]).then_inc(mrow_sb(), 1)
                e.wait_ge(par_ready.sem, par_ready.upto(l, 1))
                e.wait_ge(mcol_ps.sem, mcol_ps.upto(l, 4))
                own.after(V.tensor_tensor(mod[:, 0:16, :], ps[4][:, 0:32].rearrange("p (m s) -> p m s", s=2),
                                          par[:, PR_ADA:PR_ADA + 16].unsqueeze(2).to_broadcast([128, 16, 2]), ADD))
                gains(l, 0)
                norm_scale(l, 0, 0, True)
                for m in range(9):
                    taken(e, l, ("rw", m))
                    wl = par[:, PR_SHIFT + m:PR_SHIFT + m + 1]
                    wr = par[:, PR_SHIFT + 18 + m:PR_SHIFT + 19 + m]
                    r_ = raw[:, m % 2, :]
                    V.scalar_tensor_tensor(ush[:, m, 0:NL], r_[:, 0:512], wl, ush[:, m, 0:NL], MUL, ADD)
                    own.after(V.scalar_tensor_tensor(ush[:, m, NL:T], r_[:, 513:641], wl, ush[:, m, NL:T], MUL, ADD))
                    V.scalar_tensor_tensor(ush[:, m, 0:NL], r_[:, 2:514], wr, ush[:, m, 0:NL], MUL, ADD)
                    V.scalar_tensor_tensor(ush[:, m, NL:T], r_[:, 515:643], wr, ush[:, m, NL:T], MUL,
                                           ADD).then_inc(conv_out(), 1)
                e.wait_ge(ld_rope.sem, ld_rope.upto(l, 16))
                for r in range(5):
                    free, lat, cx = ready(("swap", r))
                    dst = qt[:, r, 0:NL] if r < 4 else kt[:, 0:NL]
                    e.wait_ge(rot_done.sem, rot_done.upto(l, r))
                    V.tensor_tensor(rot[:, 0:NL], lat[:, :], rope[:, 1, :], MUL).then_inc(free(), 1)
                    taken(e, l, ("swap", r))
                    e.wait_ge(rot_cos.sem, rot_cos.upto(l, r + 1))
                    V.tensor_tensor(dst, dst, rot[:, 0:NL], ADD).then_inc(rot_done(), 1)
                e.wait_ge(mcol_ps.sem, mcol_ps.upto(l, 12))
                own.after(V.tensor_tensor(mod[:, 16:48, :], ps[5][:, 32:96].rearrange("p (m s) -> p m s", s=2),
                                          par[:, PR_ADA + 16:PR_ADA + 48].unsqueeze(2).to_broadcast([128, 32, 2]), ADD))
                gains(l, 1)

                def chunks(v):
                    return v.rearrange("p a (c t) -> p (a c) t", t=CH)

                def prep(t, step):
                    c0 = CC[:, 0, :].rearrange("p (c t) -> p c t", t=CH)
                    c1 = CC[:, 1, :].rearrange("p (c t) -> p c t", t=CH)
                    n = NCH
                    if step == 0:
                        taken(e, l, ("w", t, 0))
                        taken(e, l, ("w", t, 1))
                        V.tensor_tensor_scan(CC[:, 0, :], reset[:, :], S2[:, 0, :], 0.0, MUL, ADD)
                        own.after(V.tensor_tensor_scan(CC[:, 1, :], reset[:, :], S2[:, 1, :], 0.0, MUL, ADD))
                    elif step == 1:
                        V.tensor_copy(end[:, 0, :].unsqueeze(2), c0[:, :, 63:64])
                        V.tensor_copy(mid[:, 0, :].unsqueeze(2), c0[:, :, 31:32])
                        own.after(V.tensor_copy(end[:, 1, :].unsqueeze(2), c1[:, :, 63:64]))
                        own.after(V.tensor_tensor(CC[:, 1, :], S2[:, 1, :], CC[:, 1, :], SUB))
                    elif step == 2:
                        own.after(V.tensor_tensor(c1, c1, end[:, 1, :].unsqueeze(2).to_broadcast([128, NCH, CH]), ADD))
                        own.after(V.tensor_copy(mid[:, 1, :].unsqueeze(2), c1[:, :, 32:33]))
                    elif step == 3:
                        own.after(V.tensor_tensor(chunks(CC), chunks(CC),
                                                  mid[:, :, :].rearrange("p a c -> p (a c)").unsqueeze(2).to_broadcast(
                                                      [128, 2 * NCH, CH]), SUB))
                    elif step == 4:
                        own.after(V.tensor_tensor(end[:, :, :], end[:, :, :], mid[:, :, :], SUB))
                        V.tensor_tensor(S2, CC, S2, SUB).then_inc(cum_ready(), 1)
                    elif step == 5:
                        taken(e, l, ("kk", t))
                        own.after(V.reciprocal(e01[:, 0, 0:NL // 2], e01[:, 0, 0:NL // 2]))
                    elif step == 6:
                        own.after(V.reciprocal(e01[:, 0, NL // 2:T], e01[:, 0, NL // 2:T]))
                    elif step == 7:
                        V.tensor_tensor(KK, KK, e01[:, 0, :], MUL).then_inc(kk_ready(), 1)
                        e.wait_ge(kk_ready.sem, kk_ready.upto(l, t + 1))
                    elif step == 8:
                        e.wait_ge(exps_ready.sem, exps_ready.upto(l, t + 1))
                        V.tensor_tensor(dec[:, 0, 0:n - 1], eend[:, 0, 0:n - 1], emid[:, 0, 1:n], MUL)
                        V.tensor_copy(dec[:, 0, n - 1:n], eend[:, 0, n - 1:n])
                        V.tensor_copy(dec[:, 1, 0:1], eend[:, 1, 0:1])
                        own.after(V.tensor_tensor(dec[:, 1, 1:n], eend[:, 1, 1:n], emid[:, 1, 0:n - 1], MUL))
                        V.tensor_copy(dec[:, 1, LCH:LCH + 1], eend[:, 1, LCH:LCH + 1])
                    elif step == 9:
                        own.after(V.tensor_scalar(CC, h[:, 6:8, :], par[:, PR_KA + t:PR_KA + t + 1], omka[:, t:t + 1],
                                                  MUL, ADD))
                    elif step == 10:
                        own.after(V.tensor_tensor(CC, CC, ush[:, 2 + t:3 + t, :].to_broadcast([128, 2, T]), MUL))
                    elif step == 11:
                        own.after(V.tensor_tensor(h[:, 6:8, :], h[:, 6:8, :], h[:, 4:6, :], MUL))
                    elif step == 12:
                        own.after(V.tensor_tensor(h[:, 4:6, :], h[:, 4:6, :], CC, MUL))
                    elif step == 13:
                        own.after(V.scalar_tensor_tensor(h[:, 6:8, :], h[:, 6:8, :], -1.0,
                                                         KK.unsqueeze(1).to_broadcast([128, 2, T]), MUL, MUL))
                    elif step == 14:
                        e.wait_ge(ar_done.sem, ar_done.upto(l, t + 1))
                        taken(e, l, ("bonus", t))
                        V.tensor_tensor(ush[:, t, :], e01[:, 1, :], ush[:, 4 + t, :], MUL).then_inc(scaled_ready(), 1)
                        e.wait_ge(scaled_ready.sem, scaled_ready.upto(l, t + 1))

                def attention(blocks, done, t):
                    seq = [(b, i) for b in blocks for i in range(8)]

                    def softmax_in(n):
                        b, i = seq[n]
                        m = done + n
                        w = 128 * len(key_tiles(b))
                        c0, c1 = mask_cols(b)
                        free, lat, cx = ready(("s", b, i))
                        e.wait_ge(pt_ps.sem, pt_ps.upto(l, max(m - 3, 0)))
                        V.tensor_tensor(Pm[:, m % 4, 0:w], lat[:, 0:w], attmask[:, c0:c1], ADD).then_inc(free(), 1)
                        taken(e, l, ("s", b, i))
                        mx = negm[:, b % 2, i:i + 1]
                        own.after(V.tensor_reduce(mx, Pm[:, m % 4, 0:w], AX.X, MAX))
                        V.tensor_scalar(mx, mx, sink[:, i:i + 1], -1.0, MAX, MUL).then_inc(p_ready(), 1)

                    def denominator(n):
                        b, i = seq[n]
                        e.wait_ge(p_exp.sem, p_exp.upto(l, done + n + 1))
                        dn = den[:, b % 2, i:i + 1]
                        own.after(V.tensor_tensor(dn, dn, esk[:, b % 2, i:i + 1], ADD))
                        V.reciprocal(dn, dn).then_inc(den_ready(), 1)

                    for n in range(len(seq) + 1):
                        if n < len(seq):
                            softmax_in(n)
                        if n >= 1:
                            denominator(n - 1)
                        prep(t, n)

                attention(ATT_A, 0, 0)

                nchain = [0]

                def recurrence(ht):
                    for g, group in enumerate(GROUPS):
                        base = pair_index(ht, g, 0)
                        gb = 5 * base
                        ng = len(group)
                        for hd in range(2):
                            for n, (p, d, t) in enumerate(group):
                                bank = ps[2 * p + 1] if hd == 0 else ps[2 * p]
                                e.wait_ge(prod_ps.sem, prod_ps.upto(l, 2 * base + hd * ng + n + 1))
                                V.tensor_tensor(LP[p][:, hd, :].rearrange("p (a t) -> p a t", a=2),
                                                bank[:, :].rearrange("p (a t) -> p a t", a=2),
                                                masks[:, d:d + 1, :].to_broadcast([128, 2, 256]), MUL).then_inc(
                                                    prod_sb(), 1)
                        eye = mats[:, 0:1, :].to_broadcast([128, 2, 128])
                        for n, (p, d, t) in enumerate(group):
                            e.wait_ge(prod_sb.sem, prod_sb.upto(l, 2 * base + ng + n + 1))
                            own.after(V.tensor_tensor(Yi[p], LP[p][:, :, 256:384],
                                                      lvl[:, 1 - d, 0:1, :].to_broadcast([128, 2, 128]), MUL))
                            V.tensor_tensor(Yi[p], Yi[p], eye, ADD).then_inc(inv0_sb(), 1)
                        for lv in range(1, 6):
                            at = gb + (lv - 1) * ng
                            for n, (p, d, t) in enumerate(group):
                                e.wait_ge(p1_ps.sem, p1_ps.upto(l, at + n + 1))
                                V.tensor_tensor(P1[p], ps[2 * p][:, 0:256].rearrange("p (a t) -> p a t", a=2),
                                                lvl[:, d, lv:lv + 1, :].to_broadcast([128, 2, 128]), MUL).then_inc(
                                                    p1_sb(), 1)
                            for n, (p, d, t) in enumerate(group):
                                e.wait_ge(yu_ps.sem, yu_ps.upto(l, at + n + 1))
                                if lv == 1:
                                    e.wait_ge(inv0_sb.sem, inv0_sb.upto(l, base + n + 1))
                                else:
                                    e.wait_ge(yu_sb.sem, yu_sb.upto(l, at - ng + n + 1))
                                V.tensor_tensor(Yi[p], Yi[p], ps[2 * p + 1][:, 0:256].rearrange(
                                    "p (a t) -> p a t", a=2), ADD).then_inc(yu_sb(), 1)
                        for n, (p, d, t) in enumerate(group):
                            e.wait_ge(qmn_ps.sem, qmn_ps.upto(l, base + n + 1))
                            b0 = ps[2 * p]
                            c = slice(128 * t, 128 * t + 128)
                            if g == 0 and ht == 0 and n == 0:
                                e.wait_ge(mn_zero, 5)
                            V.tensor_tensor(Qt[p], b0[:, 0:128], h[:, 2 + d, c], ADD)
                            for hd in range(2):
                                o = slice(64 * hd, 64 * hd + 64)
                                V.tensor_tensor(MN[o, p, 0, :, o], PS[o, 2 * p:2 * p + 2, 128:192],
                                                mats[o, 0:1, o].to_broadcast([64, 2, 64]), ADD)
                                last = V.tensor_tensor(MN[o, p, 1, :, o],
                                                       PS[o, 2 * p:2 * p + 2, 256:320],
                                                       dec[o, d, 2 * t:2 * t + 2].unsqueeze(2).to_broadcast([64, 2, 64]),
                                                       MUL)
                            last.then_inc(qmn_sb(), 1)
                        for (p, d, t, hf, ck) in chain_steps(group):
                            if needs_state(ck, d):
                                slot, need = PLAN[(ht, g, d, ck)]
                                e.wait_ge(st_ps.sem, st_ps.upto(l, nchain[0] + 1))
                                e.wait_ge(qmn_sb.sem, qmn_sb.upto(l, base + len(group)))
                                V.scalar_tensor_tensor(St[:, d, 1 - slot, :], ps[2 * p][:, 384:512],
                                                       dec[:, d, ck:ck + 1], MN[:, p, 1, hf, :], MUL,
                                                       ADD).then_inc(st_sb(), 1)
                                nchain[0] += 1
                        for n, (p, d, t) in enumerate(y_order(group)):
                            e.wait_ge(y_ps.sem, y_ps.upto(l, base + n + 1))
                            c = slice(128 * t, 128 * t + 128)
                            yc = ush[:, 2 + ht, c]
                            if first_touch(g, d, t):
                                V.tensor_copy(yc, ps[2 * p + 1][:, 0:128]).then_inc(y_sb(), 1)
                            else:
                                e.wait_ge(y_sb.sem, y_sb.upto(l, base + n))
                                V.tensor_tensor(yc, yc, ps[2 * p + 1][:, 0:128], ADD).then_inc(y_sb(), 1)
                        if g == 1:
                            e.wait_ge(y_ps.sem, y_ps.upto(l, base + len(group)))
                            V.memset(St[:, :, 0, :], 0.0).then_inc(ctx_zero(), 1)

                recurrence(0)
                attention(ATT_B, 16, 1)
                recurrence(1)

                e.wait_ge(y_sb.sem, y_sb.upto(l, y_sb.per))
                for t in range(2):
                    free, lat, cx = ready(("mean", t))
                    y = ush[:, 2 + t, :]
                    V.tensor_tensor(y[:, 0:NL], y[:, 0:NL], lat[:, :], SUB)
                    V.tensor_tensor(y[:, NL:T], y[:, NL:T], cx[:, 0:NC_], SUB).then_inc(free(), 1)
                for t in range(2):
                    y = ush[:, 2 + t, :]
                    taken(e, l, ("var", t))
                    own.after(V.reciprocal(e01[:, t, :], e01[:, t, :]))
                    own.after(V.tensor_tensor(y, y, e01[:, t, :], MUL))
                    own.after(V.tensor_scalar(y, y, par[:, PR_LNG + t:PR_LNG + t + 1], par[:, PR_LNB + t:PR_LNB + t + 1],
                                              MUL, ADD))
                    own.after(V.tensor_tensor(y, y, ush[:, t, :], ADD))
                    free, lat, cx = ready(("g", t))
                    V.tensor_tensor(y[:, 0:NL], y[:, 0:NL], lat[:, :], MUL)
                    V.tensor_tensor(y[:, NL:T], y[:, NL:T], cx[:, 0:NC_], MUL).then_inc(free(), 1)

                def residual(name, m, gate_at, split):
                    free, lat, cx = ready(name)
                    for a, b, bank, at in ((0, split, lat, 0), (split, NL, cx, 0), (NL, T, cx, NL - split)):
                        if a < b:
                            s = 1 if a == NL else 0
                            last = V.scalar_tensor_tensor(x[:, m, a:b], bank[:, at:at + b - a],
                                                          mod[:, gate_at + m, s:s + 1], x[:, m, a:b], MUL, ADD)
                    last.then_inc(free(), 1)

                for m in range(KT):
                    residual(("out", m), m, 16, NL)
                norm_scale(l, 1, 1, True)
                for hf in range(2):
                    for i in range(FH * hf, FH * hf + FH):
                        gfree, glat, gcx = ready(("gate", i))
                        e.wait_ge(hid_sig.sem, hid_sig.upto(l, i + 1))
                        V.tensor_tensor(tmp[:, 0:TH], tmp[:, 0:TH], glat[:, 0:TH], MUL)
                        V.tensor_tensor(tmp[:, TH:T], tmp[:, TH:T], gcx[:, 0:TH], MUL).then_inc(gfree(), 1)
                        taken(e, l, ("gate", i))
                        free, lat, cx = ready(("up", i))
                        V.tensor_tensor(tmp[:, 0:TH], tmp[:, 0:TH], lat[:, 0:TH], MUL)
                        V.tensor_tensor(tmp[:, TH:T], tmp[:, TH:T], cx[:, 0:TH], MUL).then_inc(free(), 1)
                        taken(e, l, ("up", i))
                        own.after(V.tensor_copy(hid_hi[:, i % FH, :], tmp[:, :]))
                        V.tensor_tensor(hid_lo[:, i % FH, :], tmp[:, :], hid_hi[:, i % FH, :], SUB).then_inc(hid_split(), 1)
                    for m in range(KT):
                        residual(("f2", m, hf), m, 40, TH)

            assert own.most == DVE_CHAIN, own.most
            own.l = DEPTH
            own.n = 0
            own.after(V.tensor_copy(gain[:, 2, :, :], cvec[:, 16:24].unsqueeze(2).to_broadcast([128, 8, 2])))
            norm_scale(DEPTH, 0, 2, False)

        bad = [n for n, s in signals.items() if not s.check(n)]
        assert not bad, bad


INS = ["x_prompt", "x_sample", "cache_k", "cache_v", "state_rwkv", "c", "c_ctx", "w_ada", "b_ada", "norm_mix_g",
       "norm_ffn_g", "w_in", "w_out", "attn_sink", "rwkv_shift_w", "rwkv_w0", "rwkv_w_up", "rwkv_a0", "rwkv_a_up",
       "rwkv_g_up", "rwkv_k_k", "rwkv_k_a", "rwkv_r_k", "rwkv_ln_g", "rwkv_ln_b", "ffn_w_in", "ffn_w_out",
       "norm_final_g"]
OUTS = [("y_p", (1, NC_, D)), ("y_s", (1, NL, D)), ("new_k", (1, DEPTH, NC_, 2, HD)),
        ("new_v", (1, DEPTH, NC_, 2, HD)), ("new_s", (1, DEPTH, 2, 4, HD, HD))]


def tables():
    out = {}
    p = np.arange(128)
    mats = np.zeros((128, 5, 128), np.float32)
    mats[p, 0, p] = 1.0
    mats[p, 1, p ^ 16] = 1.0
    mats[:, 2, :] = 1.0 / D
    same_head = (p[:, None] // HD) == (p[None, :] // HD)
    mats[:, 3, :] = same_head
    mats[:, 4, :] = same_head / float(HD)
    out["t_mats"] = mats
    same = (p[:, None] // CH) == (p[None, :] // CH)
    m = np.zeros((128, 2, 2, 128), np.float32)
    i, t = p[:, None], p[None, :]
    m[:, 0, 0], m[:, 0, 1] = same & (i < t), same & (i <= t)
    m[:, 1, 0], m[:, 1, 1] = same & (i > t), same & (i >= t)
    out["t_masks"] = m.reshape(128, 2, 256)
    lv = np.zeros((128, 2, 6, 128), np.float32)
    for n, size in enumerate(LEVELS):
        pair = (p[:, None] // (2 * size)) == (p[None, :] // (2 * size))
        late, early = (p[:, None] // size) % 2 == 1, (p[None, :] // size) % 2 == 0
        lv[:, 0, n] = pair & late & early
        lv[:, 1, n] = lv[:, 0, n].T
    out["t_lvl"] = lv
    am = np.zeros((128, 5, 128), np.float32)
    am[:, 1] = np.where(t >= i, 0.0, -1e30)
    am[:, 3] = np.where(t <= i, 0.0, -1e30)
    out["t_attmask"] = am.reshape(128, 640)
    j = np.arange(T)
    out["t_reset"] = np.broadcast_to((j % CH != 0).astype(np.float32), (128, T)).copy()
    d = np.arange(HD)
    a = 2 * np.pi * np.outer(d, d) / HD
    ch = np.zeros((128, 2, 128), np.float64)
    for g in range(2):
        o = slice(HD * g, HD * g + HD)
        ch[o, 0, o], ch[o, 1, o] = np.cos(a) / 8.0, np.sin(a) / 8.0
    out["t_chan"] = ch.reshape(128, 256).astype(np.float32)
    for n, name in ((NL, ""), (NC_, "x")):
        q = np.arange(n)
        a = 2 * np.pi * (np.outer(q, q) % n) / n
        for f, fn in (("c", np.cos(a)), ("s", -np.sin(a))):
            tab = (fn / math.sqrt(n)).astype(np.float32)
            out["t_dft" + f + name] = tab.reshape(n // 128, 128, n).transpose(1, 0, 2).copy().reshape(
                (128, n // 128, n) if n == NL else (128, n))
    tok = np.arange(NL)
    pos = np.stack([tok // 64, tok % 64]).astype(np.float64)
    inv = 10000.0 ** (-np.arange(16) / 16.0)
    dd = p % HD
    ang = pos[dd // 32] * inv[dd % 16][:, None]
    sign = np.where((dd % 32) < 16, -1.0, 1.0)[:, None]
    out["t_rope"] = np.stack([np.cos(ang), sign * np.sin(ang)], axis=1).astype(np.float32)
    return out


def kernel(**inputs):
    import concourse.bacc as _bacc
    from concourse.bass_utils import run_bass_kernel_spmd as _run

    nc = _bacc.Bacc("TRN2", target_bir_lowering=False, num_devices=1)
    f32 = mybir.dt.float32
    arrays, I, O = {}, {}, {}
    named = [(n, np.ascontiguousarray(inputs[n])) for n in INS] + list(tables().items())
    for name, a in named:
        arrays["in_" + name] = a
        I[name] = nc.dram_tensor("in_" + name, a.shape, f32, kind="ExternalInput").ap()
    for name, shape in OUTS:
        O[name] = nc.dram_tensor("out_" + name, shape, f32, kind="ExternalOutput").ap()
    build(nc, I, O)
    r = _run(nc, [arrays], core_ids=[0])
    return tuple(r.results[0]["out_" + name] for name, _ in OUTS)
```
